# Optimizing a Trainium2 kernel written in Bass

```python
import math
import jax, jax.numpy as jnp
from jax import lax
import numpy as np

D_MODEL = 1024
BATCH = 1
SEQ = 512
DEPTH = 2

HEAD_DIM = 64
N_MLSTM = 4
N_RET = 4
N_SB = 4
N_SWA_Q = 4
N_SWA_KV = 2
N_BRANCH = 4
W_BRANCH = 4 * HEAD_DIM
W_SWA_KV = N_SWA_KV * HEAD_DIM
CHUNK = 128
BLOCK = 128
WINDOW = 128
CONV_K = 4
D_FF = 4 * D_MODEL
N_BUCKETS = 32
MAX_DIST = 128
ROPE_BASE = 10000.0
RET_DECAY_BASE = 5.0
EPS = 1e-6

MLSTM_WIDTHS = (W_BRANCH, W_BRANCH, W_BRANCH, N_MLSTM, N_MLSTM, W_BRANCH)
RET_WIDTHS = (W_BRANCH, W_BRANCH, W_BRANCH, W_BRANCH)
SB_WIDTHS = (W_BRANCH, W_BRANCH, W_BRANCH)
SWA_WIDTHS = (N_SWA_Q * HEAD_DIM, W_SWA_KV, W_SWA_KV)
GATE_WIDTH = N_BRANCH * D_MODEL
IN_WIDTHS = (sum(MLSTM_WIDTHS), sum(RET_WIDTHS), sum(SB_WIDTHS), sum(SWA_WIDTHS), GATE_WIDTH)
D_IN = sum(IN_WIDTHS)

kernel_name = 'hybrid_gated_mlstm_ret_sb_swa_trunk'

def split_cols(x, widths):
    return jnp.split(x, [int(i) for i in np.cumsum(widths)[:-1]], axis=-1)

def rms_norm(x, g):
    xf = x.astype(jnp.float32)
    y = xf * lax.rsqrt(jnp.mean(xf * xf, axis=-1, keepdims=True) + EPS)
    return (y * g.astype(jnp.float32)).astype(x.dtype)

def to_heads(t, n):
    b, s, _ = t.shape
    return t.reshape(b, s, n, HEAD_DIM).transpose(0, 2, 1, 3)

def from_heads(t):
    b, n, s, d = t.shape
    return t.transpose(0, 2, 1, 3).reshape(b, s, n * d)

def causal_dwconv(u, w, b):
    k, ch = w.shape
    out = lax.conv_general_dilated(u, w[:, None, :], window_strides=(1,), padding=[(k - 1, 0)],
                                   dimension_numbers=('NWC', 'WIO', 'NWC'), feature_group_count=ch)
    return out + b

def rotary(t, positions):
    half = t.shape[-1] // 2
    inv = ROPE_BASE ** (-jnp.arange(half, dtype=jnp.float32) / half)
    ang = positions[:, None, :, None].astype(jnp.float32) * inv
    cos, sin = jnp.cos(ang), jnp.sin(ang)
    t1, t2 = t[..., :half], t[..., half:]
    return jnp.concatenate([t1 * cos - t2 * sin, t1 * sin + t2 * cos], axis=-1)

def t5_bucket(rel):
    n = jnp.maximum(rel, 0)
    max_exact = N_BUCKETS // 2
    nf = jnp.maximum(n, 1).astype(jnp.float32)
    large = max_exact + (jnp.log(nf / max_exact) / math.log(MAX_DIST / max_exact)
                         * (N_BUCKETS - max_exact)).astype(jnp.int32)
    large = jnp.minimum(large, N_BUCKETS - 1)
    return jnp.where(n < max_exact, n, large)

def mlstm(q, k, v, i_pre, f_pre):
    b, h, s, d = q.shape
    shp = (b, h, s // CHUNK, CHUNK)
    qc = (q * d ** -0.5).reshape(shp + (d,))
    kc = k.reshape(shp + (d,))
    vc = v.reshape(shp + (d,))
    ig = i_pre.reshape(shp)
    a = jnp.cumsum(jax.nn.log_sigmoid(f_pre).reshape(shp), axis=-1)
    a_last = a[..., -1]
    causal = jnp.tril(jnp.ones((CHUNK, CHUNK), dtype=bool))
    d_intra = jnp.where(causal, a[..., :, None] - a[..., None, :] + ig[..., None, :], -jnp.inf)
    g_loc = a_last[..., None] - a + ig
    m_loc = jnp.max(g_loc, axis=-1)
    w_loc = jnp.exp(g_loc - m_loc[..., None])
    c_loc = jnp.einsum('bhnsk,bhnsv->bhnkv', kc * w_loc[..., None], vc)
    n_loc = jnp.einsum('bhns,bhnsk->bhnk', w_loc, kc)

    def step(carry, inp):
        c_st, n_st, m_st = carry
        c_l, n_l, m_l, a_l = inp
        m_new = jnp.maximum(a_l + m_st, m_l)
        s_old = jnp.exp(a_l + m_st - m_new)
        s_new = jnp.exp(m_l - m_new)
        c_new = s_old[..., None, None] * c_st + s_new[..., None, None] * c_l
        n_new = s_old[..., None] * n_st + s_new[..., None] * n_l
        return (c_new, n_new, m_new), (c_st, n_st, m_st)

    init = (jnp.zeros((b, h, d, d), jnp.float32), jnp.zeros((b, h, d), jnp.float32),
            jnp.zeros((b, h), jnp.float32))
    xs = tuple(jnp.moveaxis(t, 2, 0) for t in (c_loc, n_loc, m_loc, a_last))
    _, (c_in, n_in, m_in) = lax.scan(step, init, xs)
    c_in = jnp.moveaxis(c_in, 0, 2)
    n_in = jnp.moveaxis(n_in, 0, 2)
    m_in = jnp.moveaxis(m_in, 0, 2)
    m_inter = a + m_in[..., None]
    m_tot = jnp.maximum(m_inter, jnp.max(d_intra, axis=-1))
    s_inter = jnp.exp(m_inter - m_tot)
    p = jnp.exp(d_intra - m_tot[..., None]) * jnp.einsum('bhnld,bhnsd->bhnls', qc, kc)
    num = (s_inter[..., None] * jnp.einsum('bhnlk,bhnkv->bhnlv', qc, c_in)
           + jnp.einsum('bhnls,bhnsv->bhnlv', p, vc))
    den = s_inter * jnp.einsum('bhnlk,bhnk->bhnl', qc, n_in) + jnp.sum(p, axis=-1)
    out = num / jnp.maximum(jnp.abs(den), jnp.exp(-m_tot))[..., None]
    return out.reshape(b, h, s, d)

def retention(q, k, v, log_gamma):
    b, h, s, d = q.shape
    n_c = s // CHUNK

    def chunk(t):
        return jnp.moveaxis(t.reshape(b, h, n_c, CHUNK, d), 2, 0)

    idx = jnp.arange(CHUNK, dtype=jnp.float32)
    lg = log_gamma[:, None]
    rel = idx[:, None] - idx[None, :]
    decay_intra = jnp.where(rel >= 0, jnp.exp(jnp.maximum(rel, 0.0)[None] * lg[..., None]), 0.0)
    decay_q = jnp.exp((idx + 1.0)[None] * lg)
    decay_k = jnp.exp((CHUNK - 1.0 - idx)[None] * lg)
    decay_c = jnp.exp(CHUNK * log_gamma)

    def step(state, inp):
        qc, kc, vc = inp
        sc = jnp.einsum('bhld,bhsd->bhls', qc, kc) * decay_intra
        o = (jnp.einsum('bhls,bhsv->bhlv', sc, vc)
             + jnp.einsum('bhlk,bhkv->bhlv', qc, state) * decay_q[..., None])
        state = decay_c[:, None, None] * state + jnp.einsum('bhsk,bhsv->bhkv', kc * decay_k[..., None], vc)
        return state, o

    _, o = lax.scan(step, jnp.zeros((b, h, d, d), jnp.float32), (chunk(q), chunk(k), chunk(v)))
    return jnp.moveaxis(o, 0, 2).reshape(b, h, s, d)

def stick_breaking(q, k, v):
    b, h, s, d = q.shape
    n_b = s // BLOCK
    scale = d ** -0.5
    qb = jnp.moveaxis(q.reshape(b, h, n_b, BLOCK, d), 2, 0)
    key_pos = jnp.arange(s)

    def one_block(args):
        q_blk, start = args
        z = jnp.einsum('bhtd,bhsd->bhts', q_blk, k) * scale
        before = key_pos[None, :] < (start + jnp.arange(BLOCK))[:, None]
        log_keep = jnp.where(before, jax.nn.log_sigmoid(-z), 0.0)
        between = lax.cumsum(log_keep, axis=3, reverse=True) - log_keep
        weight = jnp.where(before, jnp.exp(jax.nn.log_sigmoid(z) + between), 0.0)
        return jnp.einsum('bhts,bhsd->bhtd', weight, v)

    out = lax.map(one_block, (qb, jnp.arange(n_b) * BLOCK))
    return jnp.moveaxis(out, 0, 2).reshape(b, h, s, d)

def swa_with_sinks(q, k, v, sinks, rel_bias, positions):
    b, hq, s, d = q.shape
    g = k.shape[1]
    r = hq // g
    n_b = s // BLOCK
    qb = q.reshape(b, g, r, n_b, BLOCK, d)

    def band(t):
        tb = t.reshape(b, g, n_b, BLOCK, d)
        prev = jnp.concatenate([jnp.zeros_like(tb[:, :, :1]), tb[:, :, :-1]], axis=2)
        return jnp.concatenate([prev, tb], axis=3)

    kw, vw = band(k), band(v)
    pos_b = positions.reshape(b, n_b, BLOCK)
    pos_prev = jnp.concatenate([pos_b[:, :1] - BLOCK, pos_b[:, :-1]], axis=1)
    pos_k = jnp.concatenate([pos_prev, pos_b], axis=2)
    bucket = t5_bucket(pos_b[..., :, None] - pos_k[..., None, :])
    bias = jnp.moveaxis(rel_bias[bucket].astype(jnp.float32), -1, 1).reshape(b, g, r, n_b, BLOCK, 2 * BLOCK)
    kj = jnp.arange(2 * BLOCK)[None, :]
    dist = (jnp.arange(BLOCK)[:, None] + BLOCK) - kj
    key_abs = (jnp.arange(n_b) * BLOCK - BLOCK)[:, None, None] + kj[None]
    valid = (dist >= 0) & (dist < WINDOW) & (key_abs >= 0)
    logits = jnp.einsum('bgrnid,bgnjd->bgrnij', qb, kw) * d ** -0.5 + bias
    logits = jnp.where(valid, logits, -jnp.inf)
    sink = sinks.reshape(g, r)[None, :, :, None, None, None]
    m = jnp.maximum(jnp.max(logits, axis=-1, keepdims=True), sink)
    p = jnp.exp(logits - m)
    den = jnp.sum(p, axis=-1, keepdims=True) + jnp.exp(sink - m)
    out = jnp.einsum('bgrnij,bgnjd->bgrnid', p / den, vw)
    return out.reshape(b, hq, s, d)

def token_mixer(h, positions, w_in, conv_w, conv_b, gate_b, ret_g, q_g, k_g, sinks, rel_bias,
                w_up, w_out, log_gamma):
    f32 = jnp.float32
    b, s, _ = h.shape
    p_ml, p_ret, p_sb, p_swa, p_gate = split_cols(h @ w_in, IN_WIDTHS)

    mq, mk, mv, mi, mf, mo = split_cols(p_ml, MLSTM_WIDTHS)
    qk = jax.nn.silu(causal_dwconv(jnp.concatenate([mq, mk], axis=-1), conv_w, conv_b))
    mq, mk = jnp.split(qk, 2, axis=-1)
    i_pre = jnp.moveaxis((mi + gate_b[0]).astype(f32), -1, 1)
    f_pre = jnp.moveaxis((mf + gate_b[1]).astype(f32), -1, 1)
    h_ml = mlstm(to_heads(mq, N_MLSTM).astype(f32), to_heads(mk, N_MLSTM).astype(f32),
                 to_heads(mv, N_MLSTM).astype(f32), i_pre, f_pre)
    out_ml = from_heads(h_ml) * jax.nn.sigmoid(mo.astype(f32))

    rq, rk, rv, rg = split_cols(p_ret, RET_WIDTHS)
    rq = rotary(to_heads(rq, N_RET).astype(f32), positions)
    rk = rotary(to_heads(rk, N_RET).astype(f32), positions) * HEAD_DIM ** -0.5
    h_ret = from_heads(retention(rq, rk, to_heads(rv, N_RET).astype(f32), log_gamma))
    h_ret = rms_norm(h_ret.reshape(b, s, N_RET, HEAD_DIM), ret_g.reshape(N_RET, HEAD_DIM)).reshape(b, s, W_BRANCH)
    out_ret = h_ret * jax.nn.silu(rg.astype(f32))

    sq, sk, sv = split_cols(p_sb, SB_WIDTHS)
    out_sb = from_heads(stick_breaking(to_heads(sq, N_SB).astype(f32), to_heads(sk, N_SB).astype(f32),
                                       to_heads(sv, N_SB).astype(f32)))

    aq, ak, av = split_cols(p_swa, SWA_WIDTHS)
    aq = rms_norm(to_heads(aq, N_SWA_Q).astype(f32), q_g)
    ak = rms_norm(to_heads(ak, N_SWA_KV).astype(f32), k_g)
    out_swa = from_heads(swa_with_sinks(aq, ak, to_heads(av, N_SWA_KV).astype(f32),
                                        sinks.astype(f32), rel_bias, positions))

    branches = jnp.stack([out_ml, out_ret, out_sb, out_swa], axis=2).astype(h.dtype)
    up = jnp.einsum('bsnw,nwd->bsnd', branches, w_up)
    gates = jax.nn.sigmoid(p_gate.reshape(b, s, N_BRANCH, D_MODEL))
    merged = jnp.sum(gates * up, axis=2)
    return merged @ w_out

def setup_inputs(seed: int = 0) -> dict:
    key = jax.random.key(seed)
    ks = jax.random.split(key, 20)
    nrm = jax.random.normal
    x = nrm(ks[0], (BATCH, SEQ, D_MODEL), jnp.float32)
    c = nrm(ks[1], (BATCH, D_MODEL), jnp.float32)
    start = jax.random.randint(ks[2], (BATCH, 1), 0, 1024, dtype=jnp.int32)
    positions = (start + jnp.arange(SEQ, dtype=jnp.int32)[None, :]).astype(jnp.int32)
    w_ada = nrm(ks[3], (DEPTH, 2, D_MODEL, 3 * D_MODEL), jnp.float32) * (0.5 * D_MODEL ** -0.5)
    b_ada = nrm(ks[4], (DEPTH, 2, 3 * D_MODEL), jnp.float32) * 0.02
    norm_g = 1.0 + 0.02 * nrm(ks[5], (DEPTH, 2, D_MODEL), jnp.float32)
    w_in = nrm(ks[6], (DEPTH, D_MODEL, D_IN), jnp.float32) * D_MODEL ** -0.5
    mlstm_conv_w = nrm(ks[7], (DEPTH, CONV_K, 2 * W_BRANCH), jnp.float32) * CONV_K ** -0.5
    mlstm_conv_b = 0.02 * nrm(ks[8], (DEPTH, 2 * W_BRANCH), jnp.float32)
    i_bias = 0.1 * nrm(ks[9], (DEPTH, 1, N_MLSTM), jnp.float32)
    f_bias = 3.0 + 3.0 * jax.random.uniform(ks[10], (DEPTH, 1, N_MLSTM), jnp.float32)
    mlstm_gate_b = jnp.concatenate([i_bias, f_bias], axis=1)
    ret_norm_g = 1.0 + 0.02 * nrm(ks[11], (DEPTH, W_BRANCH), jnp.float32)
    swa_q_norm_g = 1.0 + 0.02 * nrm(ks[12], (DEPTH, HEAD_DIM), jnp.float32)
    swa_k_norm_g = 1.0 + 0.02 * nrm(ks[13], (DEPTH, HEAD_DIM), jnp.float32)
    swa_sinks = nrm(ks[14], (DEPTH, N_SWA_Q), jnp.float32)
    rel_bias = 0.5 * nrm(ks[15], (N_BUCKETS, N_SWA_Q), jnp.float32)
    w_up = nrm(ks[16], (DEPTH, N_BRANCH, W_BRANCH, D_MODEL), jnp.float32) * W_BRANCH ** -0.5
    w_out = nrm(ks[17], (DEPTH, D_MODEL, D_MODEL), jnp.float32) * D_MODEL ** -0.5
    w_ff1 = nrm(ks[18], (DEPTH, D_MODEL, D_FF), jnp.float32) * D_MODEL ** -0.5
    w_ff2 = nrm(ks[19], (DEPTH, D_FF, D_MODEL), jnp.float32) * D_FF ** -0.5
    return {'x': x, 'c': c, 'positions': positions, 'w_ada': w_ada, 'b_ada': b_ada, 'norm_g': norm_g,
            'w_in': w_in, 'mlstm_conv_w': mlstm_conv_w, 'mlstm_conv_b': mlstm_conv_b,
            'mlstm_gate_b': mlstm_gate_b, 'ret_norm_g': ret_norm_g, 'swa_q_norm_g': swa_q_norm_g,
            'swa_k_norm_g': swa_k_norm_g, 'swa_sinks': swa_sinks, 'rel_bias': rel_bias, 'w_up': w_up,
            'w_out': w_out, 'w_ff1': w_ff1, 'w_ff2': w_ff2}

def reference(x, c, positions, w_ada, b_ada, norm_g, w_in, mlstm_conv_w, mlstm_conv_b, mlstm_gate_b,
              ret_norm_g, swa_q_norm_g, swa_k_norm_g, swa_sinks, rel_bias, w_up, w_out, w_ff1, w_ff2):
    log_gamma = jnp.log(1.0 - jnp.exp2(-(RET_DECAY_BASE + jnp.arange(N_RET, dtype=jnp.float32))))
    c_act = jax.nn.silu(c)
    for l in range(DEPTH):
        mod = jnp.einsum('bd,jde->bje', c_act, w_ada[l]) + b_ada[l]
        shift1, scale1, gate1 = jnp.split(mod[:, 0], 3, axis=-1)
        shift2, scale2, gate2 = jnp.split(mod[:, 1], 3, axis=-1)
        h = rms_norm(x, norm_g[l, 0]) * (1.0 + scale1[:, None, :]) + shift1[:, None, :]
        mix = token_mixer(h, positions, w_in[l], mlstm_conv_w[l], mlstm_conv_b[l], mlstm_gate_b[l],
                          ret_norm_g[l], swa_q_norm_g[l], swa_k_norm_g[l], swa_sinks[l], rel_bias,
                          w_up[l], w_out[l], log_gamma)
        x = x + gate1[:, None, :] * mix.astype(x.dtype)
        h2 = rms_norm(x, norm_g[l, 1]) * (1.0 + scale2[:, None, :]) + shift2[:, None, :]
        ff = jnp.square(jax.nn.relu(h2 @ w_ff1[l])) @ w_ff2[l]
        x = x + gate2[:, None, :] * ff
    return x


_drawn_inputs = setup_inputs


def setup_inputs(seed=0):
    import zlib

    import numpy as np

    out = dict(_drawn_inputs(seed))
    spreads = {}
    factors = {'norm_g': 3.448,
     'mlstm_conv_b': 64.0,
     'ret_norm_g': 8.0,
     'swa_q_norm_g': 8.0,
     'swa_k_norm_g': 8.0,
     'swa_sinks': 34.346,
     'rel_bias': 2.822}
    for name, (base, spread) in spreads.items():
        noise = np.random.default_rng([zlib.crc32(name.encode()), seed]).standard_normal(out[name].shape)
        drawn = base * np.exp(spread * noise) if base else spread * noise
        out[name] = __import__('jax').numpy.asarray(drawn.astype(out[name].dtype))
    for name, factor in factors.items():
        out[name] = (out[name] * factor).astype(out[name].dtype)
    return out
```

```python
from contextlib import ExitStack
import math

import numpy as np

import concourse.bass as bass
from concourse import mybir
from concourse.alu_op_type import AluOpType as ALU

ACT = mybir.ActivationFunctionType
AX = mybir.AxisListType
F32 = mybir.dt.float32
F32R = mybir.dt.float32r
I32 = mybir.dt.int32

P = 128
LAYERS = 2
T = 512
D = 1024
KT = D // P
HD = 64
HEADS = 4
CH = 128
NCH = T // CH
WB = HEADS * HD
NBR = 4
DFF = 4 * D
QUARTERS = DFF // D
BUCKETS = 32
MAX_DIST = 128
EPS = 1e-6
BIG = 1.0e30
BC = 256
LOG_GAMMA = [math.log(1.0 - 2.0 ** -(5.0 + h)) for h in range(HEADS)]
COLS = {"m_q": 0, "m_k": 256, "m_v": 512, "m_if": 768, "m_o": 776, "r_q": 1032, "r_k": 1288, "r_v": 1544,
        "r_g": 1800, "s_q": 2056, "s_k": 2312, "s_v": 2568, "a_q": 2824, "a_kv": 3080, "gate": 3336}

SC_BANK = [0, 1, 2, 1]
SC_COL = [0, 0, 0, 384]
OFF = [0, 512, 1024, 896]
LEN = [T - CH * j for j in range(NCH)]
PT_BLOCKS = [(0, 1), (1, 0), (1, 1), (2, 0), (2, 1), (3, 0), (3, 1)]


EXACT = BUCKETS // 2
BUCKET_FROM = [b if b < EXACT else math.ceil(EXACT * (MAX_DIST / EXACT) ** ((b - EXACT) / (BUCKETS - EXACT)) - 1e-9)
               for b in range(BUCKETS)]
ADA_FIRST = 2 * D // BC
ADA_REST = 4 * D // BC
ADA_BLOCK = [1 + u * 34 // (ADA_REST - 1) for u in range(ADA_REST)]
TABLE_FIRST = 8


def plan():
    blocks, steps = [], []

    def block(name, *arg):
        b = len(blocks)
        blocks.append((name, *arg))
        tiles = 8 if name == "up" else 2
        for h in range(tiles):
            steps.append(("tile", b, h))
            for s in after.pop((b, h), []):
                steps.append(s)
        for s in after.pop((b, "end"), []):
            steps.append(s)

    after = {}

    def put(b, h, *s):
        after.setdefault((b, h), []).extend(s)

    names = ([("m_q",), ("m_k",), ("m_if",), ("m_v",), ("m_o",)] + [("gate", 0, g) for g in range(4)]
             + [("r_q",), ("r_k",), ("up", 0), ("r_v",), ("r_g",)] + [("gate", 1, g) for g in range(4)]
             + [("s_q",), ("s_k",), ("up", 1), ("s_v",)] + [("gate", 2, g) for g in range(4)]
             + [("a_q",), ("a_kv",), ("up", 2)] + [("gate", 3, g) for g in range(4)] + [("up", 3)]
             + [("out", g) for g in range(4)])
    no = {n: i for i, n in enumerate(names)}
    put(no[("m_v",)], 0, ("ifrows",))
    put(no[("m_o",)], 0, ("gcol",))
    put(no[("m_o",)], "end", ("qk", 0, 0))
    put(no[("gate", 0, 0)], "end", ("qk", 0, 1), ("pv", 0, 0))
    put(no[("gate", 0, 1)], "end", ("qk", 0, 2), ("pv", 0, 1))
    put(no[("gate", 0, 2)], "end", ("qk", 0, 3), ("pv", 0, 2))
    put(no[("gate", 0, 3)], "end", ("gate_tanh", 0))
    put(no[("r_q",)], 0, ("pv", 0, 3))
    put(no[("r_q",)], 1, ("rot", 0))
    put(no[("r_k",)], 0, ("rot", 1))
    put(no[("r_k",)], 1, ("rot", 2))
    put(no[("up", 0)], 1, ("rot", 3))
    put(no[("r_g",)], "end", ("qk", 1, 0))
    put(no[("gate", 1, 0)], "end", ("qk", 1, 1), ("pv", 1, 0))
    put(no[("gate", 1, 1)], "end", ("qk", 1, 2), ("pv", 1, 1))
    put(no[("gate", 1, 2)], 0, ("hnorm", 0))
    put(no[("gate", 1, 2)], "end", ("qk", 1, 3), ("pv", 1, 2))
    put(no[("gate", 1, 3)], "end", ("gate_tanh", 1), ("pv", 1, 3))
    put(no[("s_q",)], 0, ("hnorm", 1))
    put(no[("s_k",)], "end", ("qk", 2, 0))
    put(no[("s_v",)], 1, ("suffix", 0))
    put(no[("gate", 2, 0)], 0, ("qk", 2, 1), ("pv", 2, 0))
    put(no[("gate", 2, 1)], 0, ("suffix", 1))
    put(no[("gate", 2, 1)], 1, ("qk", 2, 2), ("pv", 2, 1))
    put(no[("gate", 2, 2)], 1, ("suffix", 2))
    put(no[("gate", 2, 3)], 0, ("qk", 2, 3), ("pv", 2, 2))
    put(no[("gate", 2, 3)], "end", ("gate_tanh", 2))
    put(no[("a_q",)], 0, ("suffix", 3))
    put(no[("a_q",)], 1, ("pv", 2, 3), ("anorm", 0))
    put(no[("a_kv",)], 0, ("anorm", 1))
    put(no[("a_kv",)], 1, ("anorm", 2))
    put(no[("up", 2)], 3, ("qk", 3, 0))
    put(no[("gate", 3, 0)], 0, ("ptrans", 0), ("qk", 3, 1))
    put(no[("gate", 3, 0)], 1, ("pv", 3, 0))
    put(no[("gate", 3, 1)], 0, ("ptrans", 1), ("qk", 3, 2))
    put(no[("gate", 3, 1)], 1, ("pv", 3, 1))
    put(no[("gate", 3, 2)], 0, ("ptrans", 2), ("qk", 3, 3))
    put(no[("gate", 3, 2)], 1, ("pv", 3, 2))
    put(no[("gate", 3, 3)], 0, ("ptrans", 3), ("pv", 3, 3))
    put(no[("gate", 3, 3)], "end", ("gate_tanh", 3))
    for u, b in enumerate(ADA_BLOCK):
        put(b, "end", ("ada", u))
        put(b + 1, 0, ("adasum", u))
    spots = [(no[("gate", n, g)], half) for n in range(3) for g in range(4) for half in range(2)]
    spots += [(no[("m_o",)], 1), (no[("r_v",)], 0), (no[("r_v",)], 1), (no[("s_q",)], 1)]
    for n, (b, half) in enumerate(sorted(spots)):
        put(b, half, ("table", n))
    steps.append(("norm", 0))
    for n in names:
        block(*n)
    assert not after
    steps.append(("norm", 1))
    return blocks, steps


BLOCKS, STEPS = plan()
PRE_BLOCKS = len(BLOCKS)
assert PRE_BLOCKS % 2 == 0
TILE_NO = {}
for _s in STEPS:
    if _s[0] == "tile":
        TILE_NO[_s[1:]] = len(TILE_NO)
PRE_TILES = len(TILE_NO)
BLOCK_NO = {b: i for i, b in enumerate(BLOCKS)}
FF_ADA = {1: 0, 4: 1}
FF_ADASUM = {2: 0, 5: 1}


def makes_aux(s):
    return (s[0] in ("norm", "ifrows", "gcol", "rot", "hnorm", "anorm", "adasum")
            or s[:2] == ("qk", 0) or s in (("pv", 0, 1), ("pv", 0, 3)))


AUX = {s: n for n, s in enumerate([s for s in STEPS if makes_aux(s)])}
PRO_AUX = 2 + 1

TABLE_STEPS = 3 + HEADS + (1 + HEADS) * (BUCKETS - 1) + 3 * HEADS + 1

_BLK = PRE_BLOCKS // 2
_TL = PRE_TILES // 2
COUNTS = {
    "raw_landed0": (0, 16 * _BLK, 64), "raw_landed1": (0, 16 * _BLK, 64),
    "hi_ready0": (0, _BLK, 4), "hi_ready1": (0, _BLK, 4), "lo_ready0": (0, _BLK, 4), "lo_ready1": (0, _BLK, 4),
    "ada_landed": (16 * 3, 16 * ADA_REST, 16 * 2), "ada_landed_b": (16 * 3, 0, 0), "ada_landed_c": (16 * 2, 0, 0),
    "ada_used": (ADA_FIRST - 1, 0, 0), "c_act_ready": (1, 0, 0), "ada_partial": (0, ADA_REST, 2),
    "bank_ready0": (4, _TL, 8), "bank_ready1": (4, _TL, 8), "bank_taken0": (4, _TL, 8), "bank_taken1": (4, _TL, 8),
    "aux_ready": (PRO_AUX, len(AUX), 2), "aux_taken": (PRO_AUX, len(AUX), 2),
    "square_ready": (0, 2 * KT + 5, 0), "square_used": (0, 2 * (KT - 1), 0), "rstd_ready": (0, 2 + 5, 0),
    "h_scaled": (0, 2 * KT, 0), "h_hi_ready": (0, 2 * KT, 0), "h_ready": (0, 2 * KT, 0),
    "feature_ready": (0, 4 + 4 + 3, 0), "conv_ready": (0, 4, 0), "silu_ready": (0, 4 + 2, 0), "rot_raw": (0, 4, 0),
    "logterm_ready": (0, 1 + 4, 0), "rows_ready": (0, 1, 0), "masked_ready": (0, 4, 0), "decay_ready": (0, 8, 0),
    "qk_ready": (0, 16, 0), "scores_taken": (0, 16, 0), "softplus_ready": (0, 4, 0), "suffix_ready": (0, 4, 0),
    "negmax_ready": (0, 4, 0), "exp_ready": (0, 4, 0), "probs_ready": (0, 4, 0),
    "ptrans_ready": (0, 4, 0), "ptrans_copied": (0, 4, 0),
    "pv_ready": (0, 16, 0), "den_ready": (0, 2, 0), "out_scaled": (0, 4, 0),
    "branch_hi_ready": (0, 8, 0), "branch_ready": (0, 8, 0), "gate_ready": (0, 4, 0),
    "merged_tile": (0, 8, 0), "merged_hi_ready": (0, 8, 0), "merged_ready": (0, 8, 0),
    "relu_ready": (0, 0, 8), "hidden_hi_ready": (0, 0, 8), "hidden_ready": (0, 0, 8),
    "vectors_loaded": (16 * 16, 0, 0), "table_order": (TABLE_STEPS, 0, 0), "x_landed": (64, 0, 0), "consts_ready": (1, 0, 0), "c_tanh": (1, 0, 0),
    "angles_ready": (1, 0, 0), "sines_ready": (2, 0, 0), "pool_order": (25, 0, 0),
    "stored": (0, 0, 0), "xt_ready": (0, 0, 0), "xt_taken": (0, 0, 0),
}
COUNTS["act_order"] = (0, 66, 0)
COUNTS["dve_order"] = (23, 224, 15)


VECTORS = COUNTS["vectors_loaded"][0]
TILES_BEFORE = [TILE_NO[(b, 0)] for b in range(PRE_BLOCKS)] + [PRE_TILES]


def at(name, n, layer=None, quarter=None):
    before, pre, per_quarter = COUNTS[name]
    if layer is None:
        return n
    if quarter is None:
        return layer * (pre + QUARTERS * per_quarter) + (before + n)
    return layer * (pre + QUARTERS * per_quarter) + quarter * per_quarter + (before + pre + n)


def after_layers(name, n=0):
    before, pre, per_quarter = COUNTS[name]
    return before + LAYERS * (pre + QUARTERS * per_quarter) + n


class Program:

    def __init__(self, engine, sems, order=None):
        self.engine, self.sems, self.order = engine, sems, order
        self.layer = self.quarter = self.last = None
        self.n = {}
        self.seen = {}
        self.tail = False

    def enter(self, layer=None, quarter=None):
        self.layer, self.quarter, self.n = layer, quarter, {}
        if self.order:
            self.last = (self.sems[self.order], at(self.order, 0, layer, quarter))

    def leave(self, region):
        self.seen[region] = dict(self.n)

    def value(self, name, n):
        return after_layers(name, n) if self.tail else at(name, n, self.layer, self.quarter)

    def count(self, name=None, n=None, by=1):
        name = name or self.order
        self.n[name] = self.n.get(name, 0) + by
        self.last = (self.sems[name], self.value(name, self.n[name] if n is None else n))
        return self.sems[name], by


def trunk(nc, x, c, positions, w_ada, b_ada, norm_g, w_in, conv_w, conv_b, gate_b, ret_g, q_g, k_g, sinks,
          rel_bias, w_up, w_out, w_ff1, w_ff2, rope_freq, out):
    with ExitStack() as ctx:
        def sb(name, cols, dtype=F32):
            return ctx.enter_context(nc.sbuf_tensor(name, [P, cols], dtype))

        sems = {name: ctx.enter_context(nc.semaphore(name)) for name in COUNTS}

        gemm = [ctx.enter_context(nc.psum_tensor(f"gemm{i}", [P, T], F32)) for i in range(2)]
        score = [ctx.enter_context(nc.psum_tensor(f"score{i}", [P, T], F32)) for i in range(3)]
        outp = ctx.enter_context(nc.psum_tensor("outp", [P, T], F32))
        denp = ctx.enter_context(nc.psum_tensor("denp", [P, T], F32))
        aux = ctx.enter_context(nc.psum_tensor("aux", [P, T], F32))

        with nc.sbuf_tensor("gates", [P, 8 * T], F32) as gates, nc.sbuf_tensor("merged", [P, 8 * T], F32) as merged:
            pass
        hid_hi = sb("hid_hi", 8 * T, F32R)
        hid_lo = sb("hid_lo", 8 * T, F32R)
        xt = sb("xt", KT * T)
        h_hi, h_lo = sb("h_hi", KT * T, F32R), sb("h_lo", KT * T, F32R)
        w_raw = [sb(f"w_raw{i}", KT * BC) for i in range(2)]
        w_hi = [sb(f"w_hi{i}", KT * BC, F32R) for i in range(2)]
        w_lo = [sb(f"w_lo{i}", KT * BC, F32R) for i in range(2)]
        ada_raw = sb("ada_raw", KT * BC)
        ada_acc = sb("ada_acc", 2 * BC)
        br_hi, br_lo = sb("br_hi", 2 * T, F32R), sb("br_lo", 2 * T, F32R)
        feat = [sb(f"feat{i}", T) for i in range(6)]
        vt = sb("vt", NCH * WB)
        bias = sb("bias", HEADS * NCH * 256)
        cos, sin, age = sb("cos", T), sb("sin", T), sb("age", T)
        wrk, prb = sb("wrk", 1280), sb("prb", 1280)
        tmp = sb("tmp", 2 * T)
        ident, neg_tri, neg_ones, ones, block_ones, rot = (
            sb(n, P) for n in ("ident", "neg_tri", "neg_ones", "ones", "block_ones", "rot"))
        mask_incl, mask_strict = sb("mask_incl", P), sb("mask_strict", P)
        sel = sb("sel", HEADS * P)
        sel_pair = sb("sel_pair", 2 * P)
        cols_a, cols_b = sb("cols_a", P), sb("cols_b", 56)
        c_act = sb("c_act", 8)
        gb, gb_cur = sb("gb", 4), sb("gb_cur", 2)
        sink_all, sink_cur = sb("sink_all", LAYERS * HEADS), sb("sink_cur", HEADS)
        mod = [sb("mod1", 24), sb("mod2", 24)]
        b_cur, g_cur, acol = sb("b_cur", 2 * ADA_REST), sb("g_cur", 16), sb("acol", 8)
        cw_cur, cb_cur, rg_cur, qk_cur = sb("cw_cur", 16), sb("cb_cur", 4), sb("rg_cur", 2), sb("qk_cur", 2)
        if_tok = sb("if_tok", NCH * 8)
        gcol = sb("gcol", NCH * HEADS)
        stat = sb("stat", 5 * NCH)

        ada_ring = (ada_raw[:, :], gates[:, 0:KT * BC], gates[:, KT * BC:2 * KT * BC])
        ada_ring_landed = ("ada_landed", "ada_landed_b", "ada_landed_c")
        tmps = [tmp[:, 0:T], tmp[:, T:2 * T]]
        x_rows = merged
        x_out = [merged[:, m * D:(m + 1) * D] for m in range(NCH)]
        own_mask = prb[:, 512:512 + P]
        vec_a, vec_b = tmp[:, 0:P], tmp[:, P:2 * P]
        row_i, row_f, row_t, row_a, row_m, row_am = (merged[0:HEADS, n * T:(n + 1) * T] for n in range(6))
        row_one = merged[0:HEADS, 6 * T:7 * T]

        def xk(k):
            return xt[:, k * T:(k + 1) * T]

        def part(t, k):
            return t[:, k * T:(k + 1) * T]

        def gate_tile(k):
            return gates[:, k * T:(k + 1) * T]

        def w_src(block, layer):
            name = block[0]
            ly = bass.ds(layer, 1)
            if name == "up":
                return w_up[ly, block[1]].rearrange("o (k p) n -> p (o k) n", p=P)
            if name == "out":
                return w_out[ly, :, block[1] * BC:(block[1] + 1) * BC].rearrange("o (k p) n -> p (o k) n", p=P)
            c0 = COLS[name] + (block[1] * D + block[2] * BC if name == "gate" else 0)
            n = 8 if name == "m_if" else BC
            return w_in[ly, :, c0:c0 + n].rearrange("o (k p) n -> p (o k) n", p=P)

        def w_view(t, block):
            if block[0] == "up":
                return t[:, :].rearrange("p (k n) -> p k n", k=2)
            if block[0] == "m_if":
                return t[:, 0:KT * 8].rearrange("p (k n) -> p k n", k=KT)
            return t[:, :].rearrange("p (k n) -> p k n", k=KT)

        def w_flat(t, block):
            return t[:, 0:KT * 8] if block[0] == "m_if" else t[:, :]

        def k_cols(h):
            return feat[2 + h // 2]

        def rows(h):
            r = HD * (h % 2)
            return slice(r, r + HD)

        FF = [("ff1", j) for j in range(4)] + [("ff2", j) for j in range(4)]
        programs = []
        block = ctx.enter_context(nc.Block())

        @block.sync
        def _(sp):
            p = Program(sp, sems)
            programs.append(("sp", p))
            n_small = 0

            def small(dst, src, scattered=False):
                nonlocal n_small
                n_small += 1
                sp.dma_start(dst, src, allow_slow_non_contiguous=scattered).then_inc(sems["vectors_loaded"], 16)

            def rows_of(a):
                return a.rearrange("(r p) -> r p", p=P)

            small(vec_a[0:96, :], b_ada.rearrange("l j (c p) -> (l j c) p", p=P))
            small(vec_a[96:128, :], norm_g.rearrange("l j (c p) -> (l j c) p", p=P))
            small(vec_b[0:32, :], conv_w.rearrange("l k (m p) -> (l k m) p", p=P))
            small(vec_b[32:40, :], conv_b.rearrange("l (m p) -> (l m) p", p=P))
            small(vec_b[40:44, :], ret_g.rearrange("l (m p) -> (l m) p", p=P))
            small(vec_b[44:52, :], c.rearrange("b (m p) -> (b m) p", p=P))
            for half in range(2):
                small(vec_b[52:54, half * HD:(half + 1) * HD], q_g)
                small(vec_b[54:56, half * HD:(half + 1) * HD], k_g)
            for m in range(NCH):
                sp.dma_start(x_rows[:, m * D:(m + 1) * D], x[0, m * P:(m + 1) * P, :]).then_inc(sems["x_landed"], 16)
            small(gb[0:HEADS, :], gate_b.rearrange("l j h -> h (l j)"), True)
            small(sink_all[:, :], sinks.rearrange("l h -> (l h)").partition_broadcast(P))
            small(wrk[:, 0:T].bitcast(I32), positions.rearrange("b t -> (b t)").partition_broadcast(P))
            small(wrk[:, 1024:1028].bitcast(I32), positions.rearrange("b (i p) -> p (b i)", p=P), True)
            small(prb[:, 1024:1152], rel_bias.rearrange("b h -> (b h)").partition_broadcast(P))
            small(prb[:, 1184:1185], rope_freq)
            assert 16 * n_small == VECTORS, n_small

            def load_ada(src, u):
                sp.wait_ge(sems["ada_partial"], p.value("ada_partial", u))
                if p.quarter is None and u == 0:
                    sp.wait_ge(sems["aux_ready"], 3)
                sp.dma_start(ada_raw[:, :].rearrange("p (k n) -> p k n", k=KT), src).then_inc(*p.count("ada_landed", by=16))

            def load_block(b, src, blk):
                s = b % 2
                sp.wait_ge(sems[f"lo_ready{s}"], p.value(f"lo_ready{s}", b // 2))
                sp.dma_start(w_view(w_raw[s], blk), src).then_inc(*p.count(f"raw_landed{s}", by=16))

            p.enter()
            for u in range(ADA_FIRST):
                if u >= 3:
                    sp.wait_ge(sems["ada_used"], u - 2)
                sp.dma_start(ada_ring[u % 3].rearrange("p (k n) -> p k n", k=KT),
                             w_ada[0, 0, :, u * BC:(u + 1) * BC].rearrange("(k p) n -> p k n", p=P)).then_inc(
                    *p.count(ada_ring_landed[u % 3], by=16))
            p.leave("before")
            with sp.Fori(0, LAYERS) as layer:
                p.enter(layer)
                for b, blk in enumerate(BLOCKS):
                    if b - 2 in ADA_BLOCK:
                        u = ADA_BLOCK.index(b - 2)
                        j, c0 = divmod(2 * D + u * BC, 3 * D)
                        load_ada(w_ada[bass.ds(layer, 1), j, :, c0:c0 + BC].rearrange("o (k p) n -> p (o k) n", p=P), u)
                    load_block(b, w_src(blk, layer), blk)
                p.leave("layer")
                with sp.Fori(0, QUARTERS) as q:
                    p.enter(layer, q)
                    for b, blk in enumerate(FF):
                        if b - 2 in FF_ADA:
                            load_ada(w_ada[1, 0, :, bass.ds(q * (2 * BC) + FF_ADA[b - 2] * BC, BC)].rearrange(
                                "(k p) n -> p k n", p=P), FF_ADA[b - 2])
                        ly = bass.ds(layer, 1)
                        if blk[0] == "ff1":
                            src = w_ff1[ly, :, bass.ds(q * D + blk[1] * BC, BC)]
                        else:
                            src = w_ff2[ly, bass.ds(q * D, D), blk[1] * BC:(blk[1] + 1) * BC]
                        load_block(b, src.rearrange("o (k p) n -> p (o k) n", p=P), blk)
                    p.leave("quarter")
            sp.wait_ge(sems["lo_ready0"], after_layers("lo_ready0"))
            sp.dma_start(w_raw[0][:, 0:1], rope_freq).then_inc(sems["raw_landed0"], 16)
            for m in range(NCH):
                sp.wait_ge(sems["xt_taken"], 2 * (m + 1))
                sp.dma_start(out[0, m * P:(m + 1) * P, :], x_out[m]).then_inc(sems["stored"], 16)
            sp.wait_ge(sems["stored"], 16 * NCH)

        @block.gpsimd
        def _(pool):
            p = Program(pool, sems, "pool_order")
            programs.append(("pool", p))
            g = nc.gpsimd
            p.enter()

            def keep(t, op, fill, base, pattern, mult):
                pool.wait_ge(*p.last)
                g.affine_select(out=t, in_=t, compare_op=op, fill=fill, base=base, pattern=pattern,
                                channel_multiplier=mult).then_inc(*p.count())

            g.memset(ident[:, :], 1.0).then_inc(*p.count())
            g.memset(neg_tri[:, :], -1.0).then_inc(*p.count())
            g.memset(neg_ones[:, :], -1.0).then_inc(*p.count())
            g.memset(ones[:, :], 1.0).then_inc(*p.count())
            g.memset(block_ones[:, :], 0.0).then_inc(*p.count())
            g.memset(mask_incl[:, :], 0.0).then_inc(*p.count())
            g.memset(mask_strict[:, :], 0.0).then_inc(*p.count())
            g.memset(sel[0:HEADS, :], 1.0).then_inc(*p.count())
            g.memset(sel_pair[0:HEADS, :], 1.0).then_inc(*p.count())
            rv = rot[:, :].rearrange("p (a b c) -> p a b c", a=2, b=2)
            g.memset(rv[:, :, 0, :], -1.0).then_inc(*p.count())
            g.memset(rv[:, :, 1, :], 1.0).then_inc(*p.count())
            g.iota(age[:, :], pattern=[[1, T]], base=0, channel_multiplier=-1,
               allow_small_or_imprecise_dtypes=True).then_inc(*p.count())
            pool.wait_ge(*p.last)
            g.memset(block_ones[0:HD, 0:HD], 1.0).then_inc(*p.count())
            g.memset(block_ones[HD:P, HD:P], 1.0).then_inc(*p.count())
            keep(ident[:, :], ALU.is_equal, 0.0, 0, [[-1, P]], 1)
            keep(neg_tri[:, :], ALU.is_ge, 0.0, 0, [[-1, P]], 1)
            keep(mask_incl[:, :], ALU.is_ge, -BIG, 0, [[1, P]], -1)
            keep(mask_strict[:, :], ALU.is_gt, -BIG, 0, [[1, P]], -1)
            keep(sel[0:HEADS, :].rearrange("p (h n) -> p h n", h=HEADS), ALU.is_equal, 0.0, 0,
                 [[-1, HEADS], [0, P]], 1)
            keep(sel_pair[0:HEADS, :].rearrange("p (a b n) -> p a b n", a=2, b=2), ALU.is_equal, 0.0, 0,
                 [[-2, 2], [-1, 2], [0, HD]], 1)
            keep(rv[:, :, 0, :], ALU.is_equal, 0.0, -32, [[-HD, 2], [-1, 32]], 1)
            keep(rv[:, :, 1, :], ALU.is_equal, 0.0, 0, [[-HD, 2], [-1, 32]], 1)
            keep(age[:, :], ALU.is_ge, 1.0e6, 0, [[1, T]], -1)
            pool.wait_ge(*p.last)
            g.memset(own_mask, 1.0).then_inc(*p.count())
            keep(own_mask, ALU.is_ge, 0.0, 0, [[-1, P]], 1)
            pool.wait_ge(*p.last)
            g.memset(c_act[:, :], 0.0).then_inc(*p.count("consts_ready"))
            p.leave("before")

            def lo_part(b, blk):
                s = b % 2
                pool.wait_ge(sems[f"hi_ready{s}"], p.value(f"hi_ready{s}", b // 2 + 1))
                g.tensor_tensor(w_flat(w_lo[s], blk), w_flat(w_raw[s], blk),
                                w_flat(w_hi[s], blk).bitcast(F32), ALU.subtract).then_inc(*p.count(f"lo_ready{s}"))

            with pool.Fori(0, LAYERS) as layer:
                p.enter(layer)
                for b, blk in enumerate(BLOCKS):
                    lo_part(b, blk)
                p.leave("layer")
                with pool.Fori(0, QUARTERS) as q:
                    p.enter(layer, q)
                    for b, blk in enumerate(FF):
                        lo_part(b, blk)
                    p.leave("quarter")

        @block.tensor
        def _(pe):
            p = Program(pe, sems)
            programs.append(("pe", p))
            mm = nc.tensor.matmul

            def wait_bank(tile):
                pe.wait_ge(sems[f"bank_taken{tile % 2}"], p.value(f"bank_taken{tile % 2}", tile // 2))

            def tile_done(ins, tile):
                ins.then_inc(*p.count(f"bank_ready{tile % 2}"))

            def aux_free(n):
                pe.wait_ge(sems["aux_taken"], p.value("aux_taken", n))

            def three(o, wh, wl, xh, xl, first, last):
                mm(o, wh, xh, start=first, stop=False, skip_group_check=True)
                mm(o, wh, xl, start=False, stop=False, skip_group_check=True)
                return mm(o, wl, xh, start=False, stop=last, skip_group_check=True)

            def feature_tile(b, half, tile, rhs, wait_k=None, kn=KT, blk=("x",)):
                s = b % 2
                wh, wl = w_view(w_hi[s], blk), w_view(w_lo[s], blk)
                cs = slice(half * P, (half + 1) * P)
                wait_bank(tile)
                for k in range(kn):
                    if wait_k is not None:
                        wait_k(k)
                    last = three(gemm[tile % 2][:, :], wh[:, k, cs], wl[:, k, cs], part(rhs[0], k), part(rhs[1], k),
                                 k == 0, k == kn - 1)
                return last

            def token_tile(b, half, tile, blk, chunks, cs):
                s = b % 2
                wh, wl = w_view(w_hi[s], blk), w_view(w_lo[s], blk)
                n = cs.stop - cs.start
                wait_bank(tile)
                for i, ch in enumerate(chunks):
                    for k in range(KT):
                        t0 = k * T + ch * CH
                        last = three(gemm[tile % 2][:, i * n:(i + 1) * n], h_hi[:, t0:t0 + CH], h_lo[:, t0:t0 + CH],
                                     wh[:, k, cs], wl[:, k, cs], k == 0, k == KT - 1)
                return last

            p.enter()
            pe.wait_ge(sems["consts_ready"], 1)
            pe.wait_ge(sems["vectors_loaded"], VECTORS)
            nc.tensor.transpose(aux[:, 0:P], vec_a, ident[:, :]).then_inc(*p.count("aux_ready"))
            pe.wait_ge(sems["aux_taken"], p.value("aux_taken", 1))
            mm(aux[:, 0:56], vec_b[0:56, :], ident[0:56, 0:56], start=True, stop=True).then_inc(*p.count("aux_ready"))
            pe.wait_ge(sems["x_landed"], 16 * NCH)
            for k in range(KT):
                if k >= 2:
                    wait_bank(k)
                for m in range(NCH):
                    ins = nc.tensor.transpose(gemm[k % 2][:, m * P:(m + 1) * P],
                                              x_rows[:, m * D + k * P:m * D + (k + 1) * P], ident[:, :])
                tile_done(ins, k)

            def ada_sum(u, n_aux):
                aux_free(n_aux)
                pe.wait_ge(sems["ada_partial"], p.value("ada_partial", u + 1))
                for col in range(2):
                    for a in range(2):
                        c0 = a * BC + col * P
                        ins = mm(aux[:, col:col + 1], ada_acc[:, c0:c0 + P], ones[:, 0:1], start=(a == 0), stop=(a == 1))
                ins.then_inc(*p.count("aux_ready"))

            aux_free(2)
            pe.wait_ge(sems["c_act_ready"], 1)
            for u in range(ADA_FIRST):
                landed = ada_ring_landed[u % 3]
                pe.wait_ge(sems[landed], 16 * (u // 3 + 1))
                for col in range(2):
                    for k in range(KT):
                        c0 = k * BC + col * P
                        ins = mm(aux[:, 2 * u + col:2 * u + col + 1], ada_ring[u % 3][:, c0:c0 + P], c_act[:, k:k + 1],
                                 start=(k == 0), stop=(k == KT - 1), skip_group_check=True)
                ins.then_inc(*p.count("ada_used" if u < ADA_FIRST - 1 else "aux_ready"))
            p.leave("before")

            def scores_triangle(h, first):
                r = rows(h)
                for j in (0, 1, 3, 2):
                    o = score[SC_BANK[j]][:, SC_COL[j]:SC_COL[j] + LEN[j]]
                    ins = mm(o, k_cols(h)[r, j * CH:(j + 1) * CH], feat[h // 2][r, j * CH:T],
                             start=(j != 3), stop=not first, skip_group_check=True)
                    if first:
                        ins = mm(o[:, 0:CH], ident[:, :], mask_strict[:, :], start=False, stop=False,
                                 skip_group_check=True)
                return ins

            def pv_triangle(h):
                r = rows(h)
                for j in range(NCH):
                    ins = mm(outp[r, j * CH:T], vt[:, j * WB + h * HD:j * WB + (h + 1) * HD],
                             prb[:, OFF[j]:OFF[j] + LEN[j]], start=(j == 0), stop=(j == NCH - 1),
                             skip_group_check=True)
                return ins

            def step(s):
                kind = s[0]
                if kind == "norm":
                    n0 = s[1] * KT
                    aux_free(AUX[s])
                    for k in range(KT):
                        pe.wait_ge(sems["square_ready"], p.value("square_ready", n0 + k + 1 + (5 if s[1] else 0)))
                        ins = mm(aux[:, :], ones[:, :], tmps[k % 2], start=(k == 0), stop=(k == KT - 1))
                        if k < KT - 1:
                            ins.then_inc(*p.count("square_used"))
                    ins.then_inc(*p.count("aux_ready"))
                elif kind == "tile":
                    tile_step(s)
                elif kind == "ifrows":
                    aux_free(AUX[s])
                    for half in range(2):
                        tl = TILE_NO[(BLOCK_NO[("m_if",)], half)]
                        pe.wait_ge(sems[f"bank_taken{tl % 2}"], p.value(f"bank_taken{tl % 2}", tl // 2 + 1))
                    for n, dst in ((0, aux), (HEADS, denp)):
                        for i in range(NCH):
                            ins = mm(dst[0:HEADS, i * CH:(i + 1) * CH], if_tok[:, i * 8 + n:i * 8 + n + HEADS],
                                     ident[:, :], start=True, stop=True)
                    ins.then_inc(*p.count("aux_ready"))
                elif kind == "gcol":
                    aux_free(AUX[s])
                    pe.wait_ge(sems["rows_ready"], p.value("rows_ready", 1))
                    for i in range(NCH):
                        ins = mm(aux[:, i * HEADS:(i + 1) * HEADS], row_i[:, i * CH:(i + 1) * CH],
                                 ident[0:HEADS, 0:HEADS], start=True, stop=True)
                    ins.then_inc(*p.count("aux_ready"))
                elif kind == "qk":
                    _, n, h = s
                    g = 4 * n + h
                    if n == 0:
                        if h == 0:
                            pe.wait_ge(sems["feature_ready"], p.value("feature_ready", 4))
                        aux_free(AUX[s])
                        mm(aux[:, :], sel[0:HEADS, h * P:(h + 1) * P], row_m, start=True, stop=True).then_inc(*p.count("aux_ready"))
                    if n == 1 and h == 0:
                        pe.wait_ge(sems["feature_ready"], p.value("feature_ready", 8))
                    if n == 3 and h == 0:
                        pe.wait_ge(sems["feature_ready"], p.value("feature_ready", 11))
                    if n == 2 and h == 0:
                        for half in range(2):
                            tl = TILE_NO[(BLOCK_NO[("s_k",)], half)]
                            pe.wait_ge(sems[f"bank_taken{tl % 2}"], p.value(f"bank_taken{tl % 2}", tl // 2 + 1))
                    pe.wait_ge(sems["scores_taken"], p.value("scores_taken", g))
                    if n < 3:
                        scores_triangle(h, n == 2).then_inc(*p.count("qk_ready"))
                    else:
                        r, kd = rows(h), feat[3 + h // 2]
                        for i in range(NCH):
                            q = feat[h // 2][r, i * CH:(i + 1) * CH]
                            o = score[i // 2][:, (i % 2) * 256:(i % 2) * 256 + 256]
                            if i == 0:
                                mm(o[:, 0:CH], q, kd[r, CH:2 * CH], start=True, stop=True)
                                ins = mm(o[:, CH:256], q, kd[r, 0:CH], start=True, stop=True)
                            else:
                                ins = mm(o, q, kd[r, (i - 1) * CH:(i + 1) * CH], start=True, stop=True)
                        ins.then_inc(*p.count("qk_ready"))
                elif kind == "suffix":
                    h = s[1]
                    pe.wait_ge(sems["softplus_ready"], p.value("softplus_ready", h + 1))
                    for j in range(NCH):
                        for j2 in range(j, NCH):
                            c0 = SC_COL[j] + (j2 - j) * CH
                            last = mm(score[SC_BANK[j]][:, c0:c0 + LEN[j2]], (neg_tri if j2 == j else neg_ones)[:, :],
                                      wrk[:, OFF[j2]:OFF[j2] + LEN[j2]], start=False, stop=(j2 == NCH - 1),
                                      skip_group_check=True)
                    last.then_inc(*p.count("suffix_ready"))
                elif kind == "ptrans":
                    h = s[1]
                    pe.wait_ge(sems["probs_ready"], p.value("probs_ready", h + 1))
                    if h >= 1:
                        pe.wait_ge(sems["ptrans_copied"], p.value("ptrans_copied", h))
                    for n, (i, half) in enumerate(PT_BLOCKS):
                        dst = (score[2] if n < 4 else denp)[:, (n % 4) * CH:(n % 4 + 1) * CH]
                        c0 = i * 256 + half * CH
                        ins = nc.tensor.transpose(dst, prb[:, c0:c0 + CH], ident[:, :])
                    ins.then_inc(*p.count("ptrans_ready"))
                elif kind == "pv":
                    _, n, h = s
                    g = 4 * n + h
                    r = rows(h)
                    if h % 2 == 0:
                        pe.wait_ge(sems["branch_ready"], p.value("branch_ready", 2 * n + h // 2))
                    if h == 0:
                        v = "a_kv" if n == 3 else ("m_v", "r_v", "s_v")[n]
                        for half in range(2):
                            tl = TILE_NO[(BLOCK_NO[(v,)], half)]
                            pe.wait_ge(sems[f"bank_taken{tl % 2}"], p.value(f"bank_taken{tl % 2}", tl // 2 + 1))
                    if n < 3:
                        pe.wait_ge(sems["scores_taken"], p.value("scores_taken", g + 1))
                        if n == 0:
                            for j in range(NCH):
                                ins = mm(denp[r, j * CH:T], ones[:, 0:HD], prb[:, OFF[j]:OFF[j] + LEN[j]],
                                         start=(j == 0), stop=(j == NCH - 1), skip_group_check=True)
                        pv_triangle(h).then_inc(*p.count("pv_ready"))
                        if s in AUX:
                            aux_free(AUX[s])
                            pr = h // 2
                            mm(aux[:, :], sel_pair[0:HEADS, pr * P:(pr + 1) * P], row_am,
                               start=True, stop=True).then_inc(*p.count("aux_ready"))
                    else:
                        pe.wait_ge(sems["ptrans_copied"], p.value("ptrans_copied", h + 1))
                        for m, (i, half) in enumerate(PT_BLOCKS):
                            v0 = (i - 1 + half) * WB + (h // 2) * HD
                            ins = mm(outp[r, i * CH:(i + 1) * CH], vt[:, v0:v0 + HD], tmp[:, m * CH:(m + 1) * CH],
                                     start=(half == 0 or i == 0), stop=(half == 1), skip_group_check=True)
                        ins.then_inc(*p.count("pv_ready"))
                elif kind == "rot":
                    i = s[1]
                    aux_free(AUX[s])
                    pe.wait_ge(sems["rot_raw"], p.value("rot_raw", i + 1))
                    mm(aux[:, :], rot[:, :], part(wrk, i % 2), start=True, stop=True).then_inc(*p.count("aux_ready"))
                elif kind in ("hnorm", "anorm"):
                    i = s[1]
                    aux_free(AUX[s])
                    pe.wait_ge(sems["square_ready"], p.value("square_ready", KT + (i + 1 if kind == "hnorm" else 3 + i)))
                    t = tmps[0] if kind == "hnorm" else tmps[i % 2]
                    mm(aux[:, :], block_ones[:, :], t, start=True, stop=True).then_inc(*p.count("aux_ready"))
                elif kind == "adasum":
                    ada_sum(s[1], AUX[s])

            def tile_step(s):
                _, b, half = s
                blk = BLOCKS[b]
                name = blk[0]
                tile = TILE_NO[(b, half)]
                sl = b % 2
                if half == 0:
                    pe.wait_ge(sems[f"lo_ready{sl}"], p.value(f"lo_ready{sl}", b // 2 + 1))
                if name in ("m_v", "r_v", "s_v"):
                    ins = token_tile(b, half, tile, blk, (2 * half, 2 * half + 1), slice(0, BC))
                elif name == "m_if":
                    ins = token_tile(b, half, tile, blk, (2 * half, 2 * half + 1), slice(0, 8))
                elif name == "a_kv" and half == 1:
                    ins = token_tile(b, half, tile, blk, range(NCH), slice(P, 2 * P))
                elif name == "up":
                    if half == 0:
                        pe.wait_ge(sems["branch_ready"], p.value("branch_ready", 2 * blk[1] + 2))
                    ins = feature_tile(b, half, tile, (br_hi, br_lo), kn=2, blk=blk)
                elif blk == ("out", 0) and half == 0:
                    ins = feature_tile(b, half, tile, (h_hi, h_lo), lambda k: pe.wait_ge(sems["merged_ready"], p.value("merged_ready", k + 1)))
                elif name == "m_q" and half == 0:
                    ins = feature_tile(b, half, tile, (h_hi, h_lo), lambda k: pe.wait_ge(sems["h_ready"], p.value("h_ready", k + 1)))
                else:
                    ins = feature_tile(b, half, tile, (h_hi, h_lo))
                tile_done(ins, tile)

            with pe.Fori(0, LAYERS) as layer:
                p.enter(layer)
                for s in STEPS:
                    step(s)
                p.leave("layer")
                with pe.Fori(0, QUARTERS) as q:
                    p.enter(layer, q)
                    for b, blk in enumerate(FF):
                        pe.wait_ge(sems[f"lo_ready{b % 2}"], p.value(f"lo_ready{b % 2}", b // 2 + 1))
                        for half in range(2):
                            tile = 2 * b + half
                            if blk[0] == "ff1":
                                first = lambda k: pe.wait_ge(sems["h_ready"], at("h_ready", KT + k + 1, layer))
                                ins = feature_tile(b, half, tile, (h_hi, h_lo), first if tile == 0 else None)
                            else:
                                first = lambda k: pe.wait_ge(sems["hidden_ready"], p.value("hidden_ready", k + 1))
                                ins = feature_tile(b, half, tile, (hid_hi, hid_lo), first if tile == 8 else None)
                            tile_done(ins, tile)
                            if half == 0 and b in FF_ADASUM:
                                u = FF_ADASUM[b]
                                ada_sum(u, u)
                    p.leave("quarter")

            p.tail = True
            for m in range(NCH):
                for half in range(2):
                    n = 2 * m + half
                    if n == 0:
                        for b2 in range(2):
                            pe.wait_ge(sems[f"bank_taken{b2}"], after_layers(f"bank_taken{b2}"))
                    if n >= 2:
                        pe.wait_ge(sems["xt_taken"], n - 1)
                    for k in range(4):
                        kk = 4 * half + k
                        ins = nc.tensor.transpose(gemm[n % 2][:, k * P:(k + 1) * P],
                                                  xt[:, kk * T + m * P:kk * T + (m + 1) * P], ident[:, :])
                    ins.then_inc(sems["xt_ready"], 1)

        @block.scalar
        def _(act):
            p = Program(act, sems, "act_order")
            programs.append(("act", p))
            a = nc.scalar.activation

            def hi_part(b, blk, tiles_through):
                s = b % 2
                act.wait_ge(sems[f"raw_landed{s}"], p.value(f"raw_landed{s}", 16 * (b // 2 + 1)))
                if tiles_through is not None:
                    act.wait_ge(sems["bank_ready1"], p.value("bank_ready1", tiles_through // 2))
                nc.scalar.copy(w_flat(w_hi[s], blk), w_flat(w_raw[s], blk)).then_inc(*p.count(f"hi_ready{s}", n=b // 2 + 1))

            def rstd(n, scale, dst):
                act.wait_ge(sems["aux_ready"], p.value("aux_ready", n + 1))
                a(dst, aux[:, :], ACT.Ln, scale=scale, bias=EPS).then_inc(*p.count("aux_taken", n=n + 1))
                act.wait_ge(*p.last)
                a(dst, dst, ACT.Exp, scale=-0.5).then_inc(*p.count("rstd_ready"))

            def branch_hi(n, pair, src, scale):
                if n >= 1 and pair == 0:
                    up = TILE_NO[(BLOCK_NO[("up", n - 1)], 7)]
                    act.wait_ge(sems[f"bank_ready{up % 2}"], p.value(f"bank_ready{up % 2}", up // 2 + 1))
                nc.scalar.mul(part(br_hi, pair), src, scale).then_inc(*p.count("branch_hi_ready"))

            p.enter()
            act.wait_ge(sems["aux_taken"], p.value("aux_taken", 2))
            a(stat[:, 0:8], cols_b[:, 44:52], ACT.Tanh, scale=0.5).then_inc(*p.count("c_tanh"))
            for k in range(KT):
                act.wait_ge(sems[f"bank_ready{k % 2}"], p.value(f"bank_ready{k % 2}", k // 2 + 1))
                nc.scalar.copy(xk(k), gemm[k % 2][:, :]).then_inc(*p.count(f"bank_taken{k % 2}"))
            act.wait_ge(sems["angles_ready"], p.value("angles_ready", 1))
            a(sin[:, :], feat[0][:, :], ACT.Sin).then_inc(*p.count("sines_ready"))
            a(cos[:, :], feat[1][:, :], ACT.Sin).then_inc(*p.count("sines_ready"))
            hi_part(0, BLOCKS[0], None)
            p.leave("before")

            def step(s):
                kind = s[0]
                if kind in ("norm", "gate_tanh", "ifrows", "qk", "suffix", "ptrans", "hnorm", "anorm") or (
                        kind == "pv" and s[2] % 2 == 1):
                    act.wait_ge(*p.last)
                if kind == "norm":
                    j = s[1]
                    for k in range(KT):
                        if j == 0 and k == 0:
                            act.wait_ge(sems["bank_taken0"], p.value("bank_taken0", 0))
                            act.wait_ge(sems["bank_taken1"], p.value("bank_taken1", 0))
                        if j == 1:
                            tl = TILE_NO[(BLOCK_NO[("out", k // 2)], k % 2)]
                            act.wait_ge(sems[f"bank_taken{tl % 2}"], p.value(f"bank_taken{tl % 2}", tl // 2 + 1))
                        if k >= 2:
                            act.wait_ge(sems["square_used"], p.value("square_used", j * (KT - 1) + k - 1))
                        a(tmps[k % 2], xk(k), ACT.Square).then_inc(*p.count("square_ready"))
                    rstd(AUX[s], 1.0 / D, wrk[:, 0:T])
                    for k in range(KT):
                        act.wait_ge(sems["h_scaled"], p.value("h_scaled", j * KT + k + 1))
                        a(part(h_hi, k), part(prb, k % 2), ACT.Identity, bias=mod[j][:, k:k + 1]).then_inc(*p.count("h_hi_ready"))
                elif kind == "tile":
                    tile_step(s)
                elif kind == "gate_tanh":
                    for half in range(2):
                        tl = TILE_NO[(BLOCK_NO[("gate", s[1], 3)], half)]
                        act.wait_ge(sems[f"bank_taken{tl % 2}"], p.value(f"bank_taken{tl % 2}", tl // 2 + 1))
                    a(gates[:, :], gates[:, :], ACT.Tanh, scale=0.5).then_inc(*p.count("gate_ready"))
                elif kind == "ifrows":
                    act.wait_ge(sems["aux_taken"], p.value("aux_taken", AUX[s] + 1))
                    a(row_t, row_f, ACT.Abs).then_inc(*p.count())
                    act.wait_ge(*p.last)
                    a(row_t, row_t, ACT.Exp, scale=-1.0).then_inc(*p.count())
                    act.wait_ge(*p.last)
                    a(row_t, row_t, ACT.Ln, bias=1.0).then_inc(*p.count("logterm_ready"))
                elif kind == "qk":
                    _, n, h = s
                    g = 4 * n + h
                    if n == 0:
                        act.wait_ge(sems["aux_ready"], p.value("aux_ready", AUX[s] + 1))
                        act.wait_ge(sems["masked_ready"], p.value("masked_ready", h + 1))
                        act.wait_ge(sems["scores_taken"], p.value("scores_taken", g))
                        for j in range(NCH - 1):
                            o = wrk[:, OFF[j] + CH:OFF[j] + LEN[j]]
                            ins = a(o, aux[:, (j + 1) * CH:T], ACT.Exp, scale=-1.0,
                                    bias=gcol[:, j * HEADS + h:j * HEADS + h + 1])
                            if j < NCH - 2:
                                ins.then_inc(*p.count())
                            else:
                                ins.then_inc(*p.count("aux_taken", n=AUX[s] + 1))
                        for j in range(NCH):
                            ins = a(wrk[:, OFF[j]:OFF[j] + CH], tmps[0][:, j * CH:(j + 1) * CH], ACT.Exp,
                                    bias=gcol[:, j * HEADS + h:j * HEADS + h + 1])
                            ins.then_inc(*p.count("decay_ready" if j == NCH - 1 else None))
                    elif n == 1:
                        act.wait_ge(sems["scores_taken"], p.value("scores_taken", g))
                        if h == 0:
                            act.wait_ge(sems["feature_ready"], p.value("feature_ready", 8))
                        a(wrk[:, 0:T], age[:, :], ACT.Exp, scale=LOG_GAMMA[h]).then_inc(*p.count("decay_ready"))
                    elif n == 2:
                        act.wait_ge(sems["qk_ready"], p.value("qk_ready", g + 1))
                        for i, (c0, w) in enumerate(((0, T), (T, T), (2 * T, 256))):
                            a(wrk[:, c0:c0 + w], score[i][:, 0:w], ACT.Abs).then_inc(*p.count())
                        act.wait_ge(*p.last)
                        a(wrk[:, :], wrk[:, :], ACT.Exp, scale=-1.0).then_inc(*p.count())
                        act.wait_ge(*p.last)
                        a(wrk[:, :], wrk[:, :], ACT.Ln, bias=1.0).then_inc(*p.count("logterm_ready"))
                    else:
                        act.wait_ge(sems["negmax_ready"], p.value("negmax_ready", h + 1))
                        act.wait_ge(sems["ptrans_ready"], p.value("ptrans_ready", h))
                        act.wait_ge(sems["pv_ready"], p.value("pv_ready", 12))
                        for i in range(NCH):
                            a(prb[:, i * 256:(i + 1) * 256], wrk[:, i * 256:(i + 1) * 256], ACT.Exp,
                              bias=stat[:, NCH + i:NCH + i + 1],
                              accum_out=stat[:, 2 * NCH + i:2 * NCH + i + 1]).then_inc(*p.count())
                        a(stat[:, 3 * NCH:4 * NCH], stat[:, NCH:2 * NCH], ACT.Exp,
                          bias=sink_cur[:, h:h + 1]).then_inc(*p.count("exp_ready"))
                elif kind == "suffix":
                    h = s[1]
                    act.wait_ge(sems["suffix_ready"], p.value("suffix_ready", h + 1))
                    act.wait_ge(sems["pv_ready"], p.value("pv_ready", 8 + h))
                    for i, (c0, w) in enumerate(((0, T), (T, T), (2 * T, 256))):
                        a(prb[:, c0:c0 + w], score[i][:, 0:w], ACT.Exp).then_inc(*p.count("scores_taken" if i == 2 else None, n=8 + h + 1 if i == 2 else None))
                elif kind == "ptrans":
                    h = s[1]
                    act.wait_ge(sems["ptrans_ready"], p.value("ptrans_ready", h + 1))
                    act.wait_ge(sems["pv_ready"], p.value("pv_ready", 12 + h))
                    nc.scalar.copy(tmp[:, 0:T], score[2][:, :]).then_inc(*p.count())
                    nc.scalar.copy(tmp[:, T:7 * CH], denp[:, 0:3 * CH]).then_inc(*p.count("ptrans_copied"))
                elif kind == "pv" and s[2] % 2 == 1:
                    _, n, h = s
                    pair = h // 2
                    act.wait_ge(sems["pv_ready"], p.value("pv_ready", 4 * n + h + 1))
                    if n == 0:
                        act.wait_ge(sems["aux_ready"], p.value("aux_ready", AUX[s] + 1))
                        a(tmps[1], aux[:, :], ACT.Exp, scale=-1.0).then_inc(*p.count("aux_taken", n=AUX[s] + 1))
                        a(tmps[0], denp[:, :], ACT.Abs).then_inc(*p.count("den_ready"))
                        act.wait_ge(sems["out_scaled"], p.value("out_scaled", pair + 1))
                        branch_hi(n, pair, tmps[0], 0.5)
                    elif n == 1:
                        a(tmps[0], outp[:, :], ACT.Square).then_inc(*p.count("square_ready"))
                    else:
                        branch_hi(n, pair, outp[:, :], 1.0)
                elif kind == "hnorm":
                    rstd(AUX[s], 1.0 / HD, tmps[1])
                    act.wait_ge(sems["out_scaled"], p.value("out_scaled", 2 + s[1] + 1))
                    branch_hi(1, s[1], tmps[0], 0.5)
                elif kind == "anorm":
                    rstd(AUX[s], 1.0 / HD, tmps[s[1] % 2])

            def tile_step(s):
                _, b, half = s
                blk = BLOCKS[b]
                name = blk[0]
                tile = TILE_NO[(b, half)]
                bank, bn = gemm[tile % 2], tile // 2 + 1
                if half == 0:
                    nxt = BLOCKS[b + 1] if b + 1 < PRE_BLOCKS else FF[0]
                    hi_part(b + 1, nxt, TILES_BEFORE[b])
                act.wait_ge(*p.last)
                if name in ("m_q", "m_k"):
                    i = half + (2 if name == "m_k" else 0)
                    act.wait_ge(sems["conv_ready"], p.value("conv_ready", i + 1))
                    a(part(prb, i % 2), tmps[i % 2], ACT.Tanh, scale=0.5).then_inc(*p.count("silu_ready"))
                elif name == "m_o":
                    act.wait_ge(sems[f"bank_ready{tile % 2}"], p.value(f"bank_ready{tile % 2}", bn))
                    a(feat[4 + half][:, :], bank[:, :], ACT.Tanh, scale=0.5).then_inc(*p.count(f"bank_taken{tile % 2}", n=bn))
                elif name in ("m_v", "r_v", "s_v"):
                    act.wait_ge(sems[f"bank_ready{tile % 2}"], p.value(f"bank_ready{tile % 2}", bn))
                    nc.scalar.copy(vt[:, half * 2 * WB:(half + 1) * 2 * WB], bank[:, :]).then_inc(*p.count(f"bank_taken{tile % 2}", n=bn))
                elif name == "a_kv" and half == 1:
                    act.wait_ge(sems[f"bank_ready{tile % 2}"], p.value(f"bank_ready{tile % 2}", bn))
                    nc.scalar.copy(vt[:, :].rearrange("p (i n) -> p i n", i=NCH)[:, :, 0:P],
                                   bank[:, :].rearrange("p (i n) -> p i n", i=NCH)).then_inc(*p.count(f"bank_taken{tile % 2}", n=bn))
                elif name in ("r_q", "r_k"):
                    i = half + (2 if name == "r_k" else 0)
                    act.wait_ge(sems[f"bank_ready{tile % 2}"], p.value(f"bank_ready{tile % 2}", bn))
                    if i < 2:
                        act.wait_ge(sems["scores_taken"], p.value("scores_taken", 4))
                    else:
                        act.wait_ge(sems["feature_ready"], p.value("feature_ready", 4 + i - 1))
                    nc.scalar.copy(part(wrk, i % 2), bank[:, :]).then_inc(*p.count("rot_raw"))
                elif name == "r_g":
                    act.wait_ge(sems[f"bank_ready{tile % 2}"], p.value(f"bank_ready{tile % 2}", bn))
                    a(tmps[half], bank[:, :], ACT.Tanh, scale=0.5).then_inc(*p.count("silu_ready"))
                elif name == "a_q" or (name == "a_kv" and half == 0):
                    i = half + (2 if name == "a_kv" else 0)
                    act.wait_ge(sems[f"bank_taken{tile % 2}"], p.value(f"bank_taken{tile % 2}", bn))
                    if i == 2:
                        act.wait_ge(sems["feature_ready"], p.value("feature_ready", 9))
                    a(tmps[i % 2], feat[i][:, :], ACT.Square).then_inc(*p.count("square_ready"))
                elif name == "up" and blk[1] == 3:
                    act.wait_ge(sems["merged_tile"], p.value("merged_tile", half + 1))
                    nc.scalar.mul(part(h_hi, half), part(merged, half), 0.5).then_inc(*p.count("merged_hi_ready"))

            with act.Fori(0, LAYERS) as layer:
                p.enter(layer)
                for s in STEPS:
                    step(s)
                p.leave("layer")
                with act.Fori(0, QUARTERS) as q:
                    p.enter(layer, q)
                    for b, blk in enumerate(FF):
                        hi_part(b + 1, ("x",), 2 * b)
                        if blk[0] == "ff1":
                            for half in range(2):
                                tile = 2 * b + half
                                act.wait_ge(sems[f"bank_ready{tile % 2}"], p.value(f"bank_ready{tile % 2}", tile // 2 + 1))
                                a(tmps[tile % 2], gemm[tile % 2][:, :], ACT.Relu).then_inc(*p.count("relu_ready"))
                                act.wait_ge(sems[f"bank_taken{tile % 2}"], p.value(f"bank_taken{tile % 2}", tile // 2 + 1))
                                nc.scalar.copy(part(hid_hi, tile), part(prb, tile % 2)).then_inc(*p.count("hidden_hi_ready"))
                    p.leave("quarter")

        @block.vector
        def _(dve):
            p = Program(dve, sems, "dve_order")
            programs.append(("dve", p))
            v = nc.vector
            stt = v.scalar_tensor_tensor

            def ada_unit(u):
                dve.wait_ge(sems["ada_landed"], p.value("ada_landed", 16 * (u + 1)))
                for k in range(KT):
                    acc = ada_acc[:, (k % 2) * BC:(k % 2 + 1) * BC]
                    w = ada_raw[:, k * BC:(k + 1) * BC]
                    if k < 2:
                        ins = v.tensor_scalar(acc, w, c_act[:, k:k + 1], None, ALU.mult)
                    else:
                        dve.wait_ge(*p.last)
                        ins = stt(out=acc, in0=w, scalar=c_act[:, k:k + 1], in1=acc, op0=ALU.mult, op1=ALU.add)
                    ins.then_inc(*p.count("ada_partial" if k == KT - 1 else None))

            def ada_mod(n_aux, dst, b_col):
                dve.wait_ge(sems["aux_ready"], p.value("aux_ready", n_aux + 1))
                v.tensor_tensor(dst, aux[:, 0:2], b_col, ALU.add).then_inc(*p.count("aux_taken", n=n_aux + 1))

            p.enter()
            dve.wait_ge(sems["aux_ready"], p.value("aux_ready", 1))
            v.tensor_copy(cols_a[:, :], aux[:, 0:P]).then_inc(*p.count("aux_taken"))
            dve.wait_ge(sems["aux_ready"], p.value("aux_ready", 2))
            v.tensor_copy(cols_b[:, :], aux[:, 0:56]).then_inc(*p.count("aux_taken"))
            dve.wait_ge(sems["c_tanh"], p.value("c_tanh", 1))
            dve.wait_ge(*p.last)
            stt(out=c_act[:, :], in0=stat[:, 0:8], scalar=1.0, in1=cols_b[:, 44:52], op0=ALU.add, op1=ALU.mult).then_inc(*p.count())
            dve.wait_ge(*p.last)
            v.tensor_scalar(c_act[:, :], c_act[:, :], 0.5, None, ALU.mult).then_inc(*p.count("c_act_ready"))

            s_arg, c_arg, ang, turns, pos = (feat[n][:, :] for n in range(5))
            own, prev, pos_col = ang, turns, feat[5][:, 0:NCH]
            rel_rows, freq = prb[:, 1024:1152], prb[:, 1184:1185]
            TWO_PI = (6.28125, 0.0019350051879882812, 2.0 * math.pi - 6.28125 - 0.0019350051879882812)
            LIMIT = 3.1415925
            dve.wait_ge(sems["vectors_loaded"], VECTORS)
            v.tensor_copy(pos, wrk[:, 0:T].bitcast(I32)).then_inc(*p.count())
            v.tensor_copy(pos_col, wrk[:, 1024:1028].bitcast(I32)).then_inc(*p.count())
            dve.wait_ge(*p.last)
            v.tensor_scalar(ang, pos, freq, None, ALU.mult).then_inc(*p.count())
            dve.wait_ge(*p.last)
            v.tensor_scalar(turns, ang, 1.0 / (2.0 * math.pi), 12582912.0, ALU.mult, ALU.add).then_inc(*p.count())
            dve.wait_ge(*p.last)
            v.tensor_scalar(turns, turns, 12582912.0, None, ALU.subtract).then_inc(*p.count())
            for n, piece in enumerate(TWO_PI):
                dve.wait_ge(*p.last)
                stt(out=s_arg, in0=turns, scalar=-piece, in1=(ang if n == 0 else s_arg), op0=ALU.mult,
                    op1=ALU.add).then_inc(*p.count())
            dve.wait_ge(*p.last)
            v.tensor_scalar(c_arg, s_arg, math.pi / 2, -2.0 * math.pi, ALU.is_gt, ALU.mult).then_inc(*p.count())
            dve.wait_ge(*p.last)
            stt(out=c_arg, in0=s_arg, scalar=math.pi / 2, in1=c_arg, op0=ALU.add, op1=ALU.add).then_inc(*p.count())
            dve.wait_ge(*p.last)
            v.tensor_scalar(c_arg, c_arg, LIMIT, -LIMIT, ALU.min, ALU.max).then_inc(*p.count())
            dve.wait_ge(*p.last)
            v.tensor_scalar(s_arg, s_arg, LIMIT, -LIMIT, ALU.min, ALU.max).then_inc(*p.count("angles_ready"))

            dve.wait_ge(*p.last)
            for i in range(NCH):
                blk_i = slice(i * CH, (i + 1) * CH)
                blk_p = slice(max(i - 1, 0) * CH, (max(i - 1, 0) + 1) * CH)
                v.tensor_scalar(own[:, blk_i], pos[:, blk_i], pos_col[:, i:i + 1], None, ALU.subtract).then_inc(*p.count())
                v.tensor_scalar(prev[:, blk_i], pos[:, blk_p], pos_col[:, i:i + 1], None, ALU.subtract).then_inc(*p.count())
            dve.wait_ge(*p.last)

            def by_chunk(t):
                return t.rearrange("p (i n) -> p i n", i=NCH)

            def each_chunk(m):
                return m.rearrange("p (o n) -> p o n", o=1).broadcast_to([P, NCH, CH])

            v.tensor_tensor(own, own, prev, ALU.subtract).then_inc(*p.count())
            dve.wait_ge(*p.last)
            v.tensor_tensor(by_chunk(own), by_chunk(own), each_chunk(own_mask), ALU.mult).then_inc(*p.count())
            dve.wait_ge(*p.last)
            tables = [bias[:, h * 2 * T:(h + 1) * 2 * T].rearrange("p (i s n) -> p i s n", i=NCH, s=2)
                      for h in range(HEADS)]
            acc = [t[:, :, 0, :] for t in tables]
            dist, step_of = tables[0][:, :, 1, :], tables[1][:, :, 1, :]
            limit, delta = (tables[HEADS - 1][:, i, 1, :] for i in range(2))
            tb = Program(dve, sems, "table_order")
            programs.append(("table", tb))
            tb.enter()

            def table_bucket(b):
                dve.wait_ge(*tb.last)
                v.tensor_scalar(step_of, dist, float(BUCKET_FROM[b]), None, ALU.is_ge).then_inc(*tb.count())
                dve.wait_ge(*tb.last)
                for h in range(HEADS):
                    d = (b - 1) * HEADS + h
                    stt(out=acc[h], in0=step_of, scalar=delta[:, d:d + 1], in1=acc[h], op0=ALU.mult,
                        op1=ALU.add).then_inc(*tb.count())

            def table_masks(h):
                own_side, prev_side = tables[h][:, :, 1, :], tables[h][:, :, 0, :]
                first = 1 if h == HEADS - 1 else 0
                n = NCH - first
                limits = limit.rearrange("p (o n) -> p o n", o=1).broadcast_to([P, n, CH])
                dve.wait_ge(*tb.last)
                stt(out=own_side[:, first:, :], in0=limits, scalar=-1.0, in1=prev_side[:, first:, :], op0=ALU.mult,
                    op1=ALU.min).then_inc(*tb.count())
                dve.wait_ge(*tb.last)
                v.tensor_tensor(prev_side[:, first:, :], prev_side[:, first:, :], limits, ALU.min).then_inc(*tb.count())
                if first:
                    dve.wait_ge(*tb.last)
                    stt(out=own_side[:, 0, :], in0=limit, scalar=-1.0, in1=prev_side[:, 0, :], op0=ALU.mult,
                        op1=ALU.min).then_inc(*tb.count())
                dve.wait_ge(*tb.last)
                v.memset(prev_side[:, 0, :], -BIG).then_inc(*tb.count())

            stt(out=dist, in0=by_chunk(prev), scalar=-1.0, in1=by_chunk(own), op0=ALU.mult,
                op1=ALU.subtract).then_inc(*tb.count())
            v.tensor_tensor(delta[:, 0:(BUCKETS - 1) * HEADS], rel_rows[:, HEADS:], rel_rows[:, 0:(BUCKETS - 1) * HEADS],
                            ALU.subtract).then_inc(*tb.count())
            v.tensor_scalar(limit, own_mask, -2.0 * BIG, BIG, ALU.mult, ALU.add).then_inc(*tb.count())
            dve.wait_ge(*tb.last)
            for h in range(HEADS):
                v.tensor_scalar(acc[h], dist, 0.0, rel_rows[:, h:h + 1], ALU.mult, ALU.add).then_inc(*tb.count())
            for b in range(1, TABLE_FIRST):
                table_bucket(b)
            dve.wait_ge(sems["aux_ready"], p.value("aux_ready", 3))
            v.tensor_tensor(mod[0][:, 0:2 * KT], aux[:, 0:2 * KT], cols_a[:, 0:2 * KT], ALU.add).then_inc(*p.count("aux_taken"))
            dve.wait_ge(sems["sines_ready"], p.value("sines_ready", 2))
            dve.wait_ge(*p.last)
            v.memset(stat[:, 19:20], 0.0).then_inc(*p.count())
            p.leave("before")

            def split_lo(dst, src, scale, hi, name, n=None):
                stt(out=dst, in0=src, scalar=scale, in1=hi.bitcast(F32), op0=ALU.mult, op1=ALU.subtract).then_inc(*p.count(name, n=n))

            def step(s, layer):
                kind = s[0]
                if kind in ("norm", "ifrows", "gcol", "qk", "hnorm", "rot", "anorm", "ada", "adasum") or (
                        kind == "pv" and s[2] % 2 == 1 and s[1] != 1):
                    dve.wait_ge(*p.last)
                if kind == "norm":
                    j = s[1]
                    if j == 0:
                        dve.wait_ge(*p.last)
                        for dst, src, c0, w, per in (
                                (b_cur, cols_a, 16, 2 * ADA_REST, 48), (g_cur, cols_a, 96, 16, 16), (cw_cur, cols_b, 0, 16, 16),
                                (cb_cur, cols_b, 32, 4, 4), (rg_cur, cols_b, 40, 2, 2), (qk_cur[:, 0:1], cols_b, 52, 1, 1),
                                (qk_cur[:, 1:2], cols_b, 54, 1, 1), (sink_cur, sink_all, 0, 4, 4)):
                            v.tensor_copy(dst[:, 0:w], src[:, bass.ds(layer * per + c0, w)]).then_inc(*p.count())
                        v.tensor_copy(gb_cur[0:HEADS, :], gb[0:HEADS, bass.ds(layer * 2, 2)]).then_inc(*p.count())
                    dve.wait_ge(*p.last)
                    stt(out=acol[:, :], in0=mod[j][:, 8:16], scalar=1.0, in1=g_cur[:, 8 * j:8 * j + 8],
                        op0=ALU.add, op1=ALU.mult).then_inc(*p.count())
                    dve.wait_ge(*p.last)
                    dve.wait_ge(sems["rstd_ready"], p.value("rstd_ready", 7 if j else 1))
                    for k in range(KT + 1):
                        if k < KT:
                            if k:
                                dve.wait_ge(*p.last)
                            stt(out=part(prb, k % 2), in0=xk(k), scalar=acol[:, k:k + 1], in1=wrk[:, 0:T],
                                op0=ALU.mult, op1=ALU.mult).then_inc(*p.count("h_scaled"))
                        if k > 0:
                            dve.wait_ge(sems["h_hi_ready"], p.value("h_hi_ready", j * KT + k))
                            stt(out=part(h_lo, k - 1), in0=part(prb, (k - 1) % 2), scalar=mod[j][:, k - 1:k],
                                in1=part(h_hi, k - 1).bitcast(F32), op0=ALU.add, op1=ALU.subtract).then_inc(*p.count("h_ready"))
                elif kind == "tile":
                    tile_step(s)
                elif kind == "ifrows":
                    dve.wait_ge(sems["aux_ready"], p.value("aux_ready", AUX[s] + 1))
                    v.tensor_scalar(row_i, aux[0:HEADS, :], gb_cur[0:HEADS, 0:1], None, ALU.add).then_inc(*p.count())
                    v.tensor_scalar(row_f, denp[0:HEADS, :], gb_cur[0:HEADS, 1:2], None, ALU.add).then_inc(*p.count("aux_taken", n=AUX[s] + 1))
                    v.memset(row_one, 1.0).then_inc(*p.count())
                    dve.wait_ge(sems["logterm_ready"], p.value("logterm_ready", 1))
                    dve.wait_ge(*p.last)
                    stt(out=row_t, in0=row_f, scalar=0.0, in1=row_t, op0=ALU.min, op1=ALU.subtract).then_inc(*p.count())
                    dve.wait_ge(*p.last)
                    v.tensor_tensor_scan(row_a, row_one, row_t, 0.0, ALU.mult, ALU.add).then_inc(*p.count())
                    dve.wait_ge(*p.last)
                    v.tensor_tensor(row_i, row_i, row_a, ALU.subtract).then_inc(*p.count())
                    dve.wait_ge(*p.last)
                    v.tensor_tensor_scan(row_m, row_i, row_i, 0.0, ALU.max, ALU.max).then_inc(*p.count())
                    dve.wait_ge(*p.last)
                    v.tensor_tensor(row_am, row_a, row_m, ALU.add).then_inc(*p.count("rows_ready"))
                elif kind == "gcol":
                    dve.wait_ge(sems["aux_ready"], p.value("aux_ready", AUX[s] + 1))
                    v.tensor_copy(gcol[:, :], aux[:, 0:NCH * HEADS]).then_inc(*p.count("aux_taken", n=AUX[s] + 1))
                elif kind == "qk":
                    qk_step(s)
                elif kind == "pv" and s[2] % 2 == 1:
                    _, n, h = s
                    pair = h // 2
                    if n == 0:
                        dve.wait_ge(sems["den_ready"], p.value("den_ready", pair + 1))
                        dve.wait_ge(*p.last)
                        v.tensor_tensor(tmps[0], tmps[0], tmps[1], ALU.max).then_inc(*p.count())
                        dve.wait_ge(*p.last)
                        v.reciprocal(tmps[0], tmps[0]).then_inc(*p.count())
                        dve.wait_ge(*p.last)
                        v.tensor_tensor(tmps[0], outp[:, :], tmps[0], ALU.mult).then_inc(*p.count())
                        dve.wait_ge(*p.last)
                        stt(out=tmps[0], in0=feat[4 + pair][:, :], scalar=1.0, in1=tmps[0], op0=ALU.add,
                            op1=ALU.mult).then_inc(*p.count("out_scaled"))
                        dve.wait_ge(sems["branch_hi_ready"], p.value("branch_hi_ready", pair + 1))
                        split_lo(part(br_lo, pair), tmps[0], 0.5, part(br_hi, pair), "branch_ready")
                    elif n >= 2:
                        dve.wait_ge(sems["branch_hi_ready"], p.value("branch_hi_ready", 2 * n + pair + 1))
                        split_lo(part(br_lo, pair), outp[:, :], 1.0, part(br_hi, pair), "branch_ready")
                elif kind == "hnorm":
                    pair = s[1]
                    dve.wait_ge(sems["rstd_ready"], p.value("rstd_ready", 2 + pair))
                    stt(out=tmps[0], in0=outp[:, :], scalar=rg_cur[:, pair:pair + 1], in1=tmps[1],
                        op0=ALU.mult, op1=ALU.mult).then_inc(*p.count())
                    dve.wait_ge(*p.last)
                    v.tensor_tensor(tmps[0], tmps[0], feat[4 + pair][:, :], ALU.mult).then_inc(*p.count("out_scaled"))
                    dve.wait_ge(sems["branch_hi_ready"], p.value("branch_hi_ready", 2 + pair + 1))
                    split_lo(part(br_lo, pair), tmps[0], 0.5, part(br_hi, pair), "branch_ready")
                elif kind == "rot":
                    i = s[1]
                    dve.wait_ge(sems["aux_ready"], p.value("aux_ready", AUX[s] + 1))
                    v.tensor_tensor(part(wrk, i % 2), aux[:, :], sin[:, :], ALU.mult).then_inc(*p.count("aux_taken", n=AUX[s] + 1))
                    dve.wait_ge(*p.last)
                    v.tensor_tensor(feat[i][:, :], feat[i][:, :], part(wrk, i % 2), ALU.add).then_inc(*p.count("feature_ready"))
                elif kind == "anorm":
                    i = s[1]
                    dve.wait_ge(sems["rstd_ready"], p.value("rstd_ready", 4 + i))
                    r = tmps[i % 2]
                    if i < 2:
                        stt(out=feat[i][:, :], in0=feat[i][:, :], scalar=qk_cur[:, 0:1], in1=r, op0=ALU.mult,
                            op1=ALU.mult).then_inc(*p.count("feature_ready"))
                    else:
                        for n, (kv, to) in enumerate(((0, 0), (0, 1), (1, 0), (1, 1))):
                            f = slice(kv * HD, (kv + 1) * HD)
                            ins = stt(out=feat[3 + kv][to * HD:(to + 1) * HD, :], in0=feat[2][f, :],
                                      scalar=qk_cur[f, 1:2], in1=r[f, :], op0=ALU.mult, op1=ALU.mult)
                            ins.then_inc(*p.count("feature_ready" if n == 3 else None))
                elif kind == "ada":
                    dve.wait_ge(*p.last)
                    ada_unit(s[1])
                elif kind == "adasum":
                    j, c = divmod(2 * KT + 2 * s[1], 3 * KT)
                    ada_mod(AUX[s], mod[j][:, c:c + 2], b_cur[:, 2 * s[1]:2 * s[1] + 2])
                elif kind == "table":
                    with dve.If(layer < 1):
                        if s[1] < BUCKETS - TABLE_FIRST:
                            table_bucket(TABLE_FIRST + s[1])
                        else:
                            table_masks(s[1] - (BUCKETS - TABLE_FIRST))

            def qk_step(s):
                _, n, h = s
                g = 4 * n + h
                if n == 0:
                    dve.wait_ge(sems["aux_ready"], p.value("aux_ready", AUX[s] + 1))
                    dve.wait_ge(*p.last)
                    stt(out=by_chunk(tmps[0]), in0=by_chunk(aux[:, :]), scalar=-1.0, in1=each_chunk(mask_incl[:, :]),
                        op0=ALU.mult, op1=ALU.add).then_inc(*p.count("masked_ready"))
                if n < 2:
                    dve.wait_ge(sems["qk_ready"], p.value("qk_ready", g + 1))
                    dve.wait_ge(sems["decay_ready"], p.value("decay_ready", g + 1))
                    dve.wait_ge(sems["pv_ready"], p.value("pv_ready", g))
                    if n == 0:
                        for i, (c0, w) in enumerate(((0, T), (T, T), (2 * T, 256))):
                            ins = stt(out=prb[:, c0:c0 + w], in0=score[i][:, 0:w], scalar=0.25 * HD ** -0.5,
                                      in1=wrk[:, c0:c0 + w], op0=ALU.mult, op1=ALU.mult)
                            ins.then_inc(*p.count("scores_taken" if i == 2 else None, n=g + 1 if i == 2 else None))
                    else:
                        for j in range(NCH):
                            ins = stt(out=prb[:, OFF[j]:OFF[j] + LEN[j]],
                                      in0=score[SC_BANK[j]][:, SC_COL[j]:SC_COL[j] + LEN[j]], scalar=HD ** -0.5,
                                      in1=wrk[:, 0:LEN[j]], op0=ALU.mult, op1=ALU.mult)
                            last = j == NCH - 1
                            ins.then_inc(*p.count("scores_taken" if last else None, n=g + 1 if last else None))
                elif n == 2:
                    dve.wait_ge(sems["logterm_ready"], p.value("logterm_ready", 1 + h + 1))
                    for i, (c0, w) in enumerate(((0, T), (T, T), (2 * T, 256))):
                        ins = stt(out=wrk[:, c0:c0 + w], in0=score[i][:, 0:w], scalar=0.0, in1=wrk[:, c0:c0 + w],
                                  op0=ALU.max, op1=ALU.add)
                        ins.then_inc(*p.count("softplus_ready" if i == 2 else None))
                else:
                    dve.wait_ge(sems["qk_ready"], p.value("qk_ready", g + 1))
                    if h == 0:
                        dve.wait_ge(*tb.last)
                    for i in range(2):
                        ins = stt(out=part(wrk, i), in0=score[i][:, :], scalar=HD ** -0.5,
                                  in1=bias[:, h * 2 * T + i * T:h * 2 * T + (i + 1) * T], op0=ALU.mult, op1=ALU.add)
                        ins.then_inc(*p.count("scores_taken" if i else None, n=g + 1 if i else None))
                    dve.wait_ge(*p.last)
                    v.tensor_reduce(stat[:, 0:NCH], wrk[:, 0:2 * T].rearrange("p (i n) -> p i n", i=NCH), AX.X,
                                    ALU.max).then_inc(*p.count())
                    dve.wait_ge(*p.last)
                    v.tensor_scalar(stat[:, NCH:2 * NCH], stat[:, 0:NCH], sink_cur[:, h:h + 1], -1.0, ALU.max,
                                    ALU.mult).then_inc(*p.count("negmax_ready"))
                    dve.wait_ge(sems["exp_ready"], p.value("exp_ready", h + 1))
                    den = stat[:, 4 * NCH:5 * NCH]
                    v.tensor_tensor(den, stat[:, 2 * NCH:3 * NCH], stat[:, 3 * NCH:4 * NCH], ALU.add).then_inc(*p.count())
                    dve.wait_ge(*p.last)
                    v.reciprocal(den, den).then_inc(*p.count())
                    dve.wait_ge(*p.last)
                    for i in range(NCH):
                        pi = prb[:, i * 256:(i + 1) * 256]
                        v.tensor_scalar(pi, pi, den[:, i:i + 1], None, ALU.mult).then_inc(*p.count("probs_ready" if i == NCH - 1 else None))

            def tile_step(s):
                _, b, half = s
                blk = BLOCKS[b]
                name = blk[0]
                tile = TILE_NO[(b, half)]
                bank, taken, bn = gemm[tile % 2], f"bank_taken{tile % 2}", tile // 2 + 1
                if name in ("m_q", "m_k"):
                    i = half + (2 if name == "m_k" else 0)
                    u = tmps[i % 2]
                    dve.wait_ge(sems[f"bank_ready{tile % 2}"], p.value(f"bank_ready{tile % 2}", bn))
                    dve.wait_ge(*p.last)
                    v.tensor_scalar(u, bank[:, :], cw_cur[:, 12 + i:13 + i], cb_cur[:, i:i + 1], ALU.mult, ALU.add).then_inc(*p.count())
                    for back in range(1, 4):
                        dve.wait_ge(*p.last)
                        ins = stt(out=u[:, back:T], in0=bank[:, 0:T - back],
                                  scalar=cw_cur[:, (3 - back) * 4 + i:(3 - back) * 4 + i + 1], in1=u[:, back:T],
                                  op0=ALU.mult, op1=ALU.add)
                        if back < 3:
                            ins.then_inc(*p.count())
                        else:
                            ins.then_inc(*p.count("conv_ready"))
                    v.memset(stat[:, 19:20], 0.0).then_inc(*p.count(taken, n=bn))
                    dve.wait_ge(sems["silu_ready"], p.value("silu_ready", i + 1))
                    stt(out=feat[i][:, :], in0=part(prb, i % 2), scalar=1.0, in1=u, op0=ALU.add, op1=ALU.mult).then_inc(*p.count("feature_ready"))
                elif name == "m_if":
                    dve.wait_ge(sems[f"bank_ready{tile % 2}"], p.value(f"bank_ready{tile % 2}", bn))
                    v.tensor_copy(if_tok[:, half * 16:(half + 1) * 16], bank[:, 0:16]).then_inc(*p.count(taken, n=bn))
                elif name == "gate":
                    dve.wait_ge(sems[f"bank_ready{tile % 2}"], p.value(f"bank_ready{tile % 2}", bn))
                    v.tensor_copy(gate_tile(2 * blk[2] + half), bank[:, :]).then_inc(*p.count(taken, n=bn))
                elif name in ("r_q", "r_k"):
                    i = half + (2 if name == "r_k" else 0)
                    dve.wait_ge(sems["rot_raw"], p.value("rot_raw", i + 1))
                    v.tensor_tensor(feat[i][:, :], bank[:, :], cos[:, :], ALU.mult).then_inc(*p.count(taken, n=bn))
                elif name == "r_g":
                    dve.wait_ge(sems["silu_ready"], p.value("silu_ready", 4 + half + 1))
                    stt(out=feat[4 + half][:, :], in0=tmps[half], scalar=1.0, in1=bank[:, :], op0=ALU.add,
                        op1=ALU.mult).then_inc(*p.count(taken, n=bn))
                elif name in ("s_q", "s_k"):
                    dve.wait_ge(sems[f"bank_ready{tile % 2}"], p.value(f"bank_ready{tile % 2}", bn))
                    f = feat[half + (2 if name == "s_k" else 0)][:, :]
                    v.tensor_scalar(f, bank[:, :], HD ** -0.5 if name == "s_q" else 1.0, None, ALU.mult).then_inc(*p.count(taken, n=bn))
                elif name == "a_q" or (name == "a_kv" and half == 0):
                    dve.wait_ge(sems[f"bank_ready{tile % 2}"], p.value(f"bank_ready{tile % 2}", bn))
                    v.tensor_copy(feat[half + (2 if name == "a_kv" else 0)][:, :], bank[:, :]).then_inc(*p.count(taken, n=bn))
                elif name == "up":
                    n, m = blk[1], half
                    if m == 0:
                        dve.wait_ge(sems["gate_ready"], p.value("gate_ready", n + 1))
                    dve.wait_ge(sems[f"bank_ready{tile % 2}"], p.value(f"bank_ready{tile % 2}", bn))
                    dst = part(merged, m) if n == 0 else gate_tile(m)
                    stt(out=dst, in0=gate_tile(m), scalar=1.0, in1=bank[:, :], op0=ALU.add, op1=ALU.mult).then_inc(*p.count(taken, n=bn))
                    if n > 0:
                        dve.wait_ge(*p.last)
                        v.tensor_tensor(part(merged, m), part(merged, m), gate_tile(m), ALU.add).then_inc(*p.count("merged_tile" if n == 3 else None))
                    if n == 3:
                        for k in ([m - 1] if m else []) + ([7] if m == 7 else []):
                            dve.wait_ge(sems["merged_hi_ready"], p.value("merged_hi_ready", k + 1))
                            split_lo(part(h_lo, k), part(merged, k), 0.5, part(h_hi, k), "merged_ready")
                elif name == "out":
                    m = 2 * blk[1] + half
                    dve.wait_ge(sems[f"bank_ready{tile % 2}"], p.value(f"bank_ready{tile % 2}", bn))
                    stt(out=xk(m), in0=bank[:, :], scalar=mod[0][:, 16 + m:17 + m], in1=xk(m), op0=ALU.mult,
                        op1=ALU.add).then_inc(*p.count(taken, n=bn))

            with dve.Fori(0, LAYERS) as layer:
                p.enter(layer)
                for s in STEPS:
                    step(s, layer)
                p.leave("layer")
                tb.leave("before")
                with dve.Fori(0, QUARTERS) as q:
                    p.enter(layer, q)
                    for b, blk in enumerate(FF):
                        for half in range(2):
                            tile = 2 * b + half
                            bank, taken, bn = gemm[tile % 2], f"bank_taken{tile % 2}", tile // 2 + 1
                            if blk[0] == "ff1":
                                sq = part(prb, tile % 2)
                                dve.wait_ge(sems["relu_ready"], p.value("relu_ready", tile + 1))
                                stt(out=sq, in0=bank[:, :], scalar=0.0, in1=tmps[tile % 2], op0=ALU.max,
                                    op1=ALU.mult).then_inc(*p.count(taken, n=bn))
                                dve.wait_ge(sems["hidden_hi_ready"], p.value("hidden_hi_ready", tile + 1))
                                v.tensor_tensor(part(hid_lo, tile), sq, part(hid_hi, tile).bitcast(F32),
                                                ALU.subtract).then_inc(*p.count("hidden_ready"))
                            else:
                                m = tile - 8
                                dve.wait_ge(sems[f"bank_ready{tile % 2}"], p.value(f"bank_ready{tile % 2}", bn))
                                stt(out=xk(m), in0=bank[:, :], scalar=mod[1][:, 16 + m:17 + m], in1=xk(m),
                                    op0=ALU.mult, op1=ALU.add).then_inc(*p.count(taken, n=bn))
                            if half == 0 and b in FF_ADASUM:
                                u = FF_ADASUM[b]
                                ada_mod(u, mod[0][:, bass.ds(q * 4 + 2 * u, 2)],
                                        cols_a[:, bass.ds(q * 4 + (48 + 2 * u), 2)])
                        if b in FF_ADA:
                            dve.wait_ge(*p.last)
                            ada_unit(FF_ADA[b])
                    v.memset(stat[:, 19:20], 0.0).then_inc(*p.count())
                    p.leave("quarter")

            for n in range(2 * NCH):
                dve.wait_ge(sems["xt_ready"], n + 1)
                v.tensor_copy(x_out[n // 2][:, (n % 2) * T:(n % 2 + 1) * T], gemm[n % 2][:, :]).then_inc(
                    sems["xt_taken"], 1)

    return programs


def check_counts(programs):
    total = {}
    for _, p in programs:
        for region, i in (("before", 0), ("layer", 1), ("quarter", 2)):
            for name, n in p.seen.get(region, {}).items():
                total.setdefault(name, [0, 0, 0])[i] += n
    wrong = {name: tuple(t) for name, t in total.items() if tuple(t) != COUNTS[name] and not name.startswith("hi_ready")}
    assert not wrong, wrong


_INS = ["x", "c", "positions", "w_ada", "b_ada", "norm_g", "w_in", "mlstm_conv_w", "mlstm_conv_b", "mlstm_gate_b",
        "ret_norm_g", "swa_q_norm_g", "swa_k_norm_g", "swa_sinks", "rel_bias", "w_up", "w_out", "w_ff1", "w_ff2"]


def kernel(**inputs):
    import concourse.bacc as bacc
    from concourse.bass_utils import run_bass_kernel_spmd

    nc = bacc.Bacc("TRN2", target_bir_lowering=False, num_devices=1)
    arrays = {f"in_{name}": np.ascontiguousarray(inputs[name]) for name in _INS}
    half = HD // 2
    inv = np.float32(10000.0) ** (-np.arange(half, dtype=np.float32) / np.float32(half))
    arrays["rope_freq"] = np.tile(inv, P // half).reshape(P, 1).astype(np.float32)
    args = [nc.dram_tensor(name, a.shape, mybir.dt.from_np(a.dtype), kind="ExternalInput").ap()
            for name, a in arrays.items()]
    args.append(nc.dram_tensor("out", (1, T, D), F32, kind="ExternalOutput").ap())
    check_counts(trunk(nc, *args))
    return run_bass_kernel_spmd(nc, [arrays], core_ids=[0]).results[0]["out"]
```

```python
from contextlib import ExitStack
import math

import numpy as np

import concourse.bass as bass
from concourse import mybir
from concourse.alu_op_type import AluOpType as ALU

ACT = mybir.ActivationFunctionType
AX = mybir.AxisListType
F32 = mybir.dt.float32
F32R = mybir.dt.float32r
I32 = mybir.dt.int32

P = 128
LAYERS = 2
T = 512
D = 1024
KT = D // P
HD = 64
HEADS = 4
CH = 128
NCH = T // CH
WB = HEADS * HD
NBR = 4
DFF = 4 * D
QUARTERS = DFF // D
BUCKETS = 32
MAX_DIST = 128
EPS = 1e-6
BIG = 1.0e30
BC = 256
LAG = 2
LOG_GAMMA = [math.log(1.0 - 2.0 ** -(5.0 + h)) for h in range(HEADS)]
COLS = {"m_q": 0, "m_k": 256, "m_v": 512, "m_if": 768, "m_o": 776, "r_q": 1032, "r_k": 1288, "r_v": 1544,
        "r_g": 1800, "s_q": 2056, "s_k": 2312, "s_v": 2568, "a_q": 2824, "a_kv": 3080, "gate": 3336}

SC_BANK = [0, 1, 2, 1]
SC_COL = [0, 0, 0, 384]
OFF = [0, 512, 1024, 896]
LEN = [T - CH * j for j in range(NCH)]
PT_BLOCKS = [(0, 1), (1, 0), (1, 1), (2, 0), (2, 1), (3, 0), (3, 1)]


EXACT = BUCKETS // 2
BUCKET_FROM = [b if b < EXACT else math.ceil(EXACT * (MAX_DIST / EXACT) ** ((b - EXACT) / (BUCKETS - EXACT)) - 1e-9)
               for b in range(BUCKETS)]
ADA_FIRST = 2 * D // BC
ADA_REST = 4 * D // BC
ADA_BLOCK = [0, 2, 4, 6, 8, 11, 13, 15, 17, 20, 22, 24, 26, 28, 30, 31]
TABLE_FIRST = 8


def plan():
    blocks, steps = [], []

    def block(name, *arg):
        b = len(blocks)
        blocks.append((name, *arg))
        tiles = 8 if name == "up" else 2
        for h in range(tiles):
            steps.append(("tile", b, h))
            squares = [s for s in after.get((b, h), []) if s[0] == "square"]
            steps.extend(squares)
            if h == tiles - 1:
                steps.append(("round", b + 2))
            steps.extend(s for s in after.pop((b, h), []) if s not in squares)
        for s in after.pop((b, "end"), []):
            steps.append(s)

    after = {}

    def put(b, h, *s):
        after.setdefault((b, h), []).extend(s)

    names = ([("m_q",), ("m_k",), ("m_if",), ("m_v",), ("m_o",)] + [("gate", 0, g) for g in range(4)]
             + [("r_q",), ("r_k",), ("up", 0), ("r_v",), ("r_g",)] + [("gate", 1, g) for g in range(4)]
             + [("s_q",), ("s_k",), ("up", 1), ("s_v",)] + [("gate", 2, g) for g in range(3)]
             + [("a_q",), ("a_kv",), ("gate", 2, 3), ("up", 2)] + [("gate", 3, g) for g in range(4)] + [("up", 3)]
             + [("out", g) for g in range(4)])
    no = {n: i for i, n in enumerate(names)}
    for u, b in enumerate(ADA_BLOCK):
        assert names[b + 1][0] != "up"
        if b + 1 in ADA_BLOCK or b == no[("gate", 2, 2)]:
            put(b + 1, 1, ("adasum", u))
        else:
            put(b + 2, 0, ("adasum", u))
    put(no[("m_v",)], 0, ("ifrows",))
    put(no[("m_o",)], 0, ("gcol",))
    put(no[("m_o",)], "end", ("qk", 0, 0))
    put(no[("gate", 0, 0)], "end", ("qk", 0, 1), ("pv", 0, 0))
    put(no[("gate", 0, 1)], "end", ("qk", 0, 2), ("pv", 0, 1))
    put(no[("gate", 0, 2)], "end", ("qk", 0, 3), ("pv", 0, 2))
    put(no[("gate", 0, 3)], "end", ("gate_tanh", 0, 0, 8))
    put(no[("r_q",)], 0, ("pv", 0, 3))
    put(no[("r_q",)], 1, ("rot", 0))
    put(no[("r_k",)], 0, ("rot", 1))
    put(no[("r_k",)], 1, ("rot", 2))
    put(no[("up", 0)], 1, ("rot", 3))
    put(no[("r_g",)], "end", ("qk", 1, 0))
    put(no[("gate", 1, 0)], "end", ("qk", 1, 1), ("pv", 1, 0))
    put(no[("gate", 1, 1)], "end", ("qk", 1, 2), ("pv", 1, 1))
    put(no[("gate", 1, 2)], 0, ("hnorm", 0))
    put(no[("gate", 1, 2)], "end", ("qk", 1, 3), ("pv", 1, 2))
    put(no[("gate", 1, 3)], "end", ("gate_tanh", 1, 0, 8), ("pv", 1, 3))
    put(no[("s_q",)], 0, ("hnorm", 1))
    put(no[("s_k",)], "end", ("qk", 2, 0))
    put(no[("up", 1)], 7, ("softplus", 0))
    put(no[("s_v",)], 0, ("suffix", 0))
    put(no[("s_v",)], 1, ("qk", 2, 1))
    put(no[("gate", 2, 0)], 0, ("pv", 2, 0), ("softplus", 1))
    put(no[("gate", 2, 0)], 1, ("suffix", 1))
    put(no[("gate", 2, 1)], 0, ("qk", 2, 2), ("pv", 2, 1))
    put(no[("gate", 2, 1)], 1, ("softplus", 2))
    put(no[("gate", 2, 2)], 0, ("suffix", 2))
    put(no[("gate", 2, 2)], 1, ("qk", 2, 3), ("pv", 2, 2))
    put(no[("gate", 2, 2)], "end", ("gate_tanh", 2, 0, 6))
    put(no[("a_q",)], 0, ("softplus", 3))
    put(no[("a_q",)], 1, ("suffix", 3), ("anorm", 0))
    put(no[("a_kv",)], 0, ("headscale", 0))
    put(no[("a_kv",)], 1, ("headscale", 1))
    put(no[("gate", 2, 3)], 0, ("headscale", 2), ("vtrans",))
    put(no[("gate", 2, 3)], "end", ("gate_tanh", 2, 6, 8))
    put(no[("a_kv",)], 0, ("pv", 2, 3), ("anorm", 1))
    put(no[("a_kv",)], 1, ("anorm", 2))
    put(no[("gate", 2, 3)], 1, ("qk", 3, 0))
    put(no[("up", 2)], 3, ("probs", 0))
    put(no[("up", 2)], 6, ("ptrans", 0))
    put(no[("up", 2)], "end", ("qk", 3, 1))
    put(no[("gate", 3, 0)], 0, ("pv", 3, 0), ("probs", 1))
    put(no[("gate", 3, 0)], 1, ("ptrans", 1), ("qk", 3, 2))
    put(no[("gate", 3, 1)], 0, ("pv", 3, 1), ("probs", 2))
    put(no[("gate", 3, 1)], 1, ("ptrans", 2), ("qk", 3, 3))
    put(no[("gate", 3, 2)], 0, ("pv", 3, 2), ("probs", 3))
    put(no[("gate", 3, 2)], 1, ("ptrans", 3))
    put(no[("gate", 3, 2)], "end", ("gate_tanh", 3, 0, 6))
    put(no[("gate", 3, 3)], 0, ("pv", 3, 3))
    put(no[("gate", 3, 3)], "end", ("gate_tanh", 3, 6, 8))
    for k in range(KT - 1):
        put(no[("out", (k + 1) // 2)], (k + 1) % 2, ("square", k))
        if k < KT - 2:
            put(no[("out", (k + 2) // 2)], (k + 2) % 2, ("squaresum", k))
    for u, b in enumerate(ADA_BLOCK):
        put(b, "end", ("ada", u))
    spots = [(no[("gate", n, g)], half) for n in range(3) for g in range(4) for half in range(2)]
    spots += [(no[("m_o",)], 1), (no[("r_v",)], 0), (no[("r_v",)], 1), (no[("s_q",)], 1)]
    for n, (b, half) in enumerate(sorted(spots)):
        put(b, half, ("table", n))
    steps.append(("norm", 0))
    steps.append(("round", 1))
    for n in names:
        block(*n)
    assert not after
    steps.append(("norm", 1))
    return blocks, steps


BLOCKS, STEPS = plan()
PRE_BLOCKS = len(BLOCKS)
assert PRE_BLOCKS % 2 == 0
TILE_NO = {}
for _s in STEPS:
    if _s[0] == "tile":
        TILE_NO[_s[1:]] = len(TILE_NO)
PRE_TILES = len(TILE_NO)
BLOCK_NO = {b: i for i, b in enumerate(BLOCKS)}
FF_ADA = {1: 0, 4: 1}
FF_ADASUM = {3: 0, 6: 1}


def makes_aux(s):
    return (s[0] in ("norm", "gcol", "vtrans", "rot", "hnorm", "anorm", "adasum")
            or s[:2] == ("qk", 0) or s in (("pv", 0, 1), ("pv", 0, 3)))


AUX_ORDER = [s for s in STEPS if makes_aux(s)]
assert STEPS.index(("squaresum", 0)) > STEPS.index(AUX_ORDER[-2])
AUX = {s: n for n, s in enumerate(AUX_ORDER)}
PRO_AUX = 2 + 1

TABLE_STEPS = 3 + HEADS + (1 + HEADS) * (BUCKETS - 1) + 3 * HEADS + 1

_BLK = PRE_BLOCKS // 2
_TL = PRE_TILES // 2
COUNTS = {
    "raw_landed0": (0, 16 * _BLK, 64), "raw_landed1": (0, 16 * _BLK, 64),
    "hi_ready0": (0, _BLK, 4), "hi_ready1": (0, _BLK, 4), "lo_ready0": (0, _BLK, 4), "lo_ready1": (0, _BLK, 4),
    "ada_landed": (16 * 3, 16 * ADA_REST, 16 * 2), "ada_landed_b": (16 * 3, 0, 0), "ada_landed_c": (16 * 2, 0, 0),
    "ada_used": (ADA_FIRST, 0, 0), "ada_row_ready": (ADA_FIRST // 2, 0, 0), "c_act_ready": (1, 0, 0), "ada_partial": (0, ADA_REST, 2),
    "bank_ready0": (4, _TL, 8), "bank_ready1": (4, _TL, 8), "bank_taken0": (4, _TL, 8), "bank_taken1": (4, _TL, 8),
    "aux_ready": (PRO_AUX, len(AUX), 2), "aux_taken": (PRO_AUX, len(AUX), 2),
    "square_ready": (0, 2 * KT + 5, 0), "square_used": (0, 2 * (KT - 1), 0), "rstd_ready": (0, 2 + 5, 0),
    "h_scaled": (0, 2 * KT, 0), "h_hi_ready": (0, 2 * KT, 0), "h_ready": (0, 2 * KT, 0),
    "feature_ready": (0, 4 + 4 + 3, 0), "conv_ready": (0, 4, 0), "silu_ready": (0, 4 + 2, 0), "rot_raw": (0, 4, 0),
    "logterm_ready": (0, 1 + 4, 0), "rows_ready": (0, 1, 0), "masked_ready": (0, 4, 0), "decay_ready": (0, 8, 0),
    "qk_ready": (0, 16, 0), "scores_taken": (0, 16, 0), "softplus_ready": (0, 4, 0), "suffix_ready": (0, 4, 0),
    "negmax_ready": (0, 4, 0), "exp_ready": (0, 4, 0), "probs_ready": (0, 4, 0),
    "ptrans_ready": (0, 4, 0), "ptrans_copied": (0, 4, 0),
    "pv_ready": (0, 16, 0), "den_ready": (0, 2, 0), "out_scaled": (0, 4, 0),
    "branch_hi_ready": (0, 8, 0), "branch_ready": (0, 8, 0), "gate_ready": (0, 6, 0),
    "merged_tile": (0, 8, 0), "merged_hi_ready": (0, 8, 0), "merged_ready": (0, 8, 0),
    "relu_ready": (0, 0, 8), "hidden_hi_ready": (0, 0, 8), "hidden_ready": (0, 0, 8),
    "columns_loaded": (16 * 10, 0, 0), "vectors_loaded": (16 * 6, 0, 0), "table_order": (TABLE_STEPS, 0, 0), "x_landed": (64, 0, 0), "consts_ready": (1, 0, 0), "c_tanh": (1, 0, 0),
    "angles_ready": (1, 0, 0), "sines_ready": (2, 0, 0), "pool_order": (25, 0, 0),
    "stored": (0, 0, 0), "xt_ready": (0, 0, 0), "xt_taken": (0, 0, 0),
}
COUNTS["act_order"] = (0, 68, 0)
COUNTS["dve_order"] = (23, 224, 15)


VECTORS = COUNTS["vectors_loaded"][0]
COLUMNS = COUNTS["columns_loaded"][0]
TILES_BEFORE = [TILE_NO[(b, 0)] for b in range(PRE_BLOCKS)] + [PRE_TILES]


def at(name, n, layer=None, quarter=None):
    before, pre, per_quarter = COUNTS[name]
    if layer is None:
        return n
    if quarter is None:
        return layer * (pre + QUARTERS * per_quarter) + (before + n)
    return layer * (pre + QUARTERS * per_quarter) + quarter * per_quarter + (before + pre + n)


def after_layers(name, n=0):
    before, pre, per_quarter = COUNTS[name]
    return before + LAYERS * (pre + QUARTERS * per_quarter) + n


class Program:

    def __init__(self, engine, sems, order=None):
        self.engine, self.sems, self.order = engine, sems, order
        self.layer = self.quarter = self.last = None
        self.n = {}
        self.seen = {}
        self.tail = False

    def enter(self, layer=None, quarter=None):
        self.layer, self.quarter, self.n = layer, quarter, {}
        if self.order:
            self.last = (self.sems[self.order], at(self.order, 0, layer, quarter))

    def leave(self, region):
        self.seen[region] = dict(self.n)

    def value(self, name, n):
        return after_layers(name, n) if self.tail else at(name, n, self.layer, self.quarter)

    def count(self, name=None, n=None, by=1):
        name = name or self.order
        self.n[name] = self.n.get(name, 0) + by
        self.last = (self.sems[name], self.value(name, self.n[name] if n is None else n))
        return self.sems[name], by


def trunk(nc, x, c, positions, w_ada, b_ada, norm_g, w_in, conv_w, conv_b, gate_b, ret_g, q_g, k_g, sinks,
          rel_bias, w_up, w_out, w_ff1, w_ff2, rope_freq, out):
    with ExitStack() as ctx:
        def sb(name, cols, dtype=F32):
            return ctx.enter_context(nc.sbuf_tensor(name, [P, cols], dtype))

        sems = {name: ctx.enter_context(nc.semaphore(name)) for name in COUNTS}

        gemm = [ctx.enter_context(nc.psum_tensor(f"gemm{i}", [P, T], F32)) for i in range(2)]
        score = [ctx.enter_context(nc.psum_tensor(f"score{i}", [P, T], F32)) for i in range(3)]
        outp = ctx.enter_context(nc.psum_tensor("outp", [P, T], F32))
        denp = ctx.enter_context(nc.psum_tensor("denp", [P, T], F32))
        aux = ctx.enter_context(nc.psum_tensor("aux", [P, T], F32))

        with nc.sbuf_tensor("gates", [P, 8 * T], F32) as gates, nc.sbuf_tensor("merged", [P, 8 * T], F32) as merged:
            pass
        hid_hi = sb("hid_hi", 8 * T, F32R)
        hid_lo = sb("hid_lo", 8 * T, F32R)
        xt = sb("xt", KT * T)
        h_hi, h_lo = sb("h_hi", KT * T, F32R), sb("h_lo", KT * T, F32R)
        w_raw = [sb(f"w_raw{i}", KT * BC) for i in range(2)]
        w_hi = [sb(f"w_hi{i}", KT * BC, F32R) for i in range(2)]
        w_lo = [sb(f"w_lo{i}", KT * BC, F32R) for i in range(2)]
        ada_raw = sb("ada_raw", KT * BC)
        ada_acc = sb("ada_acc", 2 * BC)
        br_hi, br_lo = sb("br_hi", 2 * T, F32R), sb("br_lo", 2 * T, F32R)
        feat = [sb(f"feat{i}", T) for i in range(6)]
        vt = sb("vt", NCH * WB)
        bias = sb("bias", HEADS * NCH * 256)
        cos, sin, age = sb("cos", T), sb("sin", T), sb("age", T)
        wrk, prb = sb("wrk", 1280), sb("prb", 1280)
        tmp = sb("tmp", 2 * T)
        ident, neg_tri, neg_ones, ones, block_ones, rot = (
            sb(n, P) for n in ("ident", "neg_tri", "neg_ones", "ones", "block_ones", "rot"))
        mask_incl, mask_strict = sb("mask_incl", P), sb("mask_strict", P)
        sel = sb("sel", HEADS * P)
        sel_pair = sb("sel_pair", 2 * P)
        cols_a, cols_b = sb("cols_a", P), sb("cols_b", 56)
        c_act = sb("c_act", 8)
        gb, gb_cur = sb("gb", 4), sb("gb_cur", 2)
        sink_all, sink_cur = sb("sink_all", LAYERS * HEADS), sb("sink_cur", HEADS)
        mod = [sb("mod1", 24), sb("mod2", 24)]
        b_cur, g_cur, acol = sb("b_cur", 2 * ADA_REST), sb("g_cur", 16), sb("acol", 8)
        cw_cur, cb_cur, rg_cur, qk_cur = sb("cw_cur", 16), sb("cb_cur", 4), sb("rg_cur", 2), sb("qk_cur", 2)
        gcol = sb("gcol", NCH * HEADS)
        stat = sb("stat", 5 * NCH)

        ada_ring = (ada_raw[:, :], gates[:, 0:KT * BC], gates[:, KT * BC:2 * KT * BC])
        ada_ring_landed = ("ada_landed", "ada_landed_b", "ada_landed_c")
        ada_banks = (score[0], score[1], score[2], outp)
        ada_rows = (wrk[0:1, 0:T], wrk[0:1, T:2 * T], tmp[0:1, 0:T], tmp[0:1, T:2 * T])
        tmps = [tmp[:, 0:T], tmp[:, T:2 * T]]
        x_rows = merged
        x_out = [merged[:, m * D:(m + 1) * D] for m in range(NCH)]
        own_mask = prb[:, 512:512 + P]
        vec_a, vec_b = tmp[:, 0:P], tmp[:, P:2 * P]
        row_i, row_f, row_t, row_a, row_m, row_am = (merged[0:HEADS, n * T:(n + 1) * T] for n in range(6))
        row_one = merged[0:HEADS, 6 * T:7 * T]
        row_if = merged[0:2 * HEADS, 7 * T:8 * T]

        def xk(k):
            return xt[:, k * T:(k + 1) * T]

        def part(t, k):
            return t[:, k * T:(k + 1) * T]

        def gate_tile(k):
            return gates[:, k * T:(k + 1) * T]

        def w_src(block, layer):
            name = block[0]
            ly = bass.ds(layer, 1)
            if name == "up":
                return w_up[ly, block[1]].rearrange("o (k p) n -> p (o k) n", p=P)
            if name == "out":
                return w_out[ly, :, block[1] * BC:(block[1] + 1) * BC].rearrange("o (k p) n -> p (o k) n", p=P)
            c0 = COLS[name] + (block[1] * D + block[2] * BC if name == "gate" else 0)
            n = P if name == "m_if" else BC
            return w_in[ly, :, c0:c0 + n].rearrange("o (k p) n -> p (o k) n", p=P)

        def w_view(t, block):
            if block[0] == "up":
                return t[:, :].rearrange("p (k n) -> p k n", k=2)
            if block[0] == "m_if":
                return t[:, 0:KT * P].rearrange("p (k n) -> p k n", k=KT)
            return t[:, :].rearrange("p (k n) -> p k n", k=KT)

        def w_flat(t, block):
            return t[:, 0:KT * P] if block[0] == "m_if" else t[:, :]

        def k_cols(h):
            return feat[2 + h // 2]

        def rows(h):
            r = HD * (h % 2)
            return slice(r, r + HD)

        FF = [("ff1", j) for j in range(4)] + [("ff2", j) for j in range(4)]
        programs = []
        block = ctx.enter_context(nc.Block())

        @block.sync
        def _(sp):
            p = Program(sp, sems)
            programs.append(("sp", p))
            p.enter()

            def small(dst, src, scattered=False, name="vectors_loaded"):
                sp.dma_start(dst, src, allow_slow_non_contiguous=scattered).then_inc(*p.count(name, by=16))

            def column(dst, src):
                small(dst, src, name="columns_loaded")

            def rows_of(a):
                return a.rearrange("(r p) -> r p", p=P)

            column(vec_a[0:96, :], b_ada.rearrange("l j (c p) -> (l j c) p", p=P))
            column(vec_a[96:128, :], norm_g.rearrange("l j (c p) -> (l j c) p", p=P))
            column(vec_b[0:32, :], conv_w.rearrange("l k (m p) -> (l k m) p", p=P))
            column(vec_b[32:40, :], conv_b.rearrange("l (m p) -> (l m) p", p=P))
            column(vec_b[40:44, :], ret_g.rearrange("l (m p) -> (l m) p", p=P))
            column(vec_b[44:52, :], c.rearrange("b (m p) -> (b m) p", p=P))
            for half in range(2):
                column(vec_b[52:54, half * HD:(half + 1) * HD], q_g)
                column(vec_b[54:56, half * HD:(half + 1) * HD], k_g)
            for m in range(NCH):
                sp.dma_start(x_rows[:, m * D:(m + 1) * D], x[0, m * P:(m + 1) * P, :]).then_inc(sems["x_landed"], 16)
            small(gb[0:HEADS, :], gate_b.rearrange("l j h -> h (l j)"), True)
            small(sink_all[:, :], sinks.rearrange("l h -> (l h)").partition_broadcast(P))
            small(wrk[:, 0:T].bitcast(I32), positions.rearrange("b t -> (b t)").partition_broadcast(P))
            small(wrk[:, 1024:1028].bitcast(I32), positions.rearrange("b (i p) -> p (b i)", p=P), True)
            small(prb[:, 1024:1152], rel_bias.rearrange("b h -> (b h)").partition_broadcast(P))
            small(prb[:, 1184:1185], rope_freq)

            def load_ada(src, u):
                sp.wait_ge(sems["ada_partial"], p.value("ada_partial", u))
                if p.quarter is None and u == 0:
                    sp.wait_ge(sems["aux_ready"], 3)
                sp.dma_start(ada_raw[:, :].rearrange("p (k n) -> p k n", k=KT), src).then_inc(*p.count("ada_landed", by=16))

            def load_block(b, src, blk):
                s = b % 2
                sp.wait_ge(sems[f"lo_ready{s}"], p.value(f"lo_ready{s}", b // 2))
                sp.dma_start(w_view(w_raw[s], blk), src).then_inc(*p.count(f"raw_landed{s}", by=16))

            for u in range(ADA_FIRST):
                if u >= 3:
                    sp.wait_ge(sems["ada_used"], u - 2)
                sp.dma_start(ada_ring[u % 3].rearrange("p (k n) -> p k n", k=KT),
                             w_ada[0, 0, :, u * BC:(u + 1) * BC].rearrange("(k p) n -> p k n", p=P)).then_inc(
                    *p.count(ada_ring_landed[u % 3], by=16))
            p.leave("before")
            with sp.Fori(0, LAYERS) as layer:
                p.enter(layer)
                for b, blk in enumerate(BLOCKS):
                    if b - 2 in ADA_BLOCK:
                        u = ADA_BLOCK.index(b - 2)
                        j, c0 = divmod(2 * D + u * BC, 3 * D)
                        load_ada(w_ada[bass.ds(layer, 1), j, :, c0:c0 + BC].rearrange("o (k p) n -> p (o k) n", p=P), u)
                    load_block(b, w_src(blk, layer), blk)
                p.leave("layer")
                with sp.Fori(0, QUARTERS) as q:
                    p.enter(layer, q)
                    for b, blk in enumerate(FF):
                        if b - 2 in FF_ADA:
                            load_ada(w_ada[1, 0, :, bass.ds(q * (2 * BC) + FF_ADA[b - 2] * BC, BC)].rearrange(
                                "(k p) n -> p k n", p=P), FF_ADA[b - 2])
                        ly = bass.ds(layer, 1)
                        if blk[0] == "ff1":
                            src = w_ff1[ly, :, bass.ds(q * D + blk[1] * BC, BC)]
                        else:
                            src = w_ff2[ly, bass.ds(q * D, D), blk[1] * BC:(blk[1] + 1) * BC]
                        load_block(b, src.rearrange("o (k p) n -> p (o k) n", p=P), blk)
                    p.leave("quarter")
            sp.wait_ge(sems["lo_ready0"], after_layers("lo_ready0"))
            sp.dma_start(w_raw[0][:, 0:1], rope_freq).then_inc(sems["raw_landed0"], 16)
            for m in range(NCH):
                sp.wait_ge(sems["xt_taken"], 2 * (m + 1))
                sp.dma_start(out[0, m * P:(m + 1) * P, :], x_out[m]).then_inc(sems["stored"], 16)
            sp.wait_ge(sems["stored"], 16 * NCH)

        @block.gpsimd
        def _(pool):
            p = Program(pool, sems, "pool_order")
            programs.append(("pool", p))
            g = nc.gpsimd
            p.enter()

            def keep(t, op, fill, base, pattern, mult):
                pool.wait_ge(*p.last)
                g.affine_select(out=t, in_=t, compare_op=op, fill=fill, base=base, pattern=pattern,
                                channel_multiplier=mult).then_inc(*p.count())

            g.memset(ident[:, :], 1.0).then_inc(*p.count())
            g.memset(neg_tri[:, :], -1.0).then_inc(*p.count())
            g.memset(neg_ones[:, :], -1.0).then_inc(*p.count())
            g.memset(ones[:, :], 1.0).then_inc(*p.count())
            g.memset(block_ones[:, :], 0.0).then_inc(*p.count())
            g.memset(mask_incl[:, :], 0.0).then_inc(*p.count())
            g.memset(mask_strict[:, :], 0.0).then_inc(*p.count())
            g.memset(sel[0:HEADS, :], 1.0).then_inc(*p.count())
            g.memset(sel_pair[0:HEADS, :], 1.0).then_inc(*p.count())
            rv = rot[:, :].rearrange("p (a b c) -> p a b c", a=2, b=2)
            g.memset(rv[:, :, 0, :], -1.0).then_inc(*p.count())
            g.memset(rv[:, :, 1, :], 1.0).then_inc(*p.count())
            g.iota(age[:, :], pattern=[[1, T]], base=0, channel_multiplier=-1,
               allow_small_or_imprecise_dtypes=True).then_inc(*p.count())
            pool.wait_ge(*p.last)
            g.memset(block_ones[0:HD, 0:HD], 1.0).then_inc(*p.count())
            g.memset(block_ones[HD:P, HD:P], 1.0).then_inc(*p.count())
            keep(ident[:, :], ALU.is_equal, 0.0, 0, [[-1, P]], 1)
            keep(neg_tri[:, :], ALU.is_ge, 0.0, 0, [[-1, P]], 1)
            keep(mask_incl[:, :], ALU.is_ge, -BIG, 0, [[1, P]], -1)
            keep(mask_strict[:, :], ALU.is_gt, -BIG, 0, [[1, P]], -1)
            keep(sel[0:HEADS, :].rearrange("p (h n) -> p h n", h=HEADS), ALU.is_equal, 0.0, 0,
                 [[-1, HEADS], [0, P]], 1)
            keep(sel_pair[0:HEADS, :].rearrange("p (a b n) -> p a b n", a=2, b=2), ALU.is_equal, 0.0, 0,
                 [[-2, 2], [-1, 2], [0, HD]], 1)
            keep(rv[:, :, 0, :], ALU.is_equal, 0.0, -32, [[-HD, 2], [-1, 32]], 1)
            keep(rv[:, :, 1, :], ALU.is_equal, 0.0, 0, [[-HD, 2], [-1, 32]], 1)
            keep(age[:, :], ALU.is_ge, 1.0e6, 0, [[1, T]], -1)
            pool.wait_ge(*p.last)
            g.memset(own_mask, 1.0).then_inc(*p.count())
            keep(own_mask, ALU.is_ge, 0.0, 0, [[-1, P]], 1)
            pool.wait_ge(*p.last)
            g.memset(c_act[:, :], 0.0).then_inc(*p.count("consts_ready"))
            p.leave("before")

            def lo_part(b, blk):
                s = b % 2
                pool.wait_ge(sems[f"hi_ready{s}"], p.value(f"hi_ready{s}", b // 2 + 1))
                g.tensor_tensor(w_flat(w_lo[s], blk), w_flat(w_raw[s], blk),
                                w_flat(w_hi[s], blk).bitcast(F32), ALU.subtract).then_inc(*p.count(f"lo_ready{s}"))

            with pool.Fori(0, LAYERS) as layer:
                p.enter(layer)
                for b, blk in enumerate(BLOCKS):
                    lo_part(b, blk)
                p.leave("layer")
                with pool.Fori(0, QUARTERS) as q:
                    p.enter(layer, q)
                    for b, blk in enumerate(FF):
                        lo_part(b, blk)
                    p.leave("quarter")

        @block.tensor
        def _(pe):
            p = Program(pe, sems)
            programs.append(("pe", p))
            mm = nc.tensor.matmul

            def wait_bank(tile):
                pe.wait_ge(sems[f"bank_taken{tile % 2}"], p.value(f"bank_taken{tile % 2}", tile // 2))

            def tile_done(ins, tile):
                ins.then_inc(*p.count(f"bank_ready{tile % 2}"))

            def aux_free(n):
                pe.wait_ge(sems["aux_taken"], p.value("aux_taken", n))

            def three(o, wh, wl, xh, xl, first, last):
                mm(o, wh, xh, start=first, stop=False, skip_group_check=True)
                mm(o, wh, xl, start=False, stop=False, skip_group_check=True)
                return mm(o, wl, xh, start=False, stop=last, skip_group_check=True)

            def feature_tile(b, half, tile, rhs, wait_k=None, kn=KT, blk=("x",)):
                s = b % 2
                wh, wl = w_view(w_hi[s], blk), w_view(w_lo[s], blk)
                cs = slice(half * P, (half + 1) * P)
                wait_bank(tile)
                for k in range(kn):
                    if wait_k is not None:
                        wait_k(k)
                    last = three(gemm[tile % 2][:, :], wh[:, k, cs], wl[:, k, cs], part(rhs[0], k), part(rhs[1], k),
                                 k == 0, k == kn - 1)
                return last

            def feature_pair(b, tile, wait_k):
                s = b % 2
                wh, wl = w_view(w_hi[s], ("x",)), w_view(w_lo[s], ("x",))
                for step_k in range(KT + LAG):
                    for half in range(2):
                        k = step_k - half * LAG
                        if not 0 <= k < KT:
                            continue
                        if k == 0:
                            wait_bank(tile + half)
                        if half == 0:
                            wait_k(k)
                        cs = slice(half * P, (half + 1) * P)
                        ins = three(gemm[(tile + half) % 2][:, :], wh[:, k, cs], wl[:, k, cs], part(h_hi, k),
                                    part(h_lo, k), k == 0, k == KT - 1)
                        if k == KT - 1:
                            tile_done(ins, tile + half)

            def token_tile(b, half, tile, blk, chunks, cs):
                s = b % 2
                wh, wl = w_view(w_hi[s], blk), w_view(w_lo[s], blk)
                n = cs.stop - cs.start
                wait_bank(tile)
                for i, ch in enumerate(chunks):
                    for k in range(KT):
                        t0 = k * T + ch * CH
                        last = three(gemm[tile % 2][:, i * n:(i + 1) * n], h_hi[:, t0:t0 + CH], h_lo[:, t0:t0 + CH],
                                     wh[:, k, cs], wl[:, k, cs], k == 0, k == KT - 1)
                return last

            p.enter()
            pe.wait_ge(sems["consts_ready"], 1)
            pe.wait_ge(sems["columns_loaded"], COLUMNS)
            nc.tensor.transpose(aux[:, 0:P], vec_a, ident[:, :]).then_inc(*p.count("aux_ready"))
            pe.wait_ge(sems["aux_taken"], p.value("aux_taken", 1))
            mm(aux[:, 0:56], vec_b[0:56, :], ident[0:56, 0:56], start=True, stop=True).then_inc(*p.count("aux_ready"))
            pe.wait_ge(sems["x_landed"], 16 * NCH)
            for k in range(KT):
                if k >= 2:
                    wait_bank(k)
                for m in range(NCH):
                    ins = nc.tensor.transpose(gemm[k % 2][:, m * P:(m + 1) * P],
                                              x_rows[:, m * D + k * P:m * D + (k + 1) * P], ident[:, :])
                tile_done(ins, k)

            def ada_sum(u, n_aux):
                aux_free(n_aux)
                pe.wait_ge(sems["ada_partial"], p.value("ada_partial", u + 1))
                for col in range(2):
                    for a in range(2):
                        c0 = a * BC + col * P
                        ins = mm(aux[:, col:col + 1], ada_acc[:, c0:c0 + P], ones[:, 0:1], start=(a == 0), stop=(a == 1))
                ins.then_inc(*p.count("aux_ready"))

            pe.wait_ge(sems["c_act_ready"], 1)
            for u in range(ADA_FIRST):
                pe.wait_ge(sems[ada_ring_landed[u % 3]], 16 * (u // 3 + 1))
                for k in range(KT):
                    ins = mm(ada_banks[u // 2][0:1, (u % 2) * BC:(u % 2 + 1) * BC], c_act[:, k:k + 1],
                             ada_ring[u % 3][:, k * BC:(k + 1) * BC], start=(k == 0), stop=(k == KT - 1))
                ins.then_inc(*p.count("ada_used"))
            aux_free(2)
            pe.wait_ge(sems["ada_row_ready"], ADA_FIRST // 2)
            for col in range(2 * ADA_FIRST):
                row = ada_rows[col // 4]
                ins = mm(aux[:, col:col + 1], row[:, (col % 4) * P:(col % 4 + 1) * P], ones[0:1, 0:1], start=True, stop=True)
            ins.then_inc(*p.count("aux_ready"))
            p.leave("before")

            def scores_triangle(h, first):
                r = rows(h)
                for j in (0, 1, 3, 2):
                    o = score[SC_BANK[j]][:, SC_COL[j]:SC_COL[j] + LEN[j]]
                    ins = mm(o, k_cols(h)[r, j * CH:(j + 1) * CH], feat[h // 2][r, j * CH:T],
                             start=(j != 3), stop=not first, skip_group_check=True)
                    if first:
                        ins = mm(o[:, 0:CH], ident[:, :], mask_strict[:, :], start=False, stop=False,
                                 skip_group_check=True)
                return ins

            def pv_triangle(h):
                r = rows(h)
                for j in range(NCH):
                    ins = mm(outp[r, j * CH:T], vt[:, j * WB + h * HD:j * WB + (h + 1) * HD],
                             prb[:, OFF[j]:OFF[j] + LEN[j]], start=(j == 0), stop=(j == NCH - 1),
                             skip_group_check=True)
                return ins

            def step(s):
                kind = s[0]
                if kind in ("norm", "squaresum"):
                    second = kind == "squaresum" or s[1] == 1
                    ks = [s[1]] if kind == "squaresum" else [KT - 2, KT - 1] if second else range(KT)
                    for k in ks:
                        if k == 0:
                            aux_free(AUX[("norm", 1 if second else 0)])
                        pe.wait_ge(sems["square_ready"], p.value("square_ready", k + 1 + (KT + 5 if second else 0)))
                        ins = mm(aux[:, :], ones[:, :], tmps[k % 2], start=(k == 0), stop=(k == KT - 1), skip_group_check=True)
                        ins.then_inc(*p.count("square_used" if k < KT - 1 else "aux_ready"))
                elif kind == "tile":
                    tile_step(s)
                elif kind == "gcol":
                    aux_free(AUX[s])
                    pe.wait_ge(sems["rows_ready"], p.value("rows_ready", 1))
                    for i in range(NCH):
                        ins = mm(aux[:, i * HEADS:(i + 1) * HEADS], row_i[:, i * CH:(i + 1) * CH],
                                 ident[0:HEADS, 0:HEADS], start=True, stop=True)
                    ins.then_inc(*p.count("aux_ready"))
                elif kind == "qk":
                    _, n, h = s
                    g = 4 * n + h
                    if n == 0:
                        if h == 0:
                            pe.wait_ge(sems["feature_ready"], p.value("feature_ready", 4))
                        aux_free(AUX[s])
                        mm(aux[:, :], sel[0:HEADS, h * P:(h + 1) * P], row_m, start=True, stop=True).then_inc(*p.count("aux_ready"))
                    if n == 1 and h == 0:
                        pe.wait_ge(sems["feature_ready"], p.value("feature_ready", 8))
                    if n == 3 and h == 0:
                        pe.wait_ge(sems["feature_ready"], p.value("feature_ready", 11))
                    if n == 2 and h == 0:
                        for half in range(2):
                            tl = TILE_NO[(BLOCK_NO[("s_k",)], half)]
                            pe.wait_ge(sems[f"bank_taken{tl % 2}"], p.value(f"bank_taken{tl % 2}", tl // 2 + 1))
                    pe.wait_ge(sems["scores_taken"], p.value("scores_taken", g))
                    if n < 3:
                        scores_triangle(h, n == 2).then_inc(*p.count("qk_ready"))
                    else:
                        r, kd = rows(h), feat[3 + h // 2]
                        for i in range(NCH):
                            q = feat[h // 2][r, i * CH:(i + 1) * CH]
                            o = score[i // 2][:, (i % 2) * 256:(i % 2) * 256 + 256]
                            if i == 0:
                                mm(o[:, 0:CH], q, kd[r, CH:2 * CH], start=True, stop=True)
                                ins = mm(o[:, CH:256], q, kd[r, 0:CH], start=True, stop=True)
                            else:
                                ins = mm(o, q, kd[r, (i - 1) * CH:(i + 1) * CH], start=True, stop=True)
                        ins.then_inc(*p.count("qk_ready"))
                elif kind == "suffix":
                    h = s[1]
                    pe.wait_ge(sems["softplus_ready"], p.value("softplus_ready", h + 1))
                    for j in range(NCH):
                        for j2 in range(j, NCH):
                            c0 = SC_COL[j] + (j2 - j) * CH
                            last = mm(score[SC_BANK[j]][:, c0:c0 + LEN[j2]], (neg_tri if j2 == j else neg_ones)[:, :],
                                      wrk[:, OFF[j2]:OFF[j2] + LEN[j2]], start=False, stop=(j2 == NCH - 1),
                                      skip_group_check=True)
                    last.then_inc(*p.count("suffix_ready"))
                elif kind == "ptrans":
                    h = s[1]
                    pe.wait_ge(sems["probs_ready"], p.value("probs_ready", h + 1))
                    if h >= 1:
                        pe.wait_ge(sems["ptrans_copied"], p.value("ptrans_copied", h))
                    for n, (i, half) in enumerate(PT_BLOCKS):
                        dst = (score[2] if n < 4 else denp)[:, (n % 4) * CH:(n % 4 + 1) * CH]
                        c0 = i * 256 + half * CH
                        ins = nc.tensor.transpose(dst, prb[:, c0:c0 + CH], ident[:, :])
                    ins.then_inc(*p.count("ptrans_ready"))
                elif kind == "pv":
                    _, n, h = s
                    g = 4 * n + h
                    r = rows(h)
                    if h % 2 == 0:
                        pe.wait_ge(sems["branch_ready"], p.value("branch_ready", 2 * n + h // 2))
                    if h == 0 and n == 3:
                        pe.wait_ge(sems["aux_taken"], p.value("aux_taken", AUX[("vtrans",)] + 1))
                    elif h == 0:
                        for half in range(2):
                            tl = TILE_NO[(BLOCK_NO[(("m_v", "r_v", "s_v")[n],)], half)]
                            pe.wait_ge(sems[f"bank_taken{tl % 2}"], p.value(f"bank_taken{tl % 2}", tl // 2 + 1))
                    if n < 3:
                        pe.wait_ge(sems["scores_taken"], p.value("scores_taken", g + 1))
                        if n == 0:
                            for j in range(NCH):
                                ins = mm(denp[r, j * CH:T], ones[:, 0:HD], prb[:, OFF[j]:OFF[j] + LEN[j]],
                                         start=(j == 0), stop=(j == NCH - 1), skip_group_check=True)
                        pv_triangle(h).then_inc(*p.count("pv_ready"))
                        if s in AUX:
                            aux_free(AUX[s])
                            pr = h // 2
                            mm(aux[:, :], sel_pair[0:HEADS, pr * P:(pr + 1) * P], row_am,
                               start=True, stop=True).then_inc(*p.count("aux_ready"))
                    else:
                        pe.wait_ge(sems["ptrans_copied"], p.value("ptrans_copied", h + 1))
                        for m, (i, half) in enumerate(PT_BLOCKS):
                            v0 = (i - 1 + half) * WB + (h // 2) * HD
                            ins = mm(outp[r, i * CH:(i + 1) * CH], vt[:, v0:v0 + HD], tmp[:, m * CH:(m + 1) * CH],
                                     start=(half == 0 or i == 0), stop=(half == 1), skip_group_check=True)
                        ins.then_inc(*p.count("pv_ready"))
                elif kind == "rot":
                    i = s[1]
                    aux_free(AUX[s])
                    pe.wait_ge(sems["rot_raw"], p.value("rot_raw", i + 1))
                    mm(aux[:, :], rot[:, :], part(wrk, i % 2), start=True, stop=True).then_inc(*p.count("aux_ready"))
                elif kind == "vtrans":
                    tl = TILE_NO[(BLOCK_NO[("a_kv",)], 1)]
                    pe.wait_ge(sems[f"bank_taken{tl % 2}"], p.value(f"bank_taken{tl % 2}", tl // 2 + 1))
                    aux_free(AUX[s])
                    for i in range(NCH):
                        ins = nc.tensor.transpose(aux[:, i * CH:(i + 1) * CH], wrk[:, i * CH:(i + 1) * CH], ident[:, :])
                    ins.then_inc(*p.count("aux_ready"))
                elif kind in ("hnorm", "anorm"):
                    i = s[1]
                    aux_free(AUX[s])
                    pe.wait_ge(sems["square_ready"], p.value("square_ready", KT + (i + 1 if kind == "hnorm" else 3 + i)))
                    t = tmps[0] if kind == "hnorm" else tmps[i % 2]
                    mm(aux[:, :], block_ones[:, :], t, start=True, stop=True).then_inc(*p.count("aux_ready"))
                elif kind == "adasum":
                    ada_sum(s[1], AUX[s])

            def tile_step(s):
                _, b, half = s
                blk = BLOCKS[b]
                name = blk[0]
                tile = TILE_NO[(b, half)]
                sl = b % 2
                if half == 0:
                    pe.wait_ge(sems[f"lo_ready{sl}"], p.value(f"lo_ready{sl}", b // 2 + 1))
                if name in ("m_v", "r_v", "s_v"):
                    ins = token_tile(b, half, tile, blk, (2 * half, 2 * half + 1), slice(0, BC))
                elif name == "m_if" and half == 0:
                    ins = feature_tile(b, half, tile, (h_hi, h_lo), blk=blk)
                elif name == "m_if":
                    wait_bank(tile)
                    pe.wait_ge(sems[f"bank_taken{(tile - 1) % 2}"], p.value(f"bank_taken{(tile - 1) % 2}", (tile - 1) // 2 + 1))
                    ins = mm(gemm[tile % 2][0:P - HEADS, :], ident[0:2 * HEADS, HEADS:P], row_if, start=True, stop=True)
                elif name == "up":
                    if half == 0:
                        pe.wait_ge(sems["branch_ready"], p.value("branch_ready", 2 * blk[1] + 2))
                    ins = feature_tile(b, half, tile, (br_hi, br_lo), kn=2, blk=blk)
                elif blk == ("out", 0) and half == 0:
                    ins = feature_tile(b, half, tile, (h_hi, h_lo), lambda k: pe.wait_ge(sems["merged_ready"], p.value("merged_ready", k + 1)))
                elif name == "m_q":
                    if half == 0:
                        feature_pair(b, tile, lambda k: pe.wait_ge(sems["h_ready"], p.value("h_ready", k + 1)))
                    return
                else:
                    ins = feature_tile(b, half, tile, (h_hi, h_lo))
                tile_done(ins, tile)

            with pe.Fori(0, LAYERS) as layer:
                p.enter(layer)
                for s in STEPS:
                    step(s)
                p.leave("layer")
                with pe.Fori(0, QUARTERS) as q:
                    p.enter(layer, q)
                    for b, blk in enumerate(FF):
                        pe.wait_ge(sems[f"lo_ready{b % 2}"], p.value(f"lo_ready{b % 2}", b // 2 + 1))
                        if b == 0:
                            feature_pair(b, 0, lambda k: pe.wait_ge(sems["h_ready"], at("h_ready", KT + k + 1, layer)))
                            continue
                        for half in range(2):
                            tile = 2 * b + half
                            if blk[0] == "ff1":
                                ins = feature_tile(b, half, tile, (h_hi, h_lo))
                            else:
                                first = lambda k: pe.wait_ge(sems["hidden_ready"], p.value("hidden_ready", k + 1))
                                ins = feature_tile(b, half, tile, (hid_hi, hid_lo), first if tile == 8 else None)
                            tile_done(ins, tile)
                            if half == 0 and b in FF_ADASUM:
                                u = FF_ADASUM[b]
                                ada_sum(u, u)
                    p.leave("quarter")

            p.tail = True
            for m in range(NCH):
                for half in range(2):
                    n = 2 * m + half
                    if n == 0:
                        for b2 in range(2):
                            pe.wait_ge(sems[f"bank_taken{b2}"], after_layers(f"bank_taken{b2}"))
                    if n >= 2:
                        pe.wait_ge(sems["xt_taken"], n - 1)
                    for k in range(4):
                        kk = 4 * half + k
                        ins = nc.tensor.transpose(gemm[n % 2][:, k * P:(k + 1) * P],
                                                  xt[:, kk * T + m * P:kk * T + (m + 1) * P], ident[:, :])
                    ins.then_inc(sems["xt_ready"], 1)

        @block.scalar
        def _(act):
            p = Program(act, sems, "act_order")
            programs.append(("act", p))
            a = nc.scalar.activation

            def hi_part(b, blk, tiles_through):
                s = b % 2
                act.wait_ge(sems[f"raw_landed{s}"], p.value(f"raw_landed{s}", 16 * (b // 2 + 1)))
                if tiles_through is not None:
                    act.wait_ge(sems["bank_ready1"], p.value("bank_ready1", tiles_through // 2))
                nc.scalar.copy(w_flat(w_hi[s], blk), w_flat(w_raw[s], blk)).then_inc(*p.count(f"hi_ready{s}", n=b // 2 + 1))

            def rstd(n, scale, dst):
                act.wait_ge(sems["aux_ready"], p.value("aux_ready", n + 1))
                a(dst, aux[:, :], ACT.Ln, scale=scale, bias=EPS).then_inc(*p.count("aux_taken", n=n + 1))
                act.wait_ge(*p.last)
                a(dst, dst, ACT.Exp, scale=-0.5).then_inc(*p.count("rstd_ready"))

            def branch_hi(n, pair, src, scale):
                if n >= 1 and pair == 0:
                    up = TILE_NO[(BLOCK_NO[("up", n - 1)], 7)]
                    act.wait_ge(sems[f"bank_ready{up % 2}"], p.value(f"bank_ready{up % 2}", up // 2 + 1))
                nc.scalar.mul(part(br_hi, pair), src, scale).then_inc(*p.count("branch_hi_ready"))

            p.enter()
            act.wait_ge(sems["aux_taken"], p.value("aux_taken", 2))
            a(stat[:, 0:8], cols_b[:, 44:52], ACT.Tanh, scale=0.5).then_inc(*p.count("c_tanh"))
            for k in range(KT):
                act.wait_ge(sems[f"bank_ready{k % 2}"], p.value(f"bank_ready{k % 2}", k // 2 + 1))
                nc.scalar.copy(xk(k), gemm[k % 2][:, :]).then_inc(*p.count(f"bank_taken{k % 2}"))
            act.wait_ge(sems["angles_ready"], p.value("angles_ready", 1))
            a(sin[:, :], feat[0][:, :], ACT.Sin).then_inc(*p.count("sines_ready"))
            a(cos[:, :], feat[1][:, :], ACT.Sin).then_inc(*p.count("sines_ready"))
            for n in range(ADA_FIRST // 2):
                act.wait_ge(sems["ada_used"], 2 * (n + 1))
                nc.scalar.copy(ada_rows[n], ada_banks[n][0:1, :]).then_inc(*p.count("ada_row_ready"))
            act.wait_ge(sems["aux_ready"], 3)
            hi_part(0, BLOCKS[0], None)
            p.leave("before")

            def step(s):
                kind = s[0]
                if kind in ("norm", "square", "gate_tanh", "ifrows", "qk", "suffix", "ptrans", "hnorm", "anorm") or (
                        kind == "pv" and s[2] % 2 == 1):
                    act.wait_ge(*p.last)
                if kind in ("norm", "square"):
                    j = 1 if kind == "square" else s[1]
                    for k in ([s[1]] if kind == "square" else [KT - 1] if j else range(KT)):
                        if j == 0 and k == 0:
                            act.wait_ge(sems["bank_taken0"], p.value("bank_taken0", 0))
                            act.wait_ge(sems["bank_taken1"], p.value("bank_taken1", 0))
                        if j == 1:
                            tl = TILE_NO[(BLOCK_NO[("out", k // 2)], k % 2)]
                            act.wait_ge(sems[f"bank_taken{tl % 2}"], p.value(f"bank_taken{tl % 2}", tl // 2 + 1))
                        if k >= 2:
                            act.wait_ge(sems["square_used"], p.value("square_used", j * (KT - 1) + k - 1))
                        if k == 0:
                            a(stat[:, 18:19], ones[:, 0:1], ACT.Ln).then_inc(*p.count())
                        a(tmps[k % 2], xk(k), ACT.Square).then_inc(*p.count("square_ready"))
                    if kind == "square":
                        return
                    rstd(AUX[s], 1.0 / D, wrk[:, 0:T])
                    for k in range(KT):
                        act.wait_ge(sems["h_scaled"], p.value("h_scaled", j * KT + k + 1))
                        a(part(h_hi, k), part(prb, k % 2), ACT.Identity, bias=mod[j][:, k:k + 1]).then_inc(*p.count("h_hi_ready"))
                elif kind == "tile":
                    tile_step(s)
                elif kind == "round":
                    b = s[1]
                    if b <= PRE_BLOCKS:
                        hi_part(b, BLOCKS[b] if b < PRE_BLOCKS else FF[0], TILES_BEFORE[b - 1])
                elif kind == "gate_tanh":
                    _, n, first, end = s
                    for half in range(2):
                        tl = TILE_NO[(BLOCK_NO[("gate", n, end // 2 - 1)], half)]
                        act.wait_ge(sems[f"bank_taken{tl % 2}"], p.value(f"bank_taken{tl % 2}", tl // 2 + 1))
                    g = gates[:, first * T:end * T]
                    a(g, g, ACT.Tanh, scale=0.5).then_inc(*p.count("gate_ready"))
                elif kind == "ifrows":
                    tl = TILE_NO[(BLOCK_NO[("m_if",)], 1)]
                    act.wait_ge(sems[f"bank_taken{tl % 2}"], p.value(f"bank_taken{tl % 2}", tl // 2 + 1))
                    a(row_t, row_f, ACT.Abs).then_inc(*p.count())
                    act.wait_ge(*p.last)
                    a(row_t, row_t, ACT.Exp, scale=-1.0).then_inc(*p.count())
                    act.wait_ge(*p.last)
                    a(row_t, row_t, ACT.Ln, bias=1.0).then_inc(*p.count("logterm_ready"))
                elif kind == "qk":
                    _, n, h = s
                    g = 4 * n + h
                    if n == 0:
                        act.wait_ge(sems["aux_ready"], p.value("aux_ready", AUX[s] + 1))
                        act.wait_ge(sems["masked_ready"], p.value("masked_ready", h + 1))
                        act.wait_ge(sems["scores_taken"], p.value("scores_taken", g))
                        for j in range(NCH - 1):
                            o = wrk[:, OFF[j] + CH:OFF[j] + LEN[j]]
                            ins = a(o, aux[:, (j + 1) * CH:T], ACT.Exp, scale=-1.0,
                                    bias=gcol[:, j * HEADS + h:j * HEADS + h + 1])
                            if j < NCH - 2:
                                ins.then_inc(*p.count())
                            else:
                                ins.then_inc(*p.count("aux_taken", n=AUX[s] + 1))
                        for j in range(NCH):
                            ins = a(wrk[:, OFF[j]:OFF[j] + CH], tmps[0][:, j * CH:(j + 1) * CH], ACT.Exp,
                                    bias=gcol[:, j * HEADS + h:j * HEADS + h + 1])
                            ins.then_inc(*p.count("decay_ready" if j == NCH - 1 else None))
                    elif n == 1:
                        act.wait_ge(sems["scores_taken"], p.value("scores_taken", g))
                        if h == 0:
                            act.wait_ge(sems["feature_ready"], p.value("feature_ready", 8))
                        a(wrk[:, 0:T], age[:, :], ACT.Exp, scale=LOG_GAMMA[h]).then_inc(*p.count("decay_ready"))
                    elif n == 2:
                        act.wait_ge(sems["qk_ready"], p.value("qk_ready", g + 1))
                        for i, (c0, w) in enumerate(((0, T), (T, T), (2 * T, 256))):
                            a(wrk[:, c0:c0 + w], score[i][:, 0:w], ACT.Abs).then_inc(*p.count())
                        act.wait_ge(*p.last)
                        a(wrk[:, :], wrk[:, :], ACT.Exp, scale=-1.0).then_inc(*p.count())
                        act.wait_ge(*p.last)
                        a(wrk[:, :], wrk[:, :], ACT.Ln, bias=1.0).then_inc(*p.count("logterm_ready"))
                    else:
                        act.wait_ge(sems["negmax_ready"], p.value("negmax_ready", h + 1))
                        act.wait_ge(sems["ptrans_ready"], p.value("ptrans_ready", h))
                        act.wait_ge(sems["pv_ready"], p.value("pv_ready", 12))
                        for i in range(NCH):
                            a(prb[:, i * 256:(i + 1) * 256], wrk[:, i * 256:(i + 1) * 256], ACT.Exp,
                              bias=stat[:, NCH + i:NCH + i + 1],
                              accum_out=stat[:, 2 * NCH + i:2 * NCH + i + 1]).then_inc(*p.count())
                        a(stat[:, 3 * NCH:4 * NCH], stat[:, NCH:2 * NCH], ACT.Exp,
                          bias=sink_cur[:, h:h + 1]).then_inc(*p.count("exp_ready"))
                elif kind == "suffix":
                    h = s[1]
                    act.wait_ge(sems["suffix_ready"], p.value("suffix_ready", h + 1))
                    act.wait_ge(sems["pv_ready"], p.value("pv_ready", 8 + h))
                    for i, (c0, w) in enumerate(((0, T), (T, T), (2 * T, 256))):
                        a(prb[:, c0:c0 + w], score[i][:, 0:w], ACT.Exp).then_inc(*p.count("scores_taken" if i == 2 else None, n=8 + h + 1 if i == 2 else None))
                elif kind == "ptrans":
                    h = s[1]
                    act.wait_ge(sems["ptrans_ready"], p.value("ptrans_ready", h + 1))
                    act.wait_ge(sems["pv_ready"], p.value("pv_ready", 12 + h))
                    nc.scalar.copy(tmp[:, 0:T], score[2][:, :]).then_inc(*p.count())
                    nc.scalar.copy(tmp[:, T:7 * CH], denp[:, 0:3 * CH]).then_inc(*p.count("ptrans_copied"))
                elif kind == "pv" and s[2] % 2 == 1:
                    _, n, h = s
                    pair = h // 2
                    act.wait_ge(sems["pv_ready"], p.value("pv_ready", 4 * n + h + 1))
                    if n == 0:
                        act.wait_ge(sems["aux_ready"], p.value("aux_ready", AUX[s] + 1))
                        a(tmps[1], aux[:, :], ACT.Exp, scale=-1.0).then_inc(*p.count("aux_taken", n=AUX[s] + 1))
                        a(tmps[0], denp[:, :], ACT.Abs).then_inc(*p.count("den_ready"))
                        act.wait_ge(sems["out_scaled"], p.value("out_scaled", pair + 1))
                        branch_hi(n, pair, tmps[0], 0.5)
                    elif n == 1:
                        a(tmps[0], outp[:, :], ACT.Square).then_inc(*p.count("square_ready"))
                    else:
                        branch_hi(n, pair, outp[:, :], 1.0)
                elif kind == "hnorm":
                    rstd(AUX[s], 1.0 / HD, tmps[1])
                    act.wait_ge(sems["out_scaled"], p.value("out_scaled", 2 + s[1] + 1))
                    branch_hi(1, s[1], tmps[0], 0.5)
                elif kind == "anorm":
                    rstd(AUX[s], 1.0 / HD, tmps[s[1] % 2])
                elif kind == "vtrans":
                    act.wait_ge(sems["aux_ready"], p.value("aux_ready", AUX[s] + 1))
                    nc.scalar.copy(vt[:, :].rearrange("p (i n) -> p i n", i=NCH)[:, :, 0:P],
                                   aux[:, :].rearrange("p (i n) -> p i n", i=NCH)).then_inc(*p.count("aux_taken", n=AUX[s] + 1))

            def tile_step(s):
                _, b, half = s
                blk = BLOCKS[b]
                name = blk[0]
                tile = TILE_NO[(b, half)]
                bank, bn = gemm[tile % 2], tile // 2 + 1
                act.wait_ge(*p.last)
                if name in ("m_q", "m_k"):
                    i = half + (2 if name == "m_k" else 0)
                    act.wait_ge(sems["conv_ready"], p.value("conv_ready", i + 1))
                    a(part(prb, i % 2), tmps[i % 2], ACT.Tanh, scale=0.5).then_inc(*p.count("silu_ready"))
                elif name == "m_o":
                    act.wait_ge(sems[f"bank_ready{tile % 2}"], p.value(f"bank_ready{tile % 2}", bn))
                    a(feat[4 + half][:, :], bank[:, :], ACT.Tanh, scale=0.5).then_inc(*p.count(f"bank_taken{tile % 2}", n=bn))
                elif name in ("m_v", "r_v", "s_v"):
                    act.wait_ge(sems[f"bank_ready{tile % 2}"], p.value(f"bank_ready{tile % 2}", bn))
                    nc.scalar.copy(vt[:, half * 2 * WB:(half + 1) * 2 * WB], bank[:, :]).then_inc(*p.count(f"bank_taken{tile % 2}", n=bn))
                elif name == "a_kv" and half == 1:
                    act.wait_ge(sems[f"bank_ready{tile % 2}"], p.value(f"bank_ready{tile % 2}", bn))
                    nc.scalar.copy(wrk[:, 0:T], bank[:, :]).then_inc(*p.count(f"bank_taken{tile % 2}", n=bn))
                elif name in ("r_q", "r_k"):
                    i = half + (2 if name == "r_k" else 0)
                    act.wait_ge(sems[f"bank_ready{tile % 2}"], p.value(f"bank_ready{tile % 2}", bn))
                    if i < 2:
                        act.wait_ge(sems["scores_taken"], p.value("scores_taken", 4))
                    else:
                        act.wait_ge(sems["feature_ready"], p.value("feature_ready", 4 + i - 1))
                    nc.scalar.copy(part(wrk, i % 2), bank[:, :]).then_inc(*p.count("rot_raw"))
                elif name == "r_g":
                    act.wait_ge(sems[f"bank_ready{tile % 2}"], p.value(f"bank_ready{tile % 2}", bn))
                    a(tmps[half], bank[:, :], ACT.Tanh, scale=0.5).then_inc(*p.count("silu_ready"))
                elif name == "a_q" or (name == "a_kv" and half == 0):
                    i = half + (2 if name == "a_kv" else 0)
                    act.wait_ge(sems[f"bank_taken{tile % 2}"], p.value(f"bank_taken{tile % 2}", bn))
                    if i == 2:
                        act.wait_ge(sems["feature_ready"], p.value("feature_ready", 9))
                    a(tmps[i % 2], feat[i][:, :], ACT.Square).then_inc(*p.count("square_ready"))
                elif name == "up" and blk[1] == 3:
                    act.wait_ge(sems["merged_tile"], p.value("merged_tile", half + 1))
                    nc.scalar.mul(part(h_hi, half), part(merged, half), 0.5).then_inc(*p.count("merged_hi_ready"))

            with act.Fori(0, LAYERS) as layer:
                p.enter(layer)
                for s in STEPS:
                    step(s)
                p.leave("layer")
                with act.Fori(0, QUARTERS) as q:
                    p.enter(layer, q)
                    for b, blk in enumerate(FF):
                        hi_part(b + 1, ("x",), 2 * b)
                        if blk[0] == "ff1":
                            for half in range(2):
                                tile = 2 * b + half
                                act.wait_ge(sems[f"bank_ready{tile % 2}"], p.value(f"bank_ready{tile % 2}", tile // 2 + 1))
                                a(tmps[tile % 2], gemm[tile % 2][:, :], ACT.Relu).then_inc(*p.count("relu_ready"))
                                act.wait_ge(sems[f"bank_taken{tile % 2}"], p.value(f"bank_taken{tile % 2}", tile // 2 + 1))
                                nc.scalar.copy(part(hid_hi, tile), part(prb, tile % 2)).then_inc(*p.count("hidden_hi_ready"))
                    p.leave("quarter")

        @block.vector
        def _(dve):
            p = Program(dve, sems, "dve_order")
            programs.append(("dve", p))
            v = nc.vector
            stt = v.scalar_tensor_tensor

            def ada_unit(u):
                dve.wait_ge(sems["ada_landed"], p.value("ada_landed", 16 * (u + 1)))
                for k in range(KT):
                    acc = ada_acc[:, (k % 2) * BC:(k % 2 + 1) * BC]
                    w = ada_raw[:, k * BC:(k + 1) * BC]
                    if k < 2:
                        ins = v.tensor_scalar(acc, w, c_act[:, k:k + 1], None, ALU.mult)
                    else:
                        dve.wait_ge(*p.last)
                        ins = stt(out=acc, in0=w, scalar=c_act[:, k:k + 1], in1=acc, op0=ALU.mult, op1=ALU.add)
                    ins.then_inc(*p.count("ada_partial" if k == KT - 1 else None))

            def ada_mod(n_aux, dst, b_col):
                dve.wait_ge(sems["aux_ready"], p.value("aux_ready", n_aux + 1))
                v.tensor_tensor(dst, aux[:, 0:2], b_col, ALU.add).then_inc(*p.count("aux_taken", n=n_aux + 1))

            p.enter()
            dve.wait_ge(sems["aux_ready"], p.value("aux_ready", 1))
            v.tensor_copy(cols_a[:, :], aux[:, 0:P]).then_inc(*p.count("aux_taken"))
            dve.wait_ge(sems["aux_ready"], p.value("aux_ready", 2))
            v.tensor_copy(cols_b[:, :], aux[:, 0:56]).then_inc(*p.count("aux_taken"))
            dve.wait_ge(sems["c_tanh"], p.value("c_tanh", 1))
            dve.wait_ge(*p.last)
            stt(out=c_act[:, :], in0=stat[:, 0:8], scalar=1.0, in1=cols_b[:, 44:52], op0=ALU.add, op1=ALU.mult).then_inc(*p.count())
            dve.wait_ge(*p.last)
            v.tensor_scalar(c_act[:, :], c_act[:, :], 0.5, None, ALU.mult).then_inc(*p.count("c_act_ready"))

            s_arg, c_arg, ang, turns, pos = (feat[n][:, :] for n in range(5))
            own, prev, pos_col = ang, turns, feat[5][:, 0:NCH]
            rel_rows, freq = prb[:, 1024:1152], prb[:, 1184:1185]
            TWO_PI = (6.28125, 0.0019350051879882812, 2.0 * math.pi - 6.28125 - 0.0019350051879882812)
            LIMIT = 3.1415925
            dve.wait_ge(sems["vectors_loaded"], VECTORS)
            v.tensor_copy(pos, wrk[:, 0:T].bitcast(I32)).then_inc(*p.count())
            v.tensor_copy(pos_col, wrk[:, 1024:1028].bitcast(I32)).then_inc(*p.count())
            dve.wait_ge(*p.last)
            v.tensor_scalar(ang, pos, freq, None, ALU.mult).then_inc(*p.count())
            dve.wait_ge(*p.last)
            v.tensor_scalar(turns, ang, 1.0 / (2.0 * math.pi), 12582912.0, ALU.mult, ALU.add).then_inc(*p.count())
            dve.wait_ge(*p.last)
            v.tensor_scalar(turns, turns, 12582912.0, None, ALU.subtract).then_inc(*p.count())
            for n, piece in enumerate(TWO_PI):
                dve.wait_ge(*p.last)
                stt(out=s_arg, in0=turns, scalar=-piece, in1=(ang if n == 0 else s_arg), op0=ALU.mult,
                    op1=ALU.add).then_inc(*p.count())
            dve.wait_ge(*p.last)
            v.tensor_scalar(c_arg, s_arg, math.pi / 2, -2.0 * math.pi, ALU.is_gt, ALU.mult).then_inc(*p.count())
            dve.wait_ge(*p.last)
            stt(out=c_arg, in0=s_arg, scalar=math.pi / 2, in1=c_arg, op0=ALU.add, op1=ALU.add).then_inc(*p.count())
            dve.wait_ge(*p.last)
            v.tensor_scalar(c_arg, c_arg, LIMIT, -LIMIT, ALU.min, ALU.max).then_inc(*p.count())
            dve.wait_ge(*p.last)
            v.tensor_scalar(s_arg, s_arg, LIMIT, -LIMIT, ALU.min, ALU.max).then_inc(*p.count("angles_ready"))

            dve.wait_ge(*p.last)
            for i in range(NCH):
                blk_i = slice(i * CH, (i + 1) * CH)
                blk_p = slice(max(i - 1, 0) * CH, (max(i - 1, 0) + 1) * CH)
                v.tensor_scalar(own[:, blk_i], pos[:, blk_i], pos_col[:, i:i + 1], None, ALU.subtract).then_inc(*p.count())
                v.tensor_scalar(prev[:, blk_i], pos[:, blk_p], pos_col[:, i:i + 1], None, ALU.subtract).then_inc(*p.count())
            dve.wait_ge(*p.last)

            def by_chunk(t):
                return t.rearrange("p (i n) -> p i n", i=NCH)

            def each_chunk(m):
                return m.rearrange("p (o n) -> p o n", o=1).broadcast_to([P, NCH, CH])

            v.tensor_tensor(own, own, prev, ALU.subtract).then_inc(*p.count())
            dve.wait_ge(*p.last)
            v.tensor_tensor(by_chunk(own), by_chunk(own), each_chunk(own_mask), ALU.mult).then_inc(*p.count())
            dve.wait_ge(*p.last)
            tables = [bias[:, h * 2 * T:(h + 1) * 2 * T].rearrange("p (i s n) -> p i s n", i=NCH, s=2)
                      for h in range(HEADS)]
            acc = [t[:, :, 0, :] for t in tables]
            dist, step_of = tables[0][:, :, 1, :], tables[1][:, :, 1, :]
            limit, delta = (tables[HEADS - 1][:, i, 1, :] for i in range(2))
            tb = Program(dve, sems, "table_order")
            programs.append(("table", tb))
            tb.enter()

            def table_bucket(b):
                dve.wait_ge(*tb.last)
                v.tensor_scalar(step_of, dist, float(BUCKET_FROM[b]), None, ALU.is_ge).then_inc(*tb.count())
                dve.wait_ge(*tb.last)
                for h in range(HEADS):
                    d = (b - 1) * HEADS + h
                    stt(out=acc[h], in0=step_of, scalar=delta[:, d:d + 1], in1=acc[h], op0=ALU.mult,
                        op1=ALU.add).then_inc(*tb.count())

            def table_masks(h):
                own_side, prev_side = tables[h][:, :, 1, :], tables[h][:, :, 0, :]
                first = 1 if h == HEADS - 1 else 0
                n = NCH - first
                limits = limit.rearrange("p (o n) -> p o n", o=1).broadcast_to([P, n, CH])
                dve.wait_ge(*tb.last)
                stt(out=own_side[:, first:, :], in0=limits, scalar=-1.0, in1=prev_side[:, first:, :], op0=ALU.mult,
                    op1=ALU.min).then_inc(*tb.count())
                dve.wait_ge(*tb.last)
                v.tensor_tensor(prev_side[:, first:, :], prev_side[:, first:, :], limits, ALU.min).then_inc(*tb.count())
                if first:
                    dve.wait_ge(*tb.last)
                    stt(out=own_side[:, 0, :], in0=limit, scalar=-1.0, in1=prev_side[:, 0, :], op0=ALU.mult,
                        op1=ALU.min).then_inc(*tb.count())
                dve.wait_ge(*tb.last)
                v.memset(prev_side[:, 0, :], -BIG).then_inc(*tb.count())

            stt(out=dist, in0=by_chunk(prev), scalar=-1.0, in1=by_chunk(own), op0=ALU.mult,
                op1=ALU.subtract).then_inc(*tb.count())
            v.tensor_tensor(delta[:, 0:(BUCKETS - 1) * HEADS], rel_rows[:, HEADS:], rel_rows[:, 0:(BUCKETS - 1) * HEADS],
                            ALU.subtract).then_inc(*tb.count())
            v.tensor_scalar(limit, own_mask, -2.0 * BIG, BIG, ALU.mult, ALU.add).then_inc(*tb.count())
            dve.wait_ge(*tb.last)
            for h in range(HEADS):
                v.tensor_scalar(acc[h], dist, 0.0, rel_rows[:, h:h + 1], ALU.mult, ALU.add).then_inc(*tb.count())
            for b in range(1, TABLE_FIRST):
                table_bucket(b)
            dve.wait_ge(sems["aux_ready"], p.value("aux_ready", 3))
            v.tensor_tensor(mod[0][:, 0:2 * KT], aux[:, 0:2 * KT], cols_a[:, 0:2 * KT], ALU.add).then_inc(*p.count("aux_taken"))
            dve.wait_ge(sems["sines_ready"], p.value("sines_ready", 2))
            dve.wait_ge(*p.last)
            v.memset(stat[:, 19:20], 0.0).then_inc(*p.count())
            p.leave("before")

            def split_lo(dst, src, scale, hi, name, n=None):
                stt(out=dst, in0=src, scalar=scale, in1=hi.bitcast(F32), op0=ALU.mult, op1=ALU.subtract).then_inc(*p.count(name, n=n))

            def step(s, layer):
                kind = s[0]
                if kind in ("norm", "ifrows", "gcol", "softplus", "probs", "hnorm", "rot", "headscale", "ada", "adasum") or (
                        kind == "pv" and s[2] % 2 == 1 and s[1] != 1) or (kind == "qk" and s[1] != 2):
                    dve.wait_ge(*p.last)
                if kind == "norm":
                    j = s[1]
                    if j == 0:
                        dve.wait_ge(*p.last)
                        for dst, src, c0, w, per in (
                                (b_cur, cols_a, 16, 2 * ADA_REST, 48), (g_cur, cols_a, 96, 16, 16), (cw_cur, cols_b, 0, 16, 16),
                                (cb_cur, cols_b, 32, 4, 4), (rg_cur, cols_b, 40, 2, 2), (qk_cur[:, 0:1], cols_b, 52, 1, 1),
                                (qk_cur[:, 1:2], cols_b, 54, 1, 1), (sink_cur, sink_all, 0, 4, 4)):
                            v.tensor_copy(dst[:, 0:w], src[:, bass.ds(layer * per + c0, w)]).then_inc(*p.count())
                        v.tensor_copy(gb_cur[0:HEADS, :], gb[0:HEADS, bass.ds(layer * 2, 2)]).then_inc(*p.count())
                    dve.wait_ge(*p.last)
                    stt(out=acol[:, :], in0=mod[j][:, 8:16], scalar=1.0, in1=g_cur[:, 8 * j:8 * j + 8],
                        op0=ALU.add, op1=ALU.mult).then_inc(*p.count())
                    dve.wait_ge(*p.last)
                    dve.wait_ge(sems["rstd_ready"], p.value("rstd_ready", 7 if j else 1))
                    for k in range(KT + 1):
                        if k < KT:
                            if k:
                                dve.wait_ge(*p.last)
                            stt(out=part(prb, k % 2), in0=xk(k), scalar=acol[:, k:k + 1], in1=wrk[:, 0:T],
                                op0=ALU.mult, op1=ALU.mult).then_inc(*p.count("h_scaled"))
                        if k > 0:
                            dve.wait_ge(sems["h_hi_ready"], p.value("h_hi_ready", j * KT + k))
                            stt(out=part(h_lo, k - 1), in0=part(prb, (k - 1) % 2), scalar=mod[j][:, k - 1:k],
                                in1=part(h_hi, k - 1).bitcast(F32), op0=ALU.add, op1=ALU.subtract).then_inc(*p.count("h_ready"))
                elif kind == "tile":
                    tile_step(s)
                elif kind == "ifrows":
                    v.memset(row_one, 1.0).then_inc(*p.count())
                    dve.wait_ge(sems["logterm_ready"], p.value("logterm_ready", 1))
                    dve.wait_ge(*p.last)
                    stt(out=row_t, in0=row_f, scalar=0.0, in1=row_t, op0=ALU.min, op1=ALU.subtract).then_inc(*p.count())
                    dve.wait_ge(*p.last)
                    v.tensor_tensor_scan(row_a, row_one, row_t, 0.0, ALU.mult, ALU.add).then_inc(*p.count())
                    dve.wait_ge(*p.last)
                    v.tensor_tensor(row_i, row_i, row_a, ALU.subtract).then_inc(*p.count())
                    dve.wait_ge(*p.last)
                    v.tensor_tensor_scan(row_m, row_i, row_i, 0.0, ALU.max, ALU.max).then_inc(*p.count())
                    dve.wait_ge(*p.last)
                    v.tensor_tensor(row_am, row_a, row_m, ALU.add).then_inc(*p.count("rows_ready"))
                elif kind == "gcol":
                    dve.wait_ge(sems["aux_ready"], p.value("aux_ready", AUX[s] + 1))
                    v.tensor_copy(gcol[:, :], aux[:, 0:NCH * HEADS]).then_inc(*p.count("aux_taken", n=AUX[s] + 1))
                elif kind == "qk":
                    qk_step(s)
                elif kind in ("softplus", "probs"):
                    softmax_step(s)
                elif kind == "pv" and s[2] % 2 == 1:
                    _, n, h = s
                    pair = h // 2
                    if n == 0:
                        dve.wait_ge(sems["den_ready"], p.value("den_ready", pair + 1))
                        dve.wait_ge(*p.last)
                        v.tensor_tensor(tmps[0], tmps[0], tmps[1], ALU.max).then_inc(*p.count())
                        dve.wait_ge(*p.last)
                        v.reciprocal(tmps[0], tmps[0]).then_inc(*p.count())
                        dve.wait_ge(*p.last)
                        v.tensor_tensor(tmps[0], outp[:, :], tmps[0], ALU.mult).then_inc(*p.count())
                        dve.wait_ge(*p.last)
                        stt(out=tmps[0], in0=feat[4 + pair][:, :], scalar=1.0, in1=tmps[0], op0=ALU.add,
                            op1=ALU.mult).then_inc(*p.count("out_scaled"))
                        dve.wait_ge(sems["branch_hi_ready"], p.value("branch_hi_ready", pair + 1))
                        split_lo(part(br_lo, pair), tmps[0], 0.5, part(br_hi, pair), "branch_ready")
                    elif n >= 2:
                        dve.wait_ge(sems["branch_hi_ready"], p.value("branch_hi_ready", 2 * n + pair + 1))
                        split_lo(part(br_lo, pair), outp[:, :], 1.0, part(br_hi, pair), "branch_ready")
                elif kind == "hnorm":
                    pair = s[1]
                    dve.wait_ge(sems["rstd_ready"], p.value("rstd_ready", 2 + pair))
                    stt(out=tmps[0], in0=outp[:, :], scalar=rg_cur[:, pair:pair + 1], in1=tmps[1],
                        op0=ALU.mult, op1=ALU.mult).then_inc(*p.count())
                    dve.wait_ge(*p.last)
                    v.tensor_tensor(tmps[0], tmps[0], feat[4 + pair][:, :], ALU.mult).then_inc(*p.count("out_scaled"))
                    dve.wait_ge(sems["branch_hi_ready"], p.value("branch_hi_ready", 2 + pair + 1))
                    split_lo(part(br_lo, pair), tmps[0], 0.5, part(br_hi, pair), "branch_ready")
                elif kind == "rot":
                    i = s[1]
                    dve.wait_ge(sems["aux_ready"], p.value("aux_ready", AUX[s] + 1))
                    v.tensor_tensor(part(wrk, i % 2), aux[:, :], sin[:, :], ALU.mult).then_inc(*p.count("aux_taken", n=AUX[s] + 1))
                    dve.wait_ge(*p.last)
                    v.tensor_tensor(feat[i][:, :], feat[i][:, :], part(wrk, i % 2), ALU.add).then_inc(*p.count("feature_ready"))
                elif kind == "headscale":
                    i = s[1]
                    dve.wait_ge(sems["rstd_ready"], p.value("rstd_ready", 4 + i))
                    r = tmps[i % 2]
                    if i < 2:
                        stt(out=feat[i][:, :], in0=feat[i][:, :], scalar=qk_cur[:, 0:1], in1=r, op0=ALU.mult,
                            op1=ALU.mult).then_inc(*p.count("feature_ready"))
                    else:
                        for n, (kv, to) in enumerate(((0, 0), (0, 1), (1, 0), (1, 1))):
                            f = slice(kv * HD, (kv + 1) * HD)
                            ins = stt(out=feat[3 + kv][to * HD:(to + 1) * HD, :], in0=feat[2][f, :],
                                      scalar=qk_cur[f, 1:2], in1=r[f, :], op0=ALU.mult, op1=ALU.mult)
                            ins.then_inc(*p.count("feature_ready" if n == 3 else None))
                elif kind == "ada":
                    dve.wait_ge(*p.last)
                    ada_unit(s[1])
                elif kind == "adasum":
                    j, c = divmod(2 * KT + 2 * s[1], 3 * KT)
                    ada_mod(AUX[s], mod[j][:, c:c + 2], b_cur[:, 2 * s[1]:2 * s[1] + 2])
                elif kind == "table":
                    with dve.If(layer < 1):
                        if s[1] < BUCKETS - TABLE_FIRST:
                            table_bucket(TABLE_FIRST + s[1])
                        else:
                            table_masks(s[1] - (BUCKETS - TABLE_FIRST))

            def qk_step(s):
                _, n, h = s
                g = 4 * n + h
                if n == 0:
                    dve.wait_ge(sems["aux_ready"], p.value("aux_ready", AUX[s] + 1))
                    dve.wait_ge(*p.last)
                    stt(out=by_chunk(tmps[0]), in0=by_chunk(aux[:, :]), scalar=-1.0, in1=each_chunk(mask_incl[:, :]),
                        op0=ALU.mult, op1=ALU.add).then_inc(*p.count("masked_ready"))
                if n < 2:
                    dve.wait_ge(sems["qk_ready"], p.value("qk_ready", g + 1))
                    dve.wait_ge(sems["decay_ready"], p.value("decay_ready", g + 1))
                    dve.wait_ge(sems["pv_ready"], p.value("pv_ready", g))
                    if n == 0:
                        for i, (c0, w) in enumerate(((0, T), (T, T), (2 * T, 256))):
                            ins = stt(out=prb[:, c0:c0 + w], in0=score[i][:, 0:w], scalar=0.25 * HD ** -0.5,
                                      in1=wrk[:, c0:c0 + w], op0=ALU.mult, op1=ALU.mult)
                            ins.then_inc(*p.count("scores_taken" if i == 2 else None, n=g + 1 if i == 2 else None))
                    else:
                        for j in range(NCH):
                            ins = stt(out=prb[:, OFF[j]:OFF[j] + LEN[j]],
                                      in0=score[SC_BANK[j]][:, SC_COL[j]:SC_COL[j] + LEN[j]], scalar=HD ** -0.5,
                                      in1=wrk[:, 0:LEN[j]], op0=ALU.mult, op1=ALU.mult)
                            last = j == NCH - 1
                            ins.then_inc(*p.count("scores_taken" if last else None, n=g + 1 if last else None))
                elif n == 3:
                    dve.wait_ge(sems["qk_ready"], p.value("qk_ready", g + 1))
                    if h == 0:
                        dve.wait_ge(*tb.last)
                    for i in range(2):
                        ins = stt(out=part(wrk, i), in0=score[i][:, :], scalar=HD ** -0.5,
                                  in1=bias[:, h * 2 * T + i * T:h * 2 * T + (i + 1) * T], op0=ALU.mult, op1=ALU.add)
                        ins.then_inc(*p.count("scores_taken" if i else None, n=g + 1 if i else None))
                    dve.wait_ge(*p.last)
                    v.tensor_reduce(stat[:, 0:NCH], wrk[:, 0:2 * T].rearrange("p (i n) -> p i n", i=NCH), AX.X,
                                    ALU.max).then_inc(*p.count())
                    dve.wait_ge(*p.last)
                    v.tensor_scalar(stat[:, NCH:2 * NCH], stat[:, 0:NCH], sink_cur[:, h:h + 1], -1.0, ALU.max,
                                    ALU.mult).then_inc(*p.count("negmax_ready"))

            def softmax_step(s):
                kind, h = s
                if kind == "softplus":
                    dve.wait_ge(sems["logterm_ready"], p.value("logterm_ready", 1 + h + 1))
                    for i, (c0, w) in enumerate(((0, T), (T, T), (2 * T, 256))):
                        ins = stt(out=wrk[:, c0:c0 + w], in0=score[i][:, 0:w], scalar=0.0, in1=wrk[:, c0:c0 + w],
                                  op0=ALU.max, op1=ALU.add)
                        ins.then_inc(*p.count("softplus_ready" if i == 2 else None))
                else:
                    dve.wait_ge(sems["exp_ready"], p.value("exp_ready", h + 1))
                    den = stat[:, 4 * NCH:5 * NCH]
                    v.tensor_tensor(den, stat[:, 2 * NCH:3 * NCH], stat[:, 3 * NCH:4 * NCH], ALU.add).then_inc(*p.count())
                    dve.wait_ge(*p.last)
                    v.reciprocal(den, den).then_inc(*p.count())
                    dve.wait_ge(*p.last)
                    for i in range(NCH):
                        pi = prb[:, i * 256:(i + 1) * 256]
                        v.tensor_scalar(pi, pi, den[:, i:i + 1], None, ALU.mult).then_inc(*p.count("probs_ready" if i == NCH - 1 else None))

            def tile_step(s):
                _, b, half = s
                blk = BLOCKS[b]
                name = blk[0]
                tile = TILE_NO[(b, half)]
                bank, taken, bn = gemm[tile % 2], f"bank_taken{tile % 2}", tile // 2 + 1
                if name in ("m_q", "m_k"):
                    i = half + (2 if name == "m_k" else 0)
                    u = tmps[i % 2]
                    dve.wait_ge(sems[f"bank_ready{tile % 2}"], p.value(f"bank_ready{tile % 2}", bn))
                    dve.wait_ge(*p.last)
                    v.tensor_scalar(u, bank[:, :], cw_cur[:, 12 + i:13 + i], cb_cur[:, i:i + 1], ALU.mult, ALU.add).then_inc(*p.count())
                    for back in range(1, 4):
                        dve.wait_ge(*p.last)
                        ins = stt(out=u[:, back:T], in0=bank[:, 0:T - back],
                                  scalar=cw_cur[:, (3 - back) * 4 + i:(3 - back) * 4 + i + 1], in1=u[:, back:T],
                                  op0=ALU.mult, op1=ALU.add)
                        if back < 3:
                            ins.then_inc(*p.count())
                        else:
                            ins.then_inc(*p.count("conv_ready"))
                    v.memset(stat[:, 19:20], 0.0).then_inc(*p.count(taken, n=bn))
                    dve.wait_ge(sems["silu_ready"], p.value("silu_ready", i + 1))
                    stt(out=feat[i][:, :], in0=part(prb, i % 2), scalar=1.0, in1=u, op0=ALU.add, op1=ALU.mult).then_inc(*p.count("feature_ready"))
                elif name == "m_if":
                    dve.wait_ge(sems[f"bank_ready{tile % 2}"], p.value(f"bank_ready{tile % 2}", bn))
                    if half == 0:
                        v.tensor_scalar(row_i, bank[0:HEADS, :], gb_cur[0:HEADS, 0:1], None, ALU.add).then_inc(*p.count())
                        v.tensor_copy(row_if, bank[0:2 * HEADS, :]).then_inc(*p.count(taken, n=bn))
                    else:
                        v.tensor_scalar(row_f, bank[0:HEADS, :], gb_cur[0:HEADS, 1:2], None, ALU.add).then_inc(*p.count(taken, n=bn))
                elif name == "gate":
                    dve.wait_ge(sems[f"bank_ready{tile % 2}"], p.value(f"bank_ready{tile % 2}", bn))
                    v.tensor_copy(gate_tile(2 * blk[2] + half), bank[:, :]).then_inc(*p.count(taken, n=bn))
                elif name in ("r_q", "r_k"):
                    i = half + (2 if name == "r_k" else 0)
                    dve.wait_ge(sems["rot_raw"], p.value("rot_raw", i + 1))
                    v.tensor_tensor(feat[i][:, :], bank[:, :], cos[:, :], ALU.mult).then_inc(*p.count(taken, n=bn))
                elif name == "r_g":
                    dve.wait_ge(sems["silu_ready"], p.value("silu_ready", 4 + half + 1))
                    stt(out=feat[4 + half][:, :], in0=tmps[half], scalar=1.0, in1=bank[:, :], op0=ALU.add,
                        op1=ALU.mult).then_inc(*p.count(taken, n=bn))
                elif name in ("s_q", "s_k"):
                    dve.wait_ge(sems[f"bank_ready{tile % 2}"], p.value(f"bank_ready{tile % 2}", bn))
                    f = feat[half + (2 if name == "s_k" else 0)][:, :]
                    v.tensor_scalar(f, bank[:, :], HD ** -0.5 if name == "s_q" else 1.0, None, ALU.mult).then_inc(*p.count(taken, n=bn))
                elif name == "a_q" or (name == "a_kv" and half == 0):
                    dve.wait_ge(sems[f"bank_ready{tile % 2}"], p.value(f"bank_ready{tile % 2}", bn))
                    v.tensor_copy(feat[half + (2 if name == "a_kv" else 0)][:, :], bank[:, :]).then_inc(*p.count(taken, n=bn))
                elif name == "up":
                    n, m = blk[1], half
                    if m in (0, 6):
                        dve.wait_ge(sems["gate_ready"], p.value("gate_ready", (1, 2, 3 + m // 6, 5 + m // 6)[n]))
                    dve.wait_ge(sems[f"bank_ready{tile % 2}"], p.value(f"bank_ready{tile % 2}", bn))
                    dst = part(merged, m) if n == 0 else gate_tile(m)
                    stt(out=dst, in0=gate_tile(m), scalar=1.0, in1=bank[:, :], op0=ALU.add, op1=ALU.mult).then_inc(*p.count(taken, n=bn))
                    if n > 0:
                        dve.wait_ge(*p.last)
                        v.tensor_tensor(part(merged, m), part(merged, m), gate_tile(m), ALU.add).then_inc(*p.count("merged_tile" if n == 3 else None))
                    if n == 3:
                        for k in ([m - 1] if m else []) + ([7] if m == 7 else []):
                            dve.wait_ge(sems["merged_hi_ready"], p.value("merged_hi_ready", k + 1))
                            split_lo(part(h_lo, k), part(merged, k), 0.5, part(h_hi, k), "merged_ready")
                elif name == "out":
                    m = 2 * blk[1] + half
                    dve.wait_ge(sems[f"bank_ready{tile % 2}"], p.value(f"bank_ready{tile % 2}", bn))
                    stt(out=xk(m), in0=bank[:, :], scalar=mod[0][:, 16 + m:17 + m], in1=xk(m), op0=ALU.mult,
                        op1=ALU.add).then_inc(*p.count(taken, n=bn))

            with dve.Fori(0, LAYERS) as layer:
                p.enter(layer)
                for s in STEPS:
                    step(s, layer)
                p.leave("layer")
                tb.leave("before")
                with dve.Fori(0, QUARTERS) as q:
                    p.enter(layer, q)
                    for b, blk in enumerate(FF):
                        for half in range(2):
                            tile = 2 * b + half
                            bank, taken, bn = gemm[tile % 2], f"bank_taken{tile % 2}", tile // 2 + 1
                            if blk[0] == "ff1":
                                sq = part(prb, tile % 2)
                                dve.wait_ge(sems["relu_ready"], p.value("relu_ready", tile + 1))
                                stt(out=sq, in0=bank[:, :], scalar=0.0, in1=tmps[tile % 2], op0=ALU.max,
                                    op1=ALU.mult).then_inc(*p.count(taken, n=bn))
                                dve.wait_ge(sems["hidden_hi_ready"], p.value("hidden_hi_ready", tile + 1))
                                v.tensor_tensor(part(hid_lo, tile), sq, part(hid_hi, tile).bitcast(F32),
                                                ALU.subtract).then_inc(*p.count("hidden_ready"))
                            else:
                                m = tile - 8
                                dve.wait_ge(sems[f"bank_ready{tile % 2}"], p.value(f"bank_ready{tile % 2}", bn))
                                stt(out=xk(m), in0=bank[:, :], scalar=mod[1][:, 16 + m:17 + m], in1=xk(m),
                                    op0=ALU.mult, op1=ALU.add).then_inc(*p.count(taken, n=bn))
                            if half == 0 and b in FF_ADASUM:
                                u = FF_ADASUM[b]
                                ada_mod(u, mod[0][:, bass.ds(q * 4 + 2 * u, 2)],
                                        cols_a[:, bass.ds(q * 4 + (48 + 2 * u), 2)])
                        if b in FF_ADA:
                            dve.wait_ge(*p.last)
                            ada_unit(FF_ADA[b])
                    v.memset(stat[:, 19:20], 0.0).then_inc(*p.count())
                    p.leave("quarter")

            for n in range(2 * NCH):
                dve.wait_ge(sems["xt_ready"], n + 1)
                v.tensor_copy(x_out[n // 2][:, (n % 2) * T:(n % 2 + 1) * T], gemm[n % 2][:, :]).then_inc(
                    sems["xt_taken"], 1)

    return programs


def check_counts(programs):
    total = {}
    for _, p in programs:
        for region, i in (("before", 0), ("layer", 1), ("quarter", 2)):
            for name, n in p.seen.get(region, {}).items():
                total.setdefault(name, [0, 0, 0])[i] += n
    wrong = {name: tuple(t) for name, t in total.items() if tuple(t) != COUNTS[name] and not name.startswith("hi_ready")}
    assert not wrong, wrong


_INS = ["x", "c", "positions", "w_ada", "b_ada", "norm_g", "w_in", "mlstm_conv_w", "mlstm_conv_b", "mlstm_gate_b",
        "ret_norm_g", "swa_q_norm_g", "swa_k_norm_g", "swa_sinks", "rel_bias", "w_up", "w_out", "w_ff1", "w_ff2"]


def kernel(**inputs):
    import concourse.bacc as bacc
    from concourse.bass_utils import run_bass_kernel_spmd

    nc = bacc.Bacc("TRN2", target_bir_lowering=False, num_devices=1)
    arrays = {f"in_{name}": np.ascontiguousarray(inputs[name]) for name in _INS}
    half = HD // 2
    inv = np.float32(10000.0) ** (-np.arange(half, dtype=np.float32) / np.float32(half))
    arrays["rope_freq"] = np.tile(inv, P // half).reshape(P, 1).astype(np.float32)
    args = [nc.dram_tensor(name, a.shape, mybir.dt.from_np(a.dtype), kind="ExternalInput").ap()
            for name, a in arrays.items()]
    args.append(nc.dram_tensor("out", (1, T, D), F32, kind="ExternalOutput").ap())
    check_counts(trunk(nc, *args))
    return run_bass_kernel_spmd(nc, [arrays], core_ids=[0]).results[0]["out"]
```

```python
from contextlib import ExitStack
import math

import numpy as np

import concourse.bass as bass
from concourse import mybir
from concourse.alu_op_type import AluOpType as ALU

ACT = mybir.ActivationFunctionType
AX = mybir.AxisListType
F32 = mybir.dt.float32
F32R = mybir.dt.float32r
I32 = mybir.dt.int32

P = 128
LAYERS = 2
T = 512
D = 1024
KT = D // P
HD = 64
HEADS = 4
CH = 128
NCH = T // CH
WB = HEADS * HD
NBR = 4
DFF = 4 * D
QUARTERS = DFF // D
BUCKETS = 32
MAX_DIST = 128
EPS = 1e-6
BIG = 1.0e30
BC = 256
VC = 6 * HD
LAG = 2
LOG_GAMMA = [math.log(1.0 - 2.0 ** -(5.0 + h)) for h in range(HEADS)]
COLS = {"m_q": 0, "m_k": 256, "m_v": 512, "m_if": 768, "m_o": 776, "r_q": 1032, "r_k": 1288, "r_v": 1544,
        "r_g": 1800, "s_q": 2056, "s_k": 2312, "s_v": 2568, "a_q": 2824, "a_kv": 3080, "gate": 3336}

SC_BANK = [0, 1, 2, 1]
SC_COL = [0, 0, 0, 384]
OFF = [0, 512, 1024, 896]
LEN = [T - CH * j for j in range(NCH)]
PT_BLOCKS = [(0, 1), (1, 0), (1, 1), (2, 0), (2, 1), (3, 0), (3, 1)]

EXACT = BUCKETS // 2
BUCKET_FROM = [b if b < EXACT else math.ceil(EXACT * (MAX_DIST / EXACT) ** ((b - EXACT) / (BUCKETS - EXACT)) - 1e-9)
               for b in range(BUCKETS)]
ADA_FIRST = 2 * D // BC
ADA_REST = 4 * D // BC
ADA_BLOCK = [2, 4, 6, 8, 12, 13, 15, 17, 18, 20, 21, 24, 26, 28, 29, 31]
TABLE_FIRST = 8


def plan():
    blocks, steps = [], []

    def block(name, *arg):
        b = len(blocks)
        blocks.append((name, *arg))
        tiles = 8 if name == "up" else 2
        for h in range(tiles):
            early = name in ("m_q", "m_k", "r_q", "r_k") and h == tiles - 1
            if early:
                steps.append(("round", b + 2))
            steps.append(("tile", b, h))
            first = [s for s in after.get((b, h), []) if s[0] in ("square", "gate_tanh")]
            steps.extend(first)
            if h == tiles - 1 and not early:
                steps.append(("round", b + 2))
            steps.extend(s for s in after.pop((b, h), []) if s not in first)
        for s in after.pop((b, "end"), []):
            steps.append(s)

    after = {}

    def put(b, h, *s):
        after.setdefault((b, h), []).extend(s)

    names = ([("m_q",), ("m_k",), ("m_if",), ("m_v",), ("m_o",)] + [("gate", 0, g) for g in range(4)]
             + [("r_q",), ("r_k",), ("up", 0), ("r_v",), ("r_g",)] + [("gate", 1, g) for g in range(4)]
             + [("s_q",), ("s_k",), ("up", 1), ("s_v",)] + [("gate", 2, g) for g in range(3)]
             + [("a_q",), ("a_kv",), ("gate", 2, 3), ("up", 2)] + [("gate", 3, g) for g in range(4)] + [("up", 3)]
             + [("out", g) for g in range(4)])
    no = {n: i for i, n in enumerate(names)}
    for u, b in enumerate(ADA_BLOCK):
        assert names[b + 1][0] != "up"
        if b + 1 in ADA_BLOCK or b == no[("gate", 2, 2)]:
            put(b + 1, 1, ("adasum", u))
        else:
            put(b + 2, 0, ("adasum", u))
    put(no[("m_v",)], 0, ("ifrows",))
    put(no[("m_o",)], 0, ("gcol",))
    put(no[("m_o",)], "end", ("qk", 0, 0))
    put(no[("gate", 0, 0)], "end", ("qk", 0, 1), ("pv", 0, 0))
    put(no[("gate", 0, 1)], "end", ("qk", 0, 2), ("pv", 0, 1))
    put(no[("gate", 0, 2)], 0, ("divide", 0))
    put(no[("gate", 0, 2)], "end", ("qk", 0, 3), ("pv", 0, 2))
    put(no[("gate", 0, 3)], "end", ("gate_tanh", 0, 0, 8))
    put(no[("r_q",)], 0, ("pv", 0, 3), ("divide", 1))
    put(no[("r_q",)], 1, ("rot", 0))
    put(no[("r_k",)], 0, ("rot", 1))
    put(no[("r_k",)], 1, ("rot", 2))
    put(no[("up", 0)], 1, ("rot", 3))
    put(no[("r_g",)], "end", ("qk", 1, 0))
    put(no[("gate", 1, 0)], "end", ("qk", 1, 1), ("pv", 1, 0))
    put(no[("gate", 1, 1)], "end", ("qk", 1, 2), ("pv", 1, 1))
    put(no[("gate", 1, 2)], 0, ("hnorm", 0))
    put(no[("gate", 1, 2)], "end", ("qk", 1, 3), ("pv", 1, 2))
    put(no[("gate", 1, 3)], "end", ("gate_tanh", 1, 0, 8), ("pv", 1, 3))
    put(no[("s_q",)], 0, ("hnorm", 1))
    put(no[("s_k",)], "end", ("qk", 2, 0))
    put(no[("up", 1)], 7, ("softplus", 0))
    put(no[("s_v",)], 0, ("suffix", 0))
    put(no[("s_v",)], 1, ("qk", 2, 1))
    put(no[("gate", 2, 0)], 0, ("pv", 2, 0), ("softplus", 1))
    put(no[("gate", 2, 0)], 1, ("suffix", 1))
    put(no[("gate", 2, 1)], 0, ("qk", 2, 2), ("pv", 2, 1))
    put(no[("gate", 2, 1)], 1, ("softplus", 2))
    put(no[("gate", 2, 2)], 0, ("suffix", 2))
    put(no[("gate", 2, 2)], 1, ("qk", 2, 3), ("pv", 2, 2))
    put(no[("gate", 2, 2)], "end", ("gate_tanh", 2, 0, 6))
    put(no[("a_q",)], 0, ("softplus", 3))
    put(no[("a_q",)], 1, ("suffix", 3), ("anorm", 0))
    put(no[("a_kv",)], 0, ("headscale", 0))
    put(no[("a_kv",)], 1, ("headscale", 1))
    put(no[("gate", 2, 3)], 0, ("headscale", 2), ("vtrans",))
    put(no[("gate", 2, 3)], 1, ("gate_tanh", 2, 6, 8))
    put(no[("a_kv",)], 0, ("pv", 2, 3), ("anorm", 1))
    put(no[("a_kv",)], 1, ("anorm", 2))
    put(no[("gate", 2, 3)], 1, ("qk", 3, 0))
    put(no[("up", 2)], 3, ("probs", 0))
    put(no[("up", 2)], 6, ("ptrans", 0))
    put(no[("up", 2)], "end", ("qk", 3, 1))
    put(no[("gate", 3, 0)], 0, ("pv", 3, 0), ("probs", 1))
    put(no[("gate", 3, 0)], 1, ("ptrans", 1), ("qk", 3, 2))
    put(no[("gate", 3, 1)], 0, ("pv", 3, 1), ("probs", 2))
    put(no[("gate", 3, 1)], 1, ("ptrans", 2), ("qk", 3, 3))
    put(no[("gate", 3, 2)], 0, ("pv", 3, 2), ("probs", 3))
    put(no[("gate", 3, 2)], 1, ("ptrans", 3))
    put(no[("gate", 3, 2)], "end", ("gate_tanh", 3, 0, 6))
    put(no[("gate", 3, 3)], 0, ("pv", 3, 3))
    put(no[("gate", 3, 3)], 1, ("gate_tanh", 3, 6, 8))
    for k in range(KT - 1):
        put(no[("out", (k + 1) // 2)], (k + 1) % 2, ("square", k))
        if k < KT - 2:
            put(no[("out", (k + 2) // 2)], (k + 2) % 2, ("squaresum", k))
    for u, b in enumerate(ADA_BLOCK):
        put(b, "end", ("ada", u))
    spots = [(no[("gate", n, g)], half) for n in range(3) for g in range(4) for half in range(2)
             if (n or not half) and (n, g, half) not in ((2, 3, 1), (2, 1, 0))]
    spots += [(no[("m_o",)], 1), (no[("r_v",)], 0), (no[("r_v",)], 1), (no[("r_g",)], 0), (no[("s_q",)], 1),
              (no[("s_k",)], 1), (no[("s_v",)], 0), (no[("s_q",)], 0),
              (no[("a_kv",)], 0), (no[("r_g",)], 1)]
    assert len(spots) == BUCKETS - TABLE_FIRST + HEADS
    for n, (b, half) in enumerate(sorted(spots)):
        put(b, half, ("table", n))
    steps.append(("norm", 0))
    for n in names:
        block(*n)
    assert not after
    steps.append(("norm", 1))
    return blocks, steps


BLOCKS, STEPS = plan()
PRE_BLOCKS = len(BLOCKS)
assert PRE_BLOCKS % 2 == 0
TILE_NO = {}
for _s in STEPS:
    if _s[0] == "tile":
        TILE_NO[_s[1:]] = len(TILE_NO)
PRE_TILES = len(TILE_NO)
BLOCK_NO = {b: i for i, b in enumerate(BLOCKS)}
FF_ADA = {1: 0, 4: 1}
FF_ADASUM = {3: 0, 6: 1}


def makes_aux(s):
    return (s[0] in ("norm", "gcol", "vtrans", "hnorm", "anorm", "adasum")
            or s[:2] == ("qk", 0) or s[0] == "divide")


AUX = {s: n for n, s in enumerate(s for s in STEPS if makes_aux(s))}
PRO_AUX = 2 + 1

TABLE_STEPS = 3 + HEADS + (1 + HEADS) * (BUCKETS - 1) + 3 * HEADS + 1

STARTED = ("lo_ready0", "lo_ready1", "ada_partial", "act_order", "scores_taken", "pv_ready", "ptrans_ready",
           "branch_ready")

_BLK = PRE_BLOCKS // 2
_TL = PRE_TILES // 2
COUNTS = {
    "raw_landed0": (0, 16 * _BLK, 64), "raw_landed1": (0, 16 * _BLK, 64),
    "hi_ready0": (0, _BLK, 4), "hi_ready1": (0, _BLK, 4), "lo_ready0": (1, _BLK, 4), "lo_ready1": (1, _BLK, 4),
    "ada_landed": (16 * 3, 16 * ADA_REST, 16 * 2), "ada_landed_b": (16 * 3, 0, 0), "ada_landed_c": (16 * 2, 0, 0),
    "ada_used": (ADA_FIRST, 0, 0), "ada_row_ready": (ADA_FIRST // 2, 0, 0), "c_act_ready": (1, 0, 0),
    "ada_partial": (1, ADA_REST, 2),
    "bank_ready0": (4, _TL, 8), "bank_ready1": (4, _TL, 8), "bank_taken0": (4, _TL, 8), "bank_taken1": (4, _TL, 8),
    "aux_ready": (PRO_AUX, len(AUX), 2), "aux_taken": (PRO_AUX, len(AUX), 2),
    "square_ready": (0, KT + 5, 0), "square_used": (0, KT - 2, 0), "next_square_ready": (KT, KT, 0),
    "next_square_used": (KT - 2, KT - 2, 0), "rstd_ready": (0, 2 + 5, 0),
    "h_scaled": (0, 2 * KT, 0), "h_hi_ready": (0, 2 * KT, 0), "h_ready": (0, 2 * KT, 0),
    "feature_ready": (0, 4 + 4 + 3, 0), "conv_ready": (0, 4, 0), "silu_ready": (0, 4 + 2, 0), "rot_raw": (0, 4, 0),
    "logterm_ready": (0, 1 + 4, 0), "rows_ready": (0, 1, 0), "masked_ready": (0, 4, 0), "decay_ready": (0, 8, 0),
    "qk_ready": (0, 16, 0), "scores_taken": (1, 16, 0), "softplus_ready": (0, 4, 0), "suffix_ready": (0, 4, 0),
    "strict_ready": (0, 4, 0), "negmax_ready": (0, 4, 0), "exp_ready": (0, 4, 0), "probs_ready": (0, 4, 0),
    "ptrans_ready": (1, 4, 0), "ptrans_copied": (0, 4, 0),
    "pv_ready": (1, 16, 0), "den_ready": (0, 2, 0), "out_scaled": (0, 4, 0),
    "branch_hi_ready": (0, 8, 0), "branch_ready": (1, 8, 0), "gate_ready": (0, 6, 0),
    "merged_tile": (0, 8, 0), "merged_hi_ready": (0, 8, 0), "merged_ready": (0, 8, 0),
    "relu_ready": (0, 0, 8), "hidden_hi_ready": (0, 0, 8), "hidden_ready": (0, 0, 8),
    "columns_loaded": (16 * 10, 0, 0), "vectors_loaded": (16 * 6, 0, 0), "x_landed": (64, 0, 0),
    "table_order": (TABLE_STEPS, 0, 0), "consts_ready": (1, 0, 0), "c_tanh": (1, 0, 0),
    "angles_ready": (1, 0, 0), "sines_ready": (5, 0, 0), "pool_order": (22, 0, 0),
    "stored": (0, 0, 0), "xt_ready": (0, 0, 0), "xt_taken": (0, 0, 0),
    "act_order": (1, 88, 0), "dve_order": (23, 254, 15),
}

VECTORS = COUNTS["vectors_loaded"][0]
COLUMNS = COUNTS["columns_loaded"][0]
TILES_BEFORE = [TILE_NO[(b, 0)] for b in range(PRE_BLOCKS)] + [PRE_TILES]


def at(name, n, layer=None, quarter=None):
    before, pre, per_quarter = COUNTS[name]
    if layer is None:
        return n
    if quarter is None:
        return layer * (pre + QUARTERS * per_quarter) + (before + n)
    return layer * (pre + QUARTERS * per_quarter) + quarter * per_quarter + (before + pre + n)


def after_layers(name, n=0):
    before, pre, per_quarter = COUNTS[name]
    return before + LAYERS * (pre + QUARTERS * per_quarter) + n


class Program:

    def __init__(self, engine, sems, order=None):
        self.engine, self.sems, self.order = engine, sems, order
        self.layer = self.quarter = self.last = None
        self.n = {}
        self.seen = {}
        self.tail = False

    def enter(self, layer=None, quarter=None):
        self.layer, self.quarter, self.n = layer, quarter, {}
        if self.order:
            self.last = (self.sems[self.order], at(self.order, 0, layer, quarter))

    def leave(self, region):
        self.seen[region] = dict(self.n)

    def value(self, name, n):
        return after_layers(name, n) if self.tail else at(name, n, self.layer, self.quarter)

    def count(self, name=None, n=None, by=1):
        name = name or self.order
        self.n[name] = self.n.get(name, 0) + by
        self.last = (self.sems[name], self.value(name, self.n[name] if n is None else n))
        return self.sems[name], by


def trunk(nc, x, c, positions, w_ada, b_ada, norm_g, w_in, conv_w, conv_b, gate_b, ret_g, q_g, k_g, sinks,
          rel_bias, w_up, w_out, w_ff1, w_ff2, rope_freq, out):
    with ExitStack() as ctx:
        def sb(name, cols, dtype=F32):
            return ctx.enter_context(nc.sbuf_tensor(name, [P, cols], dtype))

        sems = {name: ctx.enter_context(nc.semaphore(name)) for name in COUNTS}

        gemm = [ctx.enter_context(nc.psum_tensor(f"gemm{i}", [P, T], F32)) for i in range(2)]
        score = [ctx.enter_context(nc.psum_tensor(f"score{i}", [P, T], F32)) for i in range(3)]
        outp = ctx.enter_context(nc.psum_tensor("outp", [P, T], F32))
        denp = ctx.enter_context(nc.psum_tensor("denp", [P, T], F32))
        aux = ctx.enter_context(nc.psum_tensor("aux", [P, T], F32))

        with nc.sbuf_tensor("gates", [P, 8 * T], F32) as gates, nc.sbuf_tensor("merged", [P, 8 * T], F32) as merged:
            pass
        hid_hi = sb("hid_hi", 8 * T, F32R)
        hid_lo = sb("hid_lo", 8 * T, F32R)
        xt = sb("xt", KT * T)
        h_hi, h_lo = sb("h_hi", KT * T, F32R), sb("h_lo", KT * T, F32R)
        w_raw = [sb(f"w_raw{i}", KT * BC) for i in range(2)]
        w_hi = [sb(f"w_hi{i}", KT * BC, F32R) for i in range(2)]
        w_lo = [sb(f"w_lo{i}", KT * BC, F32R) for i in range(2)]
        ada_raw = sb("ada_raw", KT * BC)
        ada_acc = sb("ada_acc", BC)
        br_hi, br_lo = sb("br_hi", 2 * T, F32R), sb("br_lo", 2 * T, F32R)
        feat = [sb(f"feat{i}", T) for i in range(6)]
        vt = sb("vt", NCH * VC)
        bias = sb("bias", HEADS * NCH * 256)
        cos, sin, age = sb("cos", T), sb("sin", T), sb("age", T)
        wrk, prb = sb("wrk", 1280), sb("prb", 1280)
        tmp = sb("tmp", 2 * T)
        ident, neg_tri, neg_ones, ones, block_ones = (
            sb(n, P) for n in ("ident", "neg_tri", "neg_ones", "ones", "block_ones"))
        mask_incl, mask_strict = sb("mask_incl", P), sb("mask_strict", P)
        sel = sb("sel", HEADS * P)
        sel_pair = sb("sel_pair", 2 * P)
        cols_a, cols_b = sb("cols_a", P), sb("cols_b", 56)
        c_act = sb("c_act", 8)
        gb, gb_cur = sb("gb", 4), sb("gb_cur", 2)
        sink_all, sink_cur = sb("sink_all", LAYERS * HEADS), sb("sink_cur", HEADS)
        mod = [sb("mod1", 24), sb("mod2", 24)]
        b_cur, g_cur, acol = sb("b_cur", 2 * ADA_REST), sb("g_cur", 16), sb("acol", 8)
        cw_cur, cb_cur, rg_cur, qk_cur = sb("cw_cur", 16), sb("cb_cur", 4), sb("rg_cur", 2), sb("qk_cur", 2)
        gcol = sb("gcol", NCH * HEADS)
        stat = sb("stat", 5 * NCH)
        started = sb("started", len(STARTED))

        ada_ring = (ada_raw[:, :], gates[:, 0:KT * BC], gates[:, KT * BC:2 * KT * BC])
        ada_ring_landed = ("ada_landed", "ada_landed_b", "ada_landed_c")
        ada_banks = (score[0], score[1], score[2], outp)
        ada_rows = (wrk[0:1, 0:T], merged[0:1, T:2 * T], prb[0:1, 0:T], merged[0:1, 0:T])
        tmps = [tmp[:, 0:T], tmp[:, T:2 * T]]
        square_sum = wrk[:, T:2 * T]
        later_sum = prb[:, 0:3 * CH]
        x_rows = merged
        x_out = [merged[:, m * D:(m + 1) * D] for m in range(NCH)]
        own_mask = prb[:, 512:512 + P]
        vec_a, vec_b = tmp[:, 0:P], tmp[:, P:2 * P]
        row_i, row_f, row_t, row_a, row_m, row_am = (merged[0:HEADS, n * T:(n + 1) * T] for n in range(6))
        row_one = merged[0:HEADS, 6 * T:7 * T]
        row_if = merged[0:2 * HEADS, 7 * T:8 * T]

        def xk(k):
            return xt[:, k * T:(k + 1) * T]

        def part(t, k):
            return t[:, k * T:(k + 1) * T]

        def gate_tile(k):
            return gates[:, k * T:(k + 1) * T]

        def w_src(block, layer):
            name = block[0]
            ly = bass.ds(layer, 1)
            if name == "up":
                return w_up[ly, block[1]].rearrange("o (k p) n -> p (o k) n", p=P)
            if name == "out":
                return w_out[ly, :, block[1] * BC:(block[1] + 1) * BC].rearrange("o (k p) n -> p (o k) n", p=P)
            c0 = COLS[name] + (block[1] * D + block[2] * BC if name == "gate" else 0)
            n = P if name == "m_if" else BC
            return w_in[ly, :, c0:c0 + n].rearrange("o (k p) n -> p (o k) n", p=P)

        def w_view(t, block):
            if block[0] == "up":
                return t[:, :].rearrange("p (k n) -> p k n", k=2)
            if block[0] == "m_if":
                return t[:, 0:KT * P].rearrange("p (k n) -> p k n", k=KT)
            return t[:, :].rearrange("p (k n) -> p k n", k=KT)

        def w_flat(t, block):
            return t[:, 0:KT * P] if block[0] == "m_if" else t[:, :]

        def k_cols(h):
            return feat[2 + h // 2]

        def v_cols(j, h):
            c0 = j * VC + (0, 2, 3, 5)[h] * HD
            return slice(c0, c0 + HD)

        def v_out(i0, i1, pair):
            c = vt[:, i0 * VC:i1 * VC].rearrange("p (i a x d) -> p i a x d", a=2, x=3, d=HD)
            return c[:, :, pair, 0:3:2, :]

        def rows(h):
            r = HD * (h % 2)
            return slice(r, r + HD)

        FF = [("ff1", j) for j in range(4)] + [("ff2", j) for j in range(4)]
        programs = []
        block = ctx.enter_context(nc.Block())

        @block.sync
        def _(sp):
            p = Program(sp, sems)
            programs.append(("sp", p))
            p.enter()

            def small(dst, src, scattered=False, name="vectors_loaded"):
                sp.dma_start(dst, src, allow_slow_non_contiguous=scattered).then_inc(*p.count(name, by=16))

            def column(dst, src):
                small(dst, src, name="columns_loaded")

            column(vec_a[0:96, :], b_ada.rearrange("l j (c p) -> (l j c) p", p=P))
            column(vec_a[96:128, :], norm_g.rearrange("l j (c p) -> (l j c) p", p=P))
            column(vec_b[0:32, :], conv_w.rearrange("l k (m p) -> (l k m) p", p=P))
            column(vec_b[32:40, :], conv_b.rearrange("l (m p) -> (l m) p", p=P))
            column(vec_b[40:44, :], ret_g.rearrange("l (m p) -> (l m) p", p=P))
            column(vec_b[44:52, :], c.rearrange("b (m p) -> (b m) p", p=P))
            for half in range(2):
                column(vec_b[52:54, half * HD:(half + 1) * HD], q_g)
                column(vec_b[54:56, half * HD:(half + 1) * HD], k_g)
            for m in range(NCH):
                sp.dma_start(x_rows[:, m * D:(m + 1) * D], x[0, m * P:(m + 1) * P, :]).then_inc(sems["x_landed"], 16)
            small(gb[0:HEADS, :], gate_b.rearrange("l j h -> h (l j)"), True)
            small(sink_all[:, :], sinks.rearrange("l h -> (l h)").partition_broadcast(P))
            small(wrk[:, 0:T].bitcast(I32), positions.rearrange("b t -> (b t)").partition_broadcast(P))
            small(wrk[:, 1024:1028].bitcast(I32), positions.rearrange("b (i p) -> p (b i)", p=P), True)
            small(prb[:, 1024:1152], rel_bias.rearrange("b h -> (b h)").partition_broadcast(P))
            small(prb[:, 1184:1185], rope_freq)

            def load_ada(src, u):
                sp.wait_ge(sems["ada_partial"], p.value("ada_partial", u))
                if p.quarter is None and u == 0:
                    sp.wait_ge(sems["aux_ready"], 3)
                sp.dma_start(ada_raw[:, :].rearrange("p (k n) -> p k n", k=KT), src).then_inc(*p.count("ada_landed", by=16))

            def load_block(b, src, blk):
                s = b % 2
                sp.wait_ge(sems[f"lo_ready{s}"], p.value(f"lo_ready{s}", b // 2))
                sp.dma_start(w_view(w_raw[s], blk), src).then_inc(*p.count(f"raw_landed{s}", by=16))

            for u in range(ADA_FIRST):
                if u >= 3:
                    sp.wait_ge(sems["ada_used"], u - 2)
                sp.dma_start(ada_ring[u % 3].rearrange("p (k n) -> p k n", k=KT),
                             w_ada[0, 0, :, u * BC:(u + 1) * BC].rearrange("(k p) n -> p k n", p=P)).then_inc(
                    *p.count(ada_ring_landed[u % 3], by=16))
            p.leave("before")
            with sp.Fori(0, LAYERS) as layer:
                p.enter(layer)
                for b, blk in enumerate(BLOCKS):
                    if b - 2 in ADA_BLOCK:
                        u = ADA_BLOCK.index(b - 2)
                        j, c0 = divmod(2 * D + u * BC, 3 * D)
                        load_ada(w_ada[bass.ds(layer, 1), j, :, c0:c0 + BC].rearrange("o (k p) n -> p (o k) n", p=P), u)
                    load_block(b, w_src(blk, layer), blk)
                p.leave("layer")
                with sp.Fori(0, QUARTERS) as q:
                    p.enter(layer, q)
                    for b, blk in enumerate(FF):
                        if b - 2 in FF_ADA:
                            load_ada(w_ada[1, 0, :, bass.ds(q * (2 * BC) + FF_ADA[b - 2] * BC, BC)].rearrange(
                                "(k p) n -> p k n", p=P), FF_ADA[b - 2])
                        ly = bass.ds(layer, 1)
                        if blk[0] == "ff1":
                            src = w_ff1[ly, :, bass.ds(q * D + blk[1] * BC, BC)]
                        else:
                            src = w_ff2[ly, bass.ds(q * D, D), blk[1] * BC:(blk[1] + 1) * BC]
                        load_block(b, src.rearrange("o (k p) n -> p (o k) n", p=P), blk)
                    p.leave("quarter")
            sp.wait_ge(sems["lo_ready0"], after_layers("lo_ready0"))
            sp.dma_start(w_raw[0][:, 0:1], rope_freq).then_inc(sems["raw_landed0"], 16)
            for m in range(NCH):
                sp.wait_ge(sems["xt_taken"], 2 * (m + 1))
                sp.dma_start(out[0, m * P:(m + 1) * P, :], x_out[m]).then_inc(sems["stored"], 16)
            sp.wait_ge(sems["stored"], 16 * NCH)

        @block.gpsimd
        def _(pool):
            p = Program(pool, sems, "pool_order")
            programs.append(("pool", p))
            g = nc.gpsimd
            p.enter()

            def keep(t, op, fill, base, pattern, mult):
                pool.wait_ge(*p.last)
                g.affine_select(out=t, in_=t, compare_op=op, fill=fill, base=base, pattern=pattern,
                                channel_multiplier=mult).then_inc(*p.count())

            g.memset(ident[:, :], 1.0).then_inc(*p.count())
            g.memset(neg_tri[:, :], -1.0).then_inc(*p.count())
            g.memset(neg_ones[:, :], -1.0).then_inc(*p.count())
            g.memset(ones[:, :], 1.0).then_inc(*p.count())
            v_ones = vt[:, :].rearrange("p (i x d) -> p i x d", i=2 * NCH, x=3)
            g.memset(v_ones[:, :, 1, :], 1.0).then_inc(*p.count())
            g.memset(block_ones[:, :], 0.0).then_inc(*p.count())
            g.memset(mask_incl[:, :], 0.0).then_inc(*p.count())
            g.memset(mask_strict[:, :], 0.0).then_inc(*p.count())
            g.memset(sel[0:HEADS, :], 1.0).then_inc(*p.count())
            g.memset(sel_pair[0:HEADS, :], 1.0).then_inc(*p.count())
            g.iota(age[:, :], pattern=[[1, T]], base=0, channel_multiplier=-1,
               allow_small_or_imprecise_dtypes=True).then_inc(*p.count())
            pool.wait_ge(*p.last)
            g.memset(block_ones[0:HD, 0:HD], 1.0).then_inc(*p.count())
            g.memset(block_ones[HD:P, HD:P], 1.0).then_inc(*p.count())
            keep(ident[:, :], ALU.is_equal, 0.0, 0, [[-1, P]], 1)
            keep(neg_tri[:, :], ALU.is_ge, 0.0, 0, [[-1, P]], 1)
            keep(mask_incl[:, :], ALU.is_ge, -BIG, 0, [[1, P]], -1)
            keep(mask_strict[:, :], ALU.is_gt, -BIG, 0, [[1, P]], -1)
            keep(sel[0:HEADS, :].rearrange("p (h n) -> p h n", h=HEADS), ALU.is_equal, 0.0, 0,
                 [[-1, HEADS], [0, P]], 1)
            keep(sel_pair[0:HEADS, :].rearrange("p (a b n) -> p a b n", a=2, b=2), ALU.is_equal, 0.0, 0,
                 [[-2, 2], [-1, 2], [0, HD]], 1)
            keep(age[:, :], ALU.is_ge, 1.0e6, 0, [[1, T]], -1)
            pool.wait_ge(*p.last)
            g.memset(own_mask, 1.0).then_inc(*p.count())
            keep(own_mask, ALU.is_ge, 0.0, 0, [[-1, P]], 1)
            pool.wait_ge(*p.last)
            g.memset(c_act[:, :], 0.0).then_inc(*p.count("consts_ready"))
            for n, name in enumerate(STARTED):
                g.memset(started[:, n:n + 1], 0.0).then_inc(sems[name], 1)
            p.leave("before")

            def lo_part(b, blk):
                s = b % 2
                pool.wait_ge(sems[f"hi_ready{s}"], p.value(f"hi_ready{s}", b // 2 + 1))
                g.tensor_tensor(w_flat(w_lo[s], blk), w_flat(w_raw[s], blk),
                                w_flat(w_hi[s], blk).bitcast(F32), ALU.subtract).then_inc(*p.count(f"lo_ready{s}"))

            with pool.Fori(0, LAYERS) as layer:
                p.enter(layer)
                for b, blk in enumerate(BLOCKS):
                    lo_part(b, blk)
                p.leave("layer")
                with pool.Fori(0, QUARTERS) as q:
                    p.enter(layer, q)
                    for b, blk in enumerate(FF):
                        lo_part(b, blk)
                    p.leave("quarter")

        @block.tensor
        def _(pe):
            p = Program(pe, sems)
            programs.append(("pe", p))
            mm = nc.tensor.matmul

            def wait_bank(tile):
                pe.wait_ge(sems[f"bank_taken{tile % 2}"], p.value(f"bank_taken{tile % 2}", tile // 2))

            def tile_done(ins, tile):
                ins.then_inc(*p.count(f"bank_ready{tile % 2}"))

            def aux_free(n):
                pe.wait_ge(sems["aux_taken"], p.value("aux_taken", n))

            def three(o, wh, wl, xh, xl, first, last):
                mm(o, wh, xh, start=first, stop=False, skip_group_check=True)
                mm(o, wh, xl, start=False, stop=False, skip_group_check=True)
                return mm(o, wl, xh, start=False, stop=last, skip_group_check=True)

            def feature_tile(b, half, tile, rhs, wait_k=None, kn=KT, blk=("x",)):
                s = b % 2
                wh, wl = w_view(w_hi[s], blk), w_view(w_lo[s], blk)
                cs = slice(half * P, (half + 1) * P)
                wait_bank(tile)
                for k in range(kn):
                    if wait_k is not None:
                        wait_k(k)
                    last = three(gemm[tile % 2][:, :], wh[:, k, cs], wl[:, k, cs], part(rhs[0], k), part(rhs[1], k),
                                 k == 0, k == kn - 1)
                return last

            def feature_pair(b, tile, wait_k):
                s = b % 2
                wh, wl = w_view(w_hi[s], ("x",)), w_view(w_lo[s], ("x",))
                for step_k in range(KT + LAG):
                    for half in range(2):
                        k = step_k - half * LAG
                        if not 0 <= k < KT:
                            continue
                        if k == 0:
                            wait_bank(tile + half)
                        if half == 0:
                            wait_k(k)
                        cs = slice(half * P, (half + 1) * P)
                        ins = three(gemm[(tile + half) % 2][:, :], wh[:, k, cs], wl[:, k, cs], part(h_hi, k),
                                    part(h_lo, k), k == 0, k == KT - 1)
                        if k == KT - 1:
                            tile_done(ins, tile + half)

            def token_tile(b, half, tile, blk, chunks, cs):
                s = b % 2
                wh, wl = w_view(w_hi[s], blk), w_view(w_lo[s], blk)
                n = cs.stop - cs.start
                wait_bank(tile)
                for i, ch in enumerate(chunks):
                    for k in range(KT):
                        t0 = k * T + ch * CH
                        last = three(gemm[tile % 2][:, i * n:(i + 1) * n], h_hi[:, t0:t0 + CH], h_lo[:, t0:t0 + CH],
                                     wh[:, k, cs], wl[:, k, cs], k == 0, k == KT - 1)
                return last

            p.enter()
            pe.wait_ge(sems["consts_ready"], 1)
            pe.wait_ge(sems["columns_loaded"], COLUMNS)
            nc.tensor.transpose(aux[:, 0:P], vec_a, ident[:, :]).then_inc(*p.count("aux_ready"))
            pe.wait_ge(sems["aux_taken"], p.value("aux_taken", 1))
            mm(aux[:, 0:56], vec_b[0:56, :], ident[0:56, 0:56], start=True, stop=True).then_inc(*p.count("aux_ready"))
            pe.wait_ge(sems["x_landed"], 16 * NCH)
            for k in range(KT):
                if k >= 2:
                    wait_bank(k)
                for m in range(NCH):
                    ins = nc.tensor.transpose(gemm[k % 2][:, m * P:(m + 1) * P],
                                              x_rows[:, m * D + k * P:m * D + (k + 1) * P], ident[:, :])
                tile_done(ins, k)

            def ada_sum(u, n_aux):
                aux_free(n_aux)
                pe.wait_ge(sems["ada_partial"], p.value("ada_partial", u + 1))
                for col in range(2):
                    ins = mm(aux[:, col:col + 1], ada_acc[:, col * P:(col + 1) * P], ones[:, 0:1], start=True, stop=True)
                ins.then_inc(*p.count("aux_ready"))

            pe.wait_ge(sems["c_act_ready"], 1)
            for u in range(ADA_FIRST):
                pe.wait_ge(sems[ada_ring_landed[u % 3]], 16 * (u // 3 + 1))
                for k in range(KT):
                    ins = mm(ada_banks[u // 2][0:1, (u % 2) * BC:(u % 2 + 1) * BC], c_act[:, k:k + 1],
                             ada_ring[u % 3][:, k * BC:(k + 1) * BC], start=(k == 0), stop=(k == KT - 1))
                ins.then_inc(*p.count("ada_used"))
            aux_free(2)
            pe.wait_ge(sems["ada_row_ready"], ADA_FIRST // 2)
            for col in range(2 * ADA_FIRST):
                row = ada_rows[col // 4]
                ins = mm(aux[:, col:col + 1], row[:, (col % 4) * P:(col % 4 + 1) * P], ones[0:1, 0:1], start=True, stop=True)
            ins.then_inc(*p.count("aux_ready"))
            p.leave("before")

            def scores_triangle(h, first):
                r = rows(h)
                for j in (0, 1, 3, 2):
                    o = score[SC_BANK[j]][:, SC_COL[j]:SC_COL[j] + LEN[j]]
                    ins = mm(o, k_cols(h)[r, j * CH:(j + 1) * CH], feat[h // 2][r, j * CH:T],
                             start=(j != 3), stop=not first, skip_group_check=True)
                return ins

            def pv_triangle(h):
                r = rows(h)
                for j in range(NCH):
                    ins = mm(outp[r, j * CH:T], vt[:, v_cols(j, h)],
                             prb[:, OFF[j]:OFF[j] + LEN[j]], start=(j == 0), stop=(j == NCH - 1),
                             skip_group_check=True)
                return ins

            def step(s):
                kind = s[0]
                if kind == "norm":
                    aux_free(AUX[s])
                    used, ready, n = (("square_used", "square_ready", (KT - 2, 5 + KT)) if s[1] else
                                      ("next_square_used", "next_square_ready", (0, 0)))
                    pe.wait_ge(sems[used], p.value(used, n[0]))
                    mm(aux[:, :], ones[:, :], square_sum, start=True, stop=False)
                    pe.wait_ge(sems[ready], p.value(ready, n[1]))
                    mm(aux[:, :], ones[:, :], tmps[(KT - 1) % 2], start=False, stop=True).then_inc(*p.count("aux_ready"))
                elif kind == "tile":
                    tile_step(s)
                elif kind == "gcol":
                    aux_free(AUX[s])
                    pe.wait_ge(sems["rows_ready"], p.value("rows_ready", 1))
                    for i in range(NCH):
                        ins = mm(aux[:, i * HEADS:(i + 1) * HEADS], row_i[:, i * CH:(i + 1) * CH],
                                 ident[0:HEADS, 0:HEADS], start=True, stop=True)
                    ins.then_inc(*p.count("aux_ready"))
                elif kind == "qk":
                    _, n, h = s
                    g = 4 * n + h
                    if n == 0:
                        if h == 0:
                            pe.wait_ge(sems["feature_ready"], p.value("feature_ready", 4))
                        aux_free(AUX[s])
                        mm(aux[:, :], sel[0:HEADS, h * P:(h + 1) * P], row_m, start=True, stop=True).then_inc(*p.count("aux_ready"))
                    if n == 1 and h == 0:
                        pe.wait_ge(sems["feature_ready"], p.value("feature_ready", 8))
                    if n == 3 and h == 0:
                        pe.wait_ge(sems["feature_ready"], p.value("feature_ready", 11))
                    if n == 2 and h == 0:
                        for half in range(2):
                            tl = TILE_NO[(BLOCK_NO[("s_k",)], half)]
                            pe.wait_ge(sems[f"bank_taken{tl % 2}"], p.value(f"bank_taken{tl % 2}", tl // 2 + 1))
                    pe.wait_ge(sems["scores_taken"], p.value("scores_taken", g))
                    if n < 3:
                        scores_triangle(h, n == 2).then_inc(*p.count("qk_ready"))
                    else:
                        r, kd = rows(h), feat[3 + h // 2]
                        for i in range(NCH):
                            q = feat[h // 2][r, i * CH:(i + 1) * CH]
                            o = score[i // 2][:, (i % 2) * 256:(i % 2) * 256 + 256]
                            if i == 0:
                                mm(o[:, 0:CH], q, kd[r, CH:2 * CH], start=True, stop=True)
                                ins = mm(o[:, CH:256], q, kd[r, 0:CH], start=True, stop=True)
                            else:
                                ins = mm(o, q, kd[r, (i - 1) * CH:(i + 1) * CH], start=True, stop=True)
                        ins.then_inc(*p.count("qk_ready"))
                elif kind == "suffix":
                    h = s[1]
                    pe.wait_ge(sems["softplus_ready"], p.value("softplus_ready", h + 1))
                    for j in range(NCH):
                        mm(score[SC_BANK[j]][:, SC_COL[j]:SC_COL[j] + LEN[j]], neg_tri[:, :],
                           wrk[:, OFF[j]:OFF[j] + LEN[j]], start=False, stop=False, skip_group_check=True)
                    later = {0: ((1, wrk[:, OFF[1]:OFF[1] + CH]), (2, later_sum[:, CH:3 * CH])),
                             1: ((1, wrk[:, OFF[2]:OFF[2] + CH]), (2, later_sum[:, 0:CH])),
                             2: ((1, wrk[:, OFF[3]:OFF[3] + CH]),)}
                    for j in range(NCH - 1):
                        for chunk, keys in later[j]:
                            c0, n = SC_COL[j] + chunk * CH, keys.shape[1]
                            last = mm(score[SC_BANK[j]][:, c0:c0 + n], neg_ones[:, :], keys, start=False, stop=True,
                                      skip_group_check=True)
                    last.then_inc(*p.count("suffix_ready"))
                elif kind == "ptrans":
                    h = s[1]
                    pe.wait_ge(sems["probs_ready"], p.value("probs_ready", h + 1))
                    if h >= 1:
                        pe.wait_ge(sems["ptrans_copied"], p.value("ptrans_copied", h))
                    for n, (i, half) in enumerate(PT_BLOCKS):
                        dst = (score[2] if n < 4 else denp)[:, (n % 4) * CH:(n % 4 + 1) * CH]
                        c0 = i * 256 + half * CH
                        ins = nc.tensor.transpose(dst, prb[:, c0:c0 + CH], ident[:, :])
                    ins.then_inc(*p.count("ptrans_ready"))
                elif kind == "pv":
                    _, n, h = s
                    g = 4 * n + h
                    r = rows(h)
                    if h % 2 == 0:
                        pe.wait_ge(sems["branch_ready"], p.value("branch_ready", 2 * n + h // 2))
                    if h == 0 and n == 3:
                        pe.wait_ge(sems["aux_taken"], p.value("aux_taken", AUX[("vtrans",)] + 1))
                    elif h == 0:
                        for half in range(2):
                            tl = TILE_NO[(BLOCK_NO[(("m_v", "r_v", "s_v")[n],)], half)]
                            pe.wait_ge(sems[f"bank_taken{tl % 2}"], p.value(f"bank_taken{tl % 2}", tl // 2 + 1))
                    if n < 3:
                        pe.wait_ge(sems["scores_taken"], p.value("scores_taken", g + 1))
                        if n == 0:
                            for j in range(NCH):
                                c0 = j * VC + (0, 1, 3, 4)[h] * HD
                                ins = mm((outp, denp)[h % 2][:, j * CH:T], vt[:, c0:c0 + P], prb[:, OFF[j]:OFF[j] + LEN[j]],
                                         start=(j == 0), stop=(j == NCH - 1), skip_group_check=True)
                        else:
                            ins = pv_triangle(h)
                        ins.then_inc(*p.count("pv_ready"))
                    else:
                        pe.wait_ge(sems["ptrans_copied"], p.value("ptrans_copied", h + 1))
                        for m, (i, half) in enumerate(PT_BLOCKS):
                            ins = mm(outp[r, i * CH:(i + 1) * CH], vt[:, v_cols(i - 1 + half, h // 2)], tmp[:, m * CH:(m + 1) * CH],
                                     start=(half == 0 or i == 0), stop=(half == 1), skip_group_check=True)
                        ins.then_inc(*p.count("pv_ready"))
                elif kind == "divide":
                    aux_free(AUX[s])
                    mm(aux[:, :], sel_pair[0:HEADS, s[1] * P:(s[1] + 1) * P], row_am,
                       start=True, stop=True).then_inc(*p.count("aux_ready"))
                elif kind == "vtrans":
                    tl = TILE_NO[(BLOCK_NO[("a_kv",)], 1)]
                    pe.wait_ge(sems[f"bank_taken{tl % 2}"], p.value(f"bank_taken{tl % 2}", tl // 2 + 1))
                    aux_free(AUX[s])
                    for i in range(NCH):
                        ins = nc.tensor.transpose(aux[:, i * CH:(i + 1) * CH], wrk[:, i * CH:(i + 1) * CH], ident[:, :])
                    ins.then_inc(*p.count("aux_ready"))
                elif kind in ("hnorm", "anorm"):
                    i = s[1]
                    aux_free(AUX[s])
                    pe.wait_ge(sems["square_ready"], p.value("square_ready", (i + 1 if kind == "hnorm" else 3 + i)))
                    t = tmps[0] if kind == "hnorm" else tmps[i % 2]
                    mm(aux[:, :], block_ones[:, :], t, start=True, stop=True).then_inc(*p.count("aux_ready"))
                elif kind == "adasum":
                    ada_sum(s[1], AUX[s])

            def tile_step(s):
                _, b, half = s
                blk = BLOCKS[b]
                name = blk[0]
                tile = TILE_NO[(b, half)]
                sl = b % 2
                if half == 0:
                    pe.wait_ge(sems[f"lo_ready{sl}"], p.value(f"lo_ready{sl}", b // 2 + 1))
                if name in ("m_v", "r_v", "s_v"):
                    ins = token_tile(b, half, tile, blk, (2 * half, 2 * half + 1), slice(0, BC))
                elif name == "m_if" and half == 0:
                    ins = feature_tile(b, half, tile, (h_hi, h_lo), blk=blk)
                elif name == "m_if":
                    wait_bank(tile)
                    pe.wait_ge(sems[f"bank_taken{(tile - 1) % 2}"], p.value(f"bank_taken{(tile - 1) % 2}", (tile - 1) // 2 + 1))
                    ins = mm(gemm[tile % 2][0:P - HEADS, :], ident[0:2 * HEADS, HEADS:P], row_if, start=True, stop=True)
                elif name == "up":
                    if half == 0:
                        pe.wait_ge(sems["branch_ready"], p.value("branch_ready", 2 * blk[1] + 2))
                    ins = feature_tile(b, half, tile, (br_hi, br_lo), kn=2, blk=blk)
                elif blk == ("out", 0) and half == 0:
                    ins = feature_tile(b, half, tile, (h_hi, h_lo), lambda k: pe.wait_ge(sems["merged_ready"], p.value("merged_ready", k + 1)))
                elif name == "m_q":
                    if half == 0:
                        feature_pair(b, tile, lambda k: pe.wait_ge(sems["h_ready"], p.value("h_ready", k + 1)))
                    return
                else:
                    ins = feature_tile(b, half, tile, (h_hi, h_lo))
                tile_done(ins, tile)

            with pe.Fori(0, LAYERS) as layer:
                p.enter(layer)
                for s in STEPS:
                    step(s)
                p.leave("layer")
                with pe.Fori(0, QUARTERS) as q:
                    p.enter(layer, q)
                    for b, blk in enumerate(FF):
                        pe.wait_ge(sems[f"lo_ready{b % 2}"], p.value(f"lo_ready{b % 2}", b // 2 + 1))
                        if b == 0:
                            feature_pair(b, 0, lambda k: pe.wait_ge(sems["h_ready"], at("h_ready", KT + k + 1, layer)))
                            continue
                        for half in range(2):
                            tile = 2 * b + half
                            if blk[0] == "ff1":
                                ins = feature_tile(b, half, tile, (h_hi, h_lo))
                            else:
                                first = lambda k: pe.wait_ge(sems["hidden_ready"], p.value("hidden_ready", k + 1))
                                ins = feature_tile(b, half, tile, (hid_hi, hid_lo), first if tile == 8 else None)
                            tile_done(ins, tile)
                            if half == 0 and b in FF_ADASUM:
                                u = FF_ADASUM[b]
                                ada_sum(u, u)
                    p.leave("quarter")

            p.tail = True
            for m in range(NCH):
                for half in range(2):
                    n = 2 * m + half
                    if n == 0:
                        for b2 in range(2):
                            pe.wait_ge(sems[f"bank_taken{b2}"], after_layers(f"bank_taken{b2}"))
                    if n >= 2:
                        pe.wait_ge(sems["xt_taken"], n - 1)
                    for k in range(4):
                        kk = 4 * half + k
                        ins = nc.tensor.transpose(gemm[n % 2][:, k * P:(k + 1) * P],
                                                  xt[:, kk * T + m * P:kk * T + (m + 1) * P], ident[:, :])
                    ins.then_inc(sems["xt_ready"], 1)

        @block.scalar
        def _(act):
            p = Program(act, sems, "act_order")
            programs.append(("act", p))
            a = nc.scalar.activation

            def hi_part(b, blk, tiles_through):
                s = b % 2
                act.wait_ge(sems[f"raw_landed{s}"], p.value(f"raw_landed{s}", 16 * (b // 2 + 1)))
                if tiles_through is not None:
                    act.wait_ge(sems["bank_ready1"], p.value("bank_ready1", tiles_through // 2))
                nc.scalar.copy(w_flat(w_hi[s], blk), w_flat(w_raw[s], blk)).then_inc(*p.count(f"hi_ready{s}", n=b // 2 + 1))

            def rstd(n, scale, dst):
                act.wait_ge(sems["aux_ready"], p.value("aux_ready", n + 1))
                a(dst, aux[:, :], ACT.Ln, scale=scale, bias=EPS).then_inc(*p.count("aux_taken", n=n + 1))
                act.wait_ge(*p.last)
                a(dst, dst, ACT.Exp, scale=-0.5).then_inc(*p.count("rstd_ready"))

            def branch_hi(n, pair, src, scale):
                if n >= 1 and pair == 0:
                    up = TILE_NO[(BLOCK_NO[("up", n - 1)], 7)]
                    act.wait_ge(sems[f"bank_ready{up % 2}"], p.value(f"bank_ready{up % 2}", up // 2 + 1))
                nc.scalar.mul(part(br_hi, pair), src, scale).then_inc(*p.count("branch_hi_ready"))

            def next_square(k):
                if k >= 2:
                    act.wait_ge(sems["next_square_used"], ahead.value("next_square_used", max(k - 2, 1)))
                a(tmps[k % 2], xk(k), ACT.Square).then_inc(*ahead.count("next_square_ready"))

            ahead = Program(act, sems)
            programs.append(("act ahead", ahead))
            ahead.enter()
            p.enter()
            act.wait_ge(sems["aux_taken"], p.value("aux_taken", 2))
            a(stat[:, 0:8], cols_b[:, 44:52], ACT.Tanh, scale=0.5).then_inc(*p.count("c_tanh"))
            for k in range(KT):
                act.wait_ge(sems[f"bank_ready{k % 2}"], p.value(f"bank_ready{k % 2}", k // 2 + 1))
                nc.scalar.copy(xk(k), gemm[k % 2][:, :]).then_inc(*p.count(f"bank_taken{k % 2}"))
            act.wait_ge(sems["angles_ready"], p.value("angles_ready", 1))
            for r in range(4):
                h = slice(r * HD // 2, (r + 1) * HD // 2)
                a(sin[h, :], feat[0][h, :], ACT.Sin, scale=(1.0 if r % 2 else -1.0)).then_inc(*p.count("sines_ready"))
            a(cos[:, :], feat[1][:, :], ACT.Sin).then_inc(*p.count("sines_ready"))
            for n in range(ADA_FIRST // 2):
                if n == ADA_FIRST // 2 - 1:
                    hi_part(0, BLOCKS[0], None)
                act.wait_ge(sems["ada_used"], 2 * (n + 1))
                nc.scalar.copy(ada_rows[n], ada_banks[n][0:1, :]).then_inc(*p.count("ada_row_ready"))
            act.wait_ge(sems["bank_taken0"], KT // 2)
            act.wait_ge(sems["bank_taken1"], KT // 2)
            for k in range(KT):
                next_square(k)
            p.leave("before")
            ahead.leave("before")

            def step(s):
                kind = s[0]
                if kind in ("norm", "square", "gate_tanh", "ifrows", "qk", "divide", "suffix", "ptrans", "hnorm",
                            "anorm") or (kind == "pv" and s[2] % 2 == 1 and s[1] > 0):
                    act.wait_ge(*p.last)
                if kind in ("norm", "square"):
                    j = 1 if kind == "square" else s[1]
                    if kind == "square" and s[1] == 0 or j == 0:
                        a(stat[:, 18:19], ones[:, 0:1], ACT.Ln).then_inc(*p.count())
                    for k in ([s[1]] if kind == "square" else [KT - 1] if j else []):
                        tl = TILE_NO[(BLOCK_NO[("out", k // 2)], k % 2)]
                        act.wait_ge(sems[f"bank_taken{tl % 2}"], p.value(f"bank_taken{tl % 2}", tl // 2 + 1))
                        if k >= 2:
                            act.wait_ge(sems["square_used"], p.value("square_used", max(k - 2, 1)))
                        a(tmps[k % 2], xk(k), ACT.Square).then_inc(*p.count("square_ready"))
                    if kind == "square":
                        return
                    rstd(AUX[s], 1.0 / D, wrk[:, 0:T])
                    for k in range(KT):
                        act.wait_ge(sems["h_scaled"], p.value("h_scaled", j * KT + k + 1))
                        a(part(h_hi, k), part(prb, k % 2), ACT.Identity, bias=mod[j][:, k:k + 1]).then_inc(*p.count("h_hi_ready"))
                elif kind == "tile":
                    tile_step(s)
                elif kind == "round":
                    b = s[1]
                    if b <= PRE_BLOCKS:
                        hi_part(b, BLOCKS[b] if b < PRE_BLOCKS else FF[0], TILES_BEFORE[b - 1])
                elif kind == "gate_tanh":
                    _, n, first, end = s
                    for half in range(2):
                        tl = TILE_NO[(BLOCK_NO[("gate", n, end // 2 - 1)], half)]
                        act.wait_ge(sems[f"bank_taken{tl % 2}"], p.value(f"bank_taken{tl % 2}", tl // 2 + 1))
                    g = gates[:, first * T:end * T]
                    a(g, g, ACT.Tanh, scale=0.5).then_inc(*p.count("gate_ready"))
                elif kind == "ifrows":
                    tl = TILE_NO[(BLOCK_NO[("m_if",)], 1)]
                    act.wait_ge(sems[f"bank_taken{tl % 2}"], p.value(f"bank_taken{tl % 2}", tl // 2 + 1))
                    a(row_t, row_f, ACT.Abs).then_inc(*p.count())
                    act.wait_ge(*p.last)
                    a(row_t, row_t, ACT.Exp, scale=-1.0).then_inc(*p.count())
                    act.wait_ge(*p.last)
                    a(row_t, row_t, ACT.Ln, bias=1.0).then_inc(*p.count("logterm_ready"))
                elif kind == "qk":
                    _, n, h = s
                    g = 4 * n + h
                    if n == 0:
                        act.wait_ge(sems["aux_ready"], p.value("aux_ready", AUX[s] + 1))
                        act.wait_ge(sems["masked_ready"], p.value("masked_ready", h + 1))
                        act.wait_ge(sems["scores_taken"], p.value("scores_taken", g))
                        for j in range(NCH - 1):
                            o = wrk[:, OFF[j] + CH:OFF[j] + LEN[j]]
                            ins = a(o, aux[:, (j + 1) * CH:T], ACT.Exp, scale=-1.0,
                                    bias=gcol[:, j * HEADS + h:j * HEADS + h + 1])
                            if j < NCH - 2:
                                ins.then_inc(*p.count())
                            else:
                                ins.then_inc(*p.count("aux_taken", n=AUX[s] + 1))
                        for j in range(NCH):
                            ins = a(wrk[:, OFF[j]:OFF[j] + CH], tmps[0][:, j * CH:(j + 1) * CH], ACT.Exp,
                                    bias=gcol[:, j * HEADS + h:j * HEADS + h + 1])
                            ins.then_inc(*p.count("decay_ready" if j == NCH - 1 else None))
                    elif n == 1:
                        act.wait_ge(sems["scores_taken"], p.value("scores_taken", g))
                        if h == 0:
                            act.wait_ge(sems["feature_ready"], p.value("feature_ready", 8))
                        a(wrk[:, 0:T], age[:, :], ACT.Exp, scale=LOG_GAMMA[h]).then_inc(*p.count("decay_ready"))
                    elif n == 2:
                        act.wait_ge(sems["strict_ready"], p.value("strict_ready", h + 1))
                        for i, (c0, w) in enumerate(((0, T), (T, T), (2 * T, 256))):
                            a(wrk[:, c0:c0 + w], score[i][:, 0:w], ACT.Abs).then_inc(*p.count())
                        act.wait_ge(*p.last)
                        a(wrk[:, :], wrk[:, :], ACT.Exp, scale=-1.0).then_inc(*p.count())
                        act.wait_ge(*p.last)
                        a(wrk[:, :], wrk[:, :], ACT.Ln, bias=1.0).then_inc(*p.count("logterm_ready"))
                    else:
                        act.wait_ge(sems["negmax_ready"], p.value("negmax_ready", h + 1))
                        act.wait_ge(sems["ptrans_ready"], p.value("ptrans_ready", h))
                        act.wait_ge(sems["pv_ready"], p.value("pv_ready", 12))
                        for i in range(NCH):
                            a(prb[:, i * 256:(i + 1) * 256], wrk[:, i * 256:(i + 1) * 256], ACT.Exp,
                              bias=stat[:, NCH + i:NCH + i + 1],
                              accum_out=stat[:, 2 * NCH + i:2 * NCH + i + 1]).then_inc(*p.count())
                        a(stat[:, 3 * NCH:4 * NCH], stat[:, NCH:2 * NCH], ACT.Exp,
                          bias=sink_cur[:, h:h + 1]).then_inc(*p.count("exp_ready"))
                elif kind == "suffix":
                    h = s[1]
                    act.wait_ge(sems["suffix_ready"], p.value("suffix_ready", h + 1))
                    act.wait_ge(sems["pv_ready"], p.value("pv_ready", 8 + h))
                    for i, (c0, w) in enumerate(((0, T), (T, T), (2 * T, 256))):
                        a(prb[:, c0:c0 + w], score[i][:, 0:w], ACT.Exp).then_inc(*p.count("scores_taken" if i == 2 else None, n=8 + h + 1 if i == 2 else None))
                elif kind == "ptrans":
                    h = s[1]
                    act.wait_ge(sems["ptrans_ready"], p.value("ptrans_ready", h + 1))
                    act.wait_ge(sems["pv_ready"], p.value("pv_ready", 12 + h))
                    nc.scalar.copy(tmp[:, 0:T], score[2][:, :]).then_inc(*p.count())
                    nc.scalar.copy(tmp[:, T:7 * CH], denp[:, 0:3 * CH]).then_inc(*p.count("ptrans_copied"))
                elif kind == "divide":
                    pair = s[1]
                    act.wait_ge(sems["aux_ready"], p.value("aux_ready", AUX[s] + 1))
                    a(tmps[1], aux[:, :], ACT.Exp, scale=-1.0).then_inc(*p.count("aux_taken", n=AUX[s] + 1))
                    a(tmps[0][0:HD, :], outp[HD:P, :], ACT.Abs).then_inc(*p.count())
                    a(tmps[0][HD:P, :], denp[0:HD, :], ACT.Abs).then_inc(*p.count("den_ready"))
                    act.wait_ge(sems["out_scaled"], p.value("out_scaled", pair + 1))
                    branch_hi(0, pair, tmps[0], 0.5)
                elif kind == "pv" and s[2] % 2 == 1 and s[1] > 0:
                    _, n, h = s
                    pair = h // 2
                    act.wait_ge(sems["pv_ready"], p.value("pv_ready", 4 * n + h + 1))
                    if n == 1:
                        a(tmps[0], outp[:, :], ACT.Square).then_inc(*p.count("square_ready"))
                    else:
                        branch_hi(n, pair, outp[:, :], 1.0)
                elif kind == "hnorm":
                    rstd(AUX[s], 1.0 / HD, tmps[1])
                    act.wait_ge(sems["out_scaled"], p.value("out_scaled", 2 + s[1] + 1))
                    branch_hi(1, s[1], tmps[0], 0.5)
                elif kind == "anorm":
                    rstd(AUX[s], 1.0 / HD, tmps[s[1] % 2])
                elif kind == "vtrans":
                    act.wait_ge(sems["aux_ready"], p.value("aux_ready", AUX[s] + 1))
                    nc.scalar.copy(v_out(0, NCH, 0), aux[:, :].rearrange("p (i b d) -> p i b d", i=NCH, b=2)).then_inc(*p.count("aux_taken", n=AUX[s] + 1))

            def tile_step(s):
                _, b, half = s
                blk = BLOCKS[b]
                name = blk[0]
                tile = TILE_NO[(b, half)]
                bank, bn = gemm[tile % 2], tile // 2 + 1
                act.wait_ge(*p.last)
                if name in ("m_q", "m_k"):
                    i = half + (2 if name == "m_k" else 0)
                    act.wait_ge(sems["conv_ready"], p.value("conv_ready", i + 1))
                    a(part(prb, i % 2), tmps[i % 2], ACT.Tanh, scale=0.5).then_inc(*p.count("silu_ready"))
                elif name == "m_o":
                    act.wait_ge(sems[f"bank_ready{tile % 2}"], p.value(f"bank_ready{tile % 2}", bn))
                    a(feat[4 + half][:, :], bank[:, :], ACT.Tanh, scale=0.5).then_inc(*p.count(f"bank_taken{tile % 2}", n=bn))
                elif name in ("m_v", "r_v", "s_v"):
                    act.wait_ge(sems[f"bank_ready{tile % 2}"], p.value(f"bank_ready{tile % 2}", bn))
                    src = bank[:, :].rearrange("p (i a b d) -> p i a b d", i=2, a=2, b=2)
                    nc.scalar.copy(v_out(2 * half, 2 * half + 2, 0), src[:, :, 0]).then_inc(*p.count())
                    nc.scalar.copy(v_out(2 * half, 2 * half + 2, 1), src[:, :, 1]).then_inc(*p.count(f"bank_taken{tile % 2}", n=bn))
                elif name == "a_kv" and half == 1:
                    act.wait_ge(sems[f"bank_ready{tile % 2}"], p.value(f"bank_ready{tile % 2}", bn))
                    nc.scalar.copy(wrk[:, 0:T], bank[:, :]).then_inc(*p.count(f"bank_taken{tile % 2}", n=bn))
                elif name in ("r_q", "r_k"):
                    i = half + (2 if name == "r_k" else 0)
                    act.wait_ge(sems[f"bank_taken{tile % 2}"], p.value(f"bank_taken{tile % 2}", bn))
                    if i < 2:
                        act.wait_ge(sems["scores_taken"], p.value("scores_taken", 4))
                    else:
                        act.wait_ge(sems["feature_ready"], p.value("feature_ready", 4 + i - 1))
                    for r in range(4):
                        src, dst = (slice(n * HD // 2, (n + 1) * HD // 2) for n in (r ^ 1, r))
                        nc.scalar.copy(part(wrk, i % 2)[dst, :], feat[i][src, :]).then_inc(*p.count("rot_raw" if r == 3 else None))
                elif name == "r_g":
                    act.wait_ge(sems[f"bank_ready{tile % 2}"], p.value(f"bank_ready{tile % 2}", bn))
                    a(tmps[half], bank[:, :], ACT.Tanh, scale=0.5).then_inc(*p.count("silu_ready"))
                elif name == "a_q" or (name == "a_kv" and half == 0):
                    i = half + (2 if name == "a_kv" else 0)
                    act.wait_ge(sems[f"bank_taken{tile % 2}"], p.value(f"bank_taken{tile % 2}", bn))
                    if i == 2:
                        act.wait_ge(sems["feature_ready"], p.value("feature_ready", 9))
                    a(tmps[i % 2], feat[i][:, :], ACT.Square).then_inc(*p.count("square_ready"))
                elif name == "up" and blk[1] == 3:
                    act.wait_ge(sems["merged_tile"], p.value("merged_tile", half + 1))
                    nc.scalar.mul(part(h_hi, half), part(merged, half), 0.5).then_inc(*p.count("merged_hi_ready"))

            with act.Fori(0, LAYERS) as layer:
                p.enter(layer)
                for s in STEPS:
                    step(s)
                p.leave("layer")
                ahead.enter(layer)
                with act.Fori(0, QUARTERS) as q:
                    p.enter(layer, q)
                    for b, blk in enumerate(FF):
                        if b > 0:
                            hi_part(b + 1, ("x",), 2 * b)
                        if b >= 5:
                            with act.If(q > QUARTERS - 2):
                                for k in (2 * (b - 5), 2 * (b - 5) + 1):
                                    act.wait_ge(sems[f"bank_taken{k % 2}"], p.value(f"bank_taken{k % 2}", 4 + k // 2 + 1))
                                    next_square(k)
                        if blk[0] == "ff1":
                            for half in range(2):
                                tile = 2 * b + half
                                act.wait_ge(sems[f"bank_ready{tile % 2}"], p.value(f"bank_ready{tile % 2}", tile // 2 + 1))
                                a(tmps[tile % 2], gemm[tile % 2][:, :], ACT.Relu).then_inc(*p.count("relu_ready"))
                                act.wait_ge(sems[f"bank_taken{tile % 2}"], p.value(f"bank_taken{tile % 2}", tile // 2 + 1))
                                nc.scalar.copy(part(hid_hi, tile), part(prb, tile % 2)).then_inc(*p.count("hidden_hi_ready"))
                    with act.If(q > QUARTERS - 2):
                        for k in (KT - 2, KT - 1):
                            act.wait_ge(sems[f"bank_taken{k % 2}"], p.value(f"bank_taken{k % 2}", 4 + k // 2 + 1))
                            next_square(k)
                    with act.If(q < QUARTERS - 1):
                        hi_part(len(FF) + 1, ("x",), 2 * len(FF))
                    p.leave("quarter")
                ahead.leave("layer")

        @block.vector
        def _(dve):
            p = Program(dve, sems, "dve_order")
            programs.append(("dve", p))
            v = nc.vector
            stt = v.scalar_tensor_tensor

            def ada_unit(u):
                dve.wait_ge(sems["ada_landed"], p.value("ada_landed", 16 * (u + 1)))
                for k in range(KT):
                    acc = ada_acc[:, :]
                    w = ada_raw[:, k * BC:(k + 1) * BC]
                    if k == 0:
                        ins = v.tensor_scalar(acc, w, c_act[:, k:k + 1], None, ALU.mult)
                    else:
                        dve.wait_ge(*p.last)
                        ins = stt(out=acc, in0=w, scalar=c_act[:, k:k + 1], in1=acc, op0=ALU.mult, op1=ALU.add)
                    ins.then_inc(*p.count("ada_partial" if k == KT - 1 else None))

            def ada_mod(n_aux, dst, b_col):
                dve.wait_ge(sems["aux_ready"], p.value("aux_ready", n_aux + 1))
                v.tensor_tensor(dst, aux[:, 0:2], b_col, ALU.add).then_inc(*p.count("aux_taken", n=n_aux + 1))

            p.enter()
            dve.wait_ge(sems["aux_ready"], p.value("aux_ready", 1))
            v.tensor_copy(cols_a[:, :], aux[:, 0:P]).then_inc(*p.count("aux_taken"))
            dve.wait_ge(sems["aux_ready"], p.value("aux_ready", 2))
            v.tensor_copy(cols_b[:, :], aux[:, 0:56]).then_inc(*p.count("aux_taken"))
            dve.wait_ge(sems["c_tanh"], p.value("c_tanh", 1))
            dve.wait_ge(*p.last)
            stt(out=c_act[:, :], in0=stat[:, 0:8], scalar=1.0, in1=cols_b[:, 44:52], op0=ALU.add, op1=ALU.mult).then_inc(*p.count())
            dve.wait_ge(*p.last)
            v.tensor_scalar(c_act[:, :], c_act[:, :], 0.5, None, ALU.mult).then_inc(*p.count("c_act_ready"))

            s_arg, c_arg, ang, turns, pos = (feat[n][:, :] for n in range(5))
            own, prev, pos_col = ang, turns, feat[5][:, 0:NCH]
            rel_rows, freq = prb[:, 1024:1152], prb[:, 1184:1185]
            TWO_PI = (6.28125, 0.0019350051879882812, 2.0 * math.pi - 6.28125 - 0.0019350051879882812)
            LIMIT = 3.1415925
            dve.wait_ge(sems["vectors_loaded"], VECTORS)
            v.tensor_copy(pos, wrk[:, 0:T].bitcast(I32)).then_inc(*p.count())
            v.tensor_copy(pos_col, wrk[:, 1024:1028].bitcast(I32)).then_inc(*p.count())
            dve.wait_ge(*p.last)
            v.tensor_scalar(ang, pos, freq, None, ALU.mult).then_inc(*p.count())
            dve.wait_ge(*p.last)
            v.tensor_scalar(turns, ang, 1.0 / (2.0 * math.pi), 12582912.0, ALU.mult, ALU.add).then_inc(*p.count())
            dve.wait_ge(*p.last)
            v.tensor_scalar(turns, turns, 12582912.0, None, ALU.subtract).then_inc(*p.count())
            for n, piece in enumerate(TWO_PI):
                dve.wait_ge(*p.last)
                stt(out=s_arg, in0=turns, scalar=-piece, in1=(ang if n == 0 else s_arg), op0=ALU.mult,
                    op1=ALU.add).then_inc(*p.count())
            dve.wait_ge(*p.last)
            v.tensor_scalar(c_arg, s_arg, math.pi / 2, -2.0 * math.pi, ALU.is_gt, ALU.mult).then_inc(*p.count())
            dve.wait_ge(*p.last)
            stt(out=c_arg, in0=s_arg, scalar=math.pi / 2, in1=c_arg, op0=ALU.add, op1=ALU.add).then_inc(*p.count())
            dve.wait_ge(*p.last)
            v.tensor_scalar(c_arg, c_arg, LIMIT, -LIMIT, ALU.min, ALU.max).then_inc(*p.count())
            dve.wait_ge(*p.last)
            v.tensor_scalar(s_arg, s_arg, LIMIT, -LIMIT, ALU.min, ALU.max).then_inc(*p.count("angles_ready"))

            dve.wait_ge(*p.last)
            for i in range(NCH):
                blk_i = slice(i * CH, (i + 1) * CH)
                blk_p = slice(max(i - 1, 0) * CH, (max(i - 1, 0) + 1) * CH)
                v.tensor_scalar(own[:, blk_i], pos[:, blk_i], pos_col[:, i:i + 1], None, ALU.subtract).then_inc(*p.count())
                v.tensor_scalar(prev[:, blk_i], pos[:, blk_p], pos_col[:, i:i + 1], None, ALU.subtract).then_inc(*p.count())
            dve.wait_ge(*p.last)

            def by_chunk(t):
                return t.rearrange("p (i n) -> p i n", i=NCH)

            def each_chunk(m):
                return m.rearrange("p (o n) -> p o n", o=1).broadcast_to([P, NCH, CH])

            v.tensor_tensor(own, own, prev, ALU.subtract).then_inc(*p.count())
            dve.wait_ge(*p.last)
            v.tensor_tensor(by_chunk(own), by_chunk(own), each_chunk(own_mask), ALU.mult).then_inc(*p.count())
            dve.wait_ge(*p.last)
            tables = [bias[:, h * 2 * T:(h + 1) * 2 * T].rearrange("p (i s n) -> p i s n", i=NCH, s=2)
                      for h in range(HEADS)]
            acc = [t[:, :, 0, :] for t in tables]
            dist, step_of = tables[0][:, :, 1, :], tables[1][:, :, 1, :]
            limit, delta = (tables[HEADS - 1][:, i, 1, :] for i in range(2))
            tb = Program(dve, sems, "table_order")
            programs.append(("table", tb))
            tb.enter()

            def table_bucket(b):
                dve.wait_ge(*tb.last)
                v.tensor_scalar(step_of, dist, float(BUCKET_FROM[b]), None, ALU.is_ge).then_inc(*tb.count())
                dve.wait_ge(*tb.last)
                for h in range(HEADS):
                    d = (b - 1) * HEADS + h
                    stt(out=acc[h], in0=step_of, scalar=delta[:, d:d + 1], in1=acc[h], op0=ALU.mult,
                        op1=ALU.add).then_inc(*tb.count())

            def table_masks(h):
                own_side, prev_side = tables[h][:, :, 1, :], tables[h][:, :, 0, :]
                first = 1 if h == HEADS - 1 else 0
                n = NCH - first
                limits = limit.rearrange("p (o n) -> p o n", o=1).broadcast_to([P, n, CH])
                dve.wait_ge(*tb.last)
                stt(out=own_side[:, first:, :], in0=limits, scalar=-1.0, in1=prev_side[:, first:, :], op0=ALU.mult,
                    op1=ALU.min).then_inc(*tb.count())
                dve.wait_ge(*tb.last)
                v.tensor_tensor(prev_side[:, first:, :], prev_side[:, first:, :], limits, ALU.min).then_inc(*tb.count())
                if first:
                    dve.wait_ge(*tb.last)
                    stt(out=own_side[:, 0, :], in0=limit, scalar=-1.0, in1=prev_side[:, 0, :], op0=ALU.mult,
                        op1=ALU.min).then_inc(*tb.count())
                dve.wait_ge(*tb.last)
                v.memset(prev_side[:, 0, :], -BIG).then_inc(*tb.count())

            stt(out=dist, in0=by_chunk(prev), scalar=-1.0, in1=by_chunk(own), op0=ALU.mult,
                op1=ALU.subtract).then_inc(*tb.count())
            v.tensor_tensor(delta[:, 0:(BUCKETS - 1) * HEADS], rel_rows[:, HEADS:], rel_rows[:, 0:(BUCKETS - 1) * HEADS],
                            ALU.subtract).then_inc(*tb.count())
            v.tensor_scalar(limit, own_mask, -2.0 * BIG, BIG, ALU.mult, ALU.add).then_inc(*tb.count())
            dve.wait_ge(*tb.last)
            for h in range(HEADS):
                v.tensor_scalar(acc[h], dist, 0.0, rel_rows[:, h:h + 1], ALU.mult, ALU.add).then_inc(*tb.count())
            for b in range(1, TABLE_FIRST):
                table_bucket(b)
            ahead = Program(dve, sems)
            programs.append(("dve ahead", ahead))
            ahead.enter()

            def add_next_square(k):
                dve.wait_ge(sems["next_square_ready"], ahead.value("next_square_ready", k + 1))
                if k > 1:
                    dve.wait_ge(*ahead.last)
                v.tensor_tensor(square_sum, tmps[0] if k == 1 else square_sum, tmps[k % 2], ALU.add).then_inc(
                    *ahead.count("next_square_used"))

            for k in range(1, KT - 1):
                add_next_square(k)
            ahead.leave("before")
            dve.wait_ge(sems["aux_ready"], p.value("aux_ready", 3))
            v.tensor_tensor(mod[0][:, 0:2 * KT], aux[:, 0:2 * KT], cols_a[:, 0:2 * KT], ALU.add).then_inc(*p.count("aux_taken"))
            dve.wait_ge(sems["sines_ready"], p.value("sines_ready", 5))
            dve.wait_ge(*p.last)
            v.memset(stat[:, 19:20], 0.0).then_inc(*p.count())
            p.leave("before")

            def split_lo(dst, src, scale, hi, name, n=None):
                stt(out=dst, in0=src, scalar=scale, in1=hi.bitcast(F32), op0=ALU.mult, op1=ALU.subtract).then_inc(*p.count(name, n=n))

            def add_square(k):
                dve.wait_ge(sems["square_ready"], p.value("square_ready", 5 + k + 1))
                dve.wait_ge(*p.last)
                v.tensor_tensor(square_sum, tmps[0] if k == 1 else square_sum, tmps[k % 2], ALU.add).then_inc(
                    *p.count("square_used"))

            def step(s, layer):
                kind = s[0]
                if kind == "qk" and s[1] == 2:
                    g = 8 + s[2]
                    dve.wait_ge(sems["qk_ready"], p.value("qk_ready", g + 1))
                    for i, n in enumerate((1, 2, 1)):
                        diagonal = by_chunk(score[i][:, :])[:, 0:NCH:NCH - 1, :] if n == 2 else by_chunk(score[i][:, :])[:, 0:1, :]
                        mask = mask_strict[:, :].rearrange("p (o n) -> p o n", o=1).broadcast_to([P, n, CH])
                        v.tensor_tensor(diagonal, diagonal, mask, ALU.add).then_inc(*p.count("strict_ready" if i == 2 else None))
                    return
                if kind in ("norm", "ifrows", "gcol", "softplus", "probs", "divide", "hnorm", "rot", "headscale", "ada",
                            "adasum") or (kind == "pv" and s[2] % 2 == 1 and s[1] > 1) or (kind == "qk" and s[1] != 2):
                    dve.wait_ge(*p.last)
                if kind == "norm":
                    j = s[1]
                    if j:
                        add_square(KT - 2)
                    if j == 0:
                        dve.wait_ge(*p.last)
                        for dst, src, c0, w, per in (
                                (b_cur, cols_a, 16, 2 * ADA_REST, 48), (g_cur, cols_a, 96, 16, 16), (cw_cur, cols_b, 0, 16, 16),
                                (cb_cur, cols_b, 32, 4, 4), (rg_cur, cols_b, 40, 2, 2), (qk_cur[:, 0:1], cols_b, 52, 1, 1),
                                (qk_cur[:, 1:2], cols_b, 54, 1, 1), (sink_cur, sink_all, 0, 4, 4)):
                            v.tensor_copy(dst[:, 0:w], src[:, bass.ds(layer * per + c0, w)]).then_inc(*p.count())
                        v.tensor_copy(gb_cur[0:HEADS, :], gb[0:HEADS, bass.ds(layer * 2, 2)]).then_inc(*p.count())
                    dve.wait_ge(*p.last)
                    stt(out=acol[:, :], in0=mod[j][:, 8:16], scalar=1.0, in1=g_cur[:, 8 * j:8 * j + 8],
                        op0=ALU.add, op1=ALU.mult).then_inc(*p.count())
                    b = PRE_BLOCKS + 1 if j else 1
                    dve.wait_ge(sems["raw_landed1"], p.value("raw_landed1", 16 * (b // 2 + 1)))
                    dve.wait_ge(sems["bank_ready1"], p.value("bank_ready1", PRE_TILES // 2 if j else 0))
                    v.tensor_copy(w_hi[1][:, :], w_raw[1][:, :]).then_inc(sems["hi_ready1"], 1)
                    dve.wait_ge(*p.last)
                    dve.wait_ge(sems["rstd_ready"], p.value("rstd_ready", 7 if j else 1))
                    for k in range(KT + 1):
                        if k < KT:
                            if k:
                                dve.wait_ge(*p.last)
                            stt(out=part(prb, k % 2), in0=xk(k), scalar=acol[:, k:k + 1], in1=wrk[:, 0:T],
                                op0=ALU.mult, op1=ALU.mult).then_inc(*p.count("h_scaled"))
                        if k > 0:
                            dve.wait_ge(sems["h_hi_ready"], p.value("h_hi_ready", j * KT + k))
                            stt(out=part(h_lo, k - 1), in0=part(prb, (k - 1) % 2), scalar=mod[j][:, k - 1:k],
                                in1=part(h_hi, k - 1).bitcast(F32), op0=ALU.add, op1=ALU.subtract).then_inc(*p.count("h_ready"))
                elif kind == "tile":
                    tile_step(s)
                elif kind == "ifrows":
                    v.memset(row_one, 1.0).then_inc(*p.count())
                    dve.wait_ge(sems["logterm_ready"], p.value("logterm_ready", 1))
                    dve.wait_ge(*p.last)
                    stt(out=row_t, in0=row_f, scalar=0.0, in1=row_t, op0=ALU.min, op1=ALU.subtract).then_inc(*p.count())
                    dve.wait_ge(*p.last)
                    v.tensor_tensor_scan(row_a, row_one, row_t, 0.0, ALU.mult, ALU.add).then_inc(*p.count())
                    dve.wait_ge(*p.last)
                    v.tensor_tensor(row_i, row_i, row_a, ALU.subtract).then_inc(*p.count())
                    dve.wait_ge(*p.last)
                    v.tensor_tensor_scan(row_m, row_i, row_i, 0.0, ALU.max, ALU.max).then_inc(*p.count())
                    dve.wait_ge(*p.last)
                    v.tensor_tensor(row_am, row_a, row_m, ALU.add).then_inc(*p.count("rows_ready"))
                elif kind == "gcol":
                    dve.wait_ge(sems["aux_ready"], p.value("aux_ready", AUX[s] + 1))
                    v.tensor_copy(gcol[:, :], aux[:, 0:NCH * HEADS]).then_inc(*p.count("aux_taken", n=AUX[s] + 1))
                elif kind == "qk":
                    qk_step(s)
                elif kind in ("softplus", "probs"):
                    softmax_step(s)
                elif kind == "divide":
                    pair = s[1]
                    dve.wait_ge(sems["den_ready"], p.value("den_ready", pair + 1))
                    v.tensor_tensor(tmps[0], tmps[0], tmps[1], ALU.max).then_inc(*p.count())
                    dve.wait_ge(*p.last)
                    v.reciprocal(tmps[0], tmps[0]).then_inc(*p.count())
                    dve.wait_ge(*p.last)
                    for r, bank in ((slice(0, HD), outp), (slice(HD, P), denp)):
                        v.tensor_tensor(tmps[0][r, :], bank[r, :], tmps[0][r, :], ALU.mult).then_inc(*p.count())
                    dve.wait_ge(*p.last)
                    stt(out=tmps[0], in0=feat[4 + pair][:, :], scalar=1.0, in1=tmps[0], op0=ALU.add,
                        op1=ALU.mult).then_inc(*p.count("out_scaled"))
                    dve.wait_ge(sems["branch_hi_ready"], p.value("branch_hi_ready", pair + 1))
                    split_lo(part(br_lo, pair), tmps[0], 0.5, part(br_hi, pair), "branch_ready")
                elif kind == "pv" and s[2] % 2 == 1:
                    _, n, h = s
                    pair = h // 2
                    if n >= 2:
                        dve.wait_ge(sems["branch_hi_ready"], p.value("branch_hi_ready", 2 * n + pair + 1))
                        split_lo(part(br_lo, pair), outp[:, :], 1.0, part(br_hi, pair), "branch_ready")
                elif kind == "hnorm":
                    pair = s[1]
                    dve.wait_ge(sems["rstd_ready"], p.value("rstd_ready", 2 + pair))
                    stt(out=tmps[0], in0=outp[:, :], scalar=rg_cur[:, pair:pair + 1], in1=tmps[1],
                        op0=ALU.mult, op1=ALU.mult).then_inc(*p.count())
                    dve.wait_ge(*p.last)
                    v.tensor_tensor(tmps[0], tmps[0], feat[4 + pair][:, :], ALU.mult).then_inc(*p.count("out_scaled"))
                    dve.wait_ge(sems["branch_hi_ready"], p.value("branch_hi_ready", 2 + pair + 1))
                    split_lo(part(br_lo, pair), tmps[0], 0.5, part(br_hi, pair), "branch_ready")
                elif kind == "rot":
                    i = s[1]
                    dve.wait_ge(sems["rot_raw"], p.value("rot_raw", i + 1))
                    v.tensor_tensor(part(wrk, i % 2), part(wrk, i % 2), sin[:, :], ALU.mult).then_inc(*p.count())
                    v.tensor_tensor(feat[i][:, :], feat[i][:, :], cos[:, :], ALU.mult).then_inc(*p.count())
                    dve.wait_ge(*p.last)
                    v.tensor_tensor(feat[i][:, :], feat[i][:, :], part(wrk, i % 2), ALU.add).then_inc(*p.count("feature_ready"))
                elif kind == "headscale":
                    i = s[1]
                    dve.wait_ge(sems["rstd_ready"], p.value("rstd_ready", 4 + i))
                    r = tmps[i % 2]
                    if i < 2:
                        stt(out=feat[i][:, :], in0=feat[i][:, :], scalar=qk_cur[:, 0:1], in1=r, op0=ALU.mult,
                            op1=ALU.mult).then_inc(*p.count("feature_ready"))
                    else:
                        for n, (kv, to) in enumerate(((0, 0), (0, 1), (1, 0), (1, 1))):
                            f = slice(kv * HD, (kv + 1) * HD)
                            ins = stt(out=feat[3 + kv][to * HD:(to + 1) * HD, :], in0=feat[2][f, :],
                                      scalar=qk_cur[f, 1:2], in1=r[f, :], op0=ALU.mult, op1=ALU.mult)
                            ins.then_inc(*p.count("feature_ready" if n == 3 else None))
                elif kind == "squaresum" and s[1] > 0:
                    add_square(s[1])
                elif kind == "ada":
                    dve.wait_ge(*p.last)
                    ada_unit(s[1])
                elif kind == "adasum":
                    j, c = divmod(2 * KT + 2 * s[1], 3 * KT)
                    ada_mod(AUX[s], mod[j][:, c:c + 2], b_cur[:, 2 * s[1]:2 * s[1] + 2])
                elif kind == "table":
                    with dve.If(layer < 1):
                        if s[1] < BUCKETS - TABLE_FIRST:
                            table_bucket(TABLE_FIRST + s[1])
                        else:
                            table_masks(s[1] - (BUCKETS - TABLE_FIRST))

            def qk_step(s):
                _, n, h = s
                g = 4 * n + h
                if n == 0:
                    dve.wait_ge(sems["aux_ready"], p.value("aux_ready", AUX[s] + 1))
                    dve.wait_ge(*p.last)
                    stt(out=by_chunk(tmps[0]), in0=by_chunk(aux[:, :]), scalar=-1.0, in1=each_chunk(mask_incl[:, :]),
                        op0=ALU.mult, op1=ALU.add).then_inc(*p.count("masked_ready"))
                if n < 2:
                    dve.wait_ge(sems["qk_ready"], p.value("qk_ready", g + 1))
                    dve.wait_ge(sems["decay_ready"], p.value("decay_ready", g + 1))
                    dve.wait_ge(sems["pv_ready"], p.value("pv_ready", g))
                    if n == 0:
                        for i, (c0, w) in enumerate(((0, T), (T, T), (2 * T, 256))):
                            ins = stt(out=prb[:, c0:c0 + w], in0=score[i][:, 0:w], scalar=0.25 * HD ** -0.5,
                                      in1=wrk[:, c0:c0 + w], op0=ALU.mult, op1=ALU.mult)
                            ins.then_inc(*p.count("scores_taken" if i == 2 else None, n=g + 1 if i == 2 else None))
                    else:
                        for j in range(NCH):
                            ins = stt(out=prb[:, OFF[j]:OFF[j] + LEN[j]],
                                      in0=score[SC_BANK[j]][:, SC_COL[j]:SC_COL[j] + LEN[j]], scalar=HD ** -0.5,
                                      in1=wrk[:, 0:LEN[j]], op0=ALU.mult, op1=ALU.mult)
                            last = j == NCH - 1
                            ins.then_inc(*p.count("scores_taken" if last else None, n=g + 1 if last else None))
                elif n == 3:
                    dve.wait_ge(sems["qk_ready"], p.value("qk_ready", g + 1))
                    if h == 0:
                        dve.wait_ge(*tb.last)
                    for i in range(2):
                        ins = stt(out=part(wrk, i), in0=score[i][:, :], scalar=HD ** -0.5,
                                  in1=bias[:, h * 2 * T + i * T:h * 2 * T + (i + 1) * T], op0=ALU.mult, op1=ALU.add)
                        ins.then_inc(*p.count("scores_taken" if i else None, n=g + 1 if i else None))
                    dve.wait_ge(*p.last)
                    v.tensor_reduce(stat[:, 0:NCH], wrk[:, 0:2 * T].rearrange("p (i n) -> p i n", i=NCH), AX.X,
                                    ALU.max).then_inc(*p.count())
                    dve.wait_ge(*p.last)
                    v.tensor_scalar(stat[:, NCH:2 * NCH], stat[:, 0:NCH], sink_cur[:, h:h + 1], -1.0, ALU.max,
                                    ALU.mult).then_inc(*p.count("negmax_ready"))

            def softmax_step(s):
                kind, h = s
                if kind == "softplus":
                    dve.wait_ge(sems["logterm_ready"], p.value("logterm_ready", 1 + h + 1))
                    for i, (c0, w) in enumerate(((0, T), (T, T), (2 * T, 256))):
                        ins = stt(out=wrk[:, c0:c0 + w], in0=score[i][:, 0:w], scalar=0.0, in1=wrk[:, c0:c0 + w],
                                  op0=ALU.max, op1=ALU.add)
                        ins.then_inc(*p.count())
                    dve.wait_ge(*p.last)
                    dve.wait_ge(sems["pv_ready"], p.value("pv_ready", 8 + h))
                    v.tensor_tensor(later_sum[:, 0:CH], wrk[:, OFF[2] + CH:OFF[2] + 2 * CH], wrk[:, OFF[3]:OFF[3] + CH],
                                    ALU.add).then_inc(*p.count())
                    v.tensor_tensor(later_sum[:, CH:2 * CH], wrk[:, OFF[1] + CH:OFF[1] + 2 * CH],
                                    wrk[:, OFF[2]:OFF[2] + CH], ALU.add).then_inc(*p.count())
                    dve.wait_ge(*p.last)
                    v.tensor_tensor(later_sum[:, 2 * CH:3 * CH], wrk[:, OFF[1] + 2 * CH:OFF[1] + 3 * CH],
                                    later_sum[:, 0:CH], ALU.add).then_inc(*p.count("softplus_ready"))
                else:
                    dve.wait_ge(sems["exp_ready"], p.value("exp_ready", h + 1))
                    den = stat[:, 4 * NCH:5 * NCH]
                    v.tensor_tensor(den, stat[:, 2 * NCH:3 * NCH], stat[:, 3 * NCH:4 * NCH], ALU.add).then_inc(*p.count())
                    dve.wait_ge(*p.last)
                    v.reciprocal(den, den).then_inc(*p.count())
                    dve.wait_ge(*p.last)
                    for i in range(NCH):
                        pi = prb[:, i * 256:(i + 1) * 256]
                        v.tensor_scalar(pi, pi, den[:, i:i + 1], None, ALU.mult).then_inc(*p.count("probs_ready" if i == NCH - 1 else None))

            def tile_step(s):
                _, b, half = s
                blk = BLOCKS[b]
                name = blk[0]
                tile = TILE_NO[(b, half)]
                bank, taken, bn = gemm[tile % 2], f"bank_taken{tile % 2}", tile // 2 + 1
                if name in ("m_q", "m_k"):
                    i = half + (2 if name == "m_k" else 0)
                    u = tmps[i % 2]
                    dve.wait_ge(sems[f"bank_ready{tile % 2}"], p.value(f"bank_ready{tile % 2}", bn))
                    dve.wait_ge(*p.last)
                    v.tensor_scalar(u, bank[:, :], cw_cur[:, 12 + i:13 + i], cb_cur[:, i:i + 1], ALU.mult, ALU.add).then_inc(*p.count())
                    for back in range(1, 4):
                        dve.wait_ge(*p.last)
                        ins = stt(out=u[:, back:T], in0=bank[:, 0:T - back],
                                  scalar=cw_cur[:, (3 - back) * 4 + i:(3 - back) * 4 + i + 1], in1=u[:, back:T],
                                  op0=ALU.mult, op1=ALU.add)
                        if back < 3:
                            ins.then_inc(*p.count())
                        else:
                            ins.then_inc(*p.count("conv_ready"))
                    v.memset(stat[:, 19:20], 0.0).then_inc(*p.count(taken, n=bn))
                    dve.wait_ge(sems["silu_ready"], p.value("silu_ready", i + 1))
                    stt(out=feat[i][:, :], in0=part(prb, i % 2), scalar=1.0, in1=u, op0=ALU.add, op1=ALU.mult).then_inc(*p.count("feature_ready"))
                elif name == "m_if":
                    dve.wait_ge(sems[f"bank_ready{tile % 2}"], p.value(f"bank_ready{tile % 2}", bn))
                    if half == 0:
                        v.tensor_copy(row_if, bank[0:2 * HEADS, :]).then_inc(*p.count(taken, n=bn))
                    else:
                        v.tensor_scalar(row_f, bank[0:HEADS, :], gb_cur[0:HEADS, 1:2], None, ALU.add).then_inc(*p.count(taken, n=bn))
                        v.tensor_scalar(row_i, row_if[0:HEADS, :], gb_cur[0:HEADS, 0:1], None, ALU.add).then_inc(*p.count())
                elif name == "gate":
                    dve.wait_ge(sems[f"bank_ready{tile % 2}"], p.value(f"bank_ready{tile % 2}", bn))
                    v.tensor_copy(gate_tile(2 * blk[2] + half), bank[:, :]).then_inc(*p.count(taken, n=bn))
                elif name in ("r_q", "r_k"):
                    i = half + (2 if name == "r_k" else 0)
                    dve.wait_ge(sems[f"bank_ready{tile % 2}"], p.value(f"bank_ready{tile % 2}", bn))
                    v.tensor_copy(feat[i][:, :], bank[:, :]).then_inc(*p.count(taken, n=bn))
                elif name == "r_g":
                    dve.wait_ge(sems["silu_ready"], p.value("silu_ready", 4 + half + 1))
                    stt(out=feat[4 + half][:, :], in0=tmps[half], scalar=1.0, in1=bank[:, :], op0=ALU.add,
                        op1=ALU.mult).then_inc(*p.count(taken, n=bn))
                elif name in ("s_q", "s_k"):
                    dve.wait_ge(sems[f"bank_ready{tile % 2}"], p.value(f"bank_ready{tile % 2}", bn))
                    f = feat[half + (2 if name == "s_k" else 0)][:, :]
                    v.tensor_scalar(f, bank[:, :], HD ** -0.5 if name == "s_q" else 1.0, None, ALU.mult).then_inc(*p.count(taken, n=bn))
                elif name == "a_q" or (name == "a_kv" and half == 0):
                    dve.wait_ge(sems[f"bank_ready{tile % 2}"], p.value(f"bank_ready{tile % 2}", bn))
                    v.tensor_copy(feat[half + (2 if name == "a_kv" else 0)][:, :], bank[:, :]).then_inc(*p.count(taken, n=bn))
                elif name == "up":
                    n, m = blk[1], half
                    if m in (0, 6):
                        dve.wait_ge(sems["gate_ready"], p.value("gate_ready", (1, 2, 3 + m // 6, 5 + m // 6)[n]))
                    dve.wait_ge(sems[f"bank_ready{tile % 2}"], p.value(f"bank_ready{tile % 2}", bn))
                    dst = part(merged, m) if n == 0 else gate_tile(m)
                    stt(out=dst, in0=gate_tile(m), scalar=1.0, in1=bank[:, :], op0=ALU.add, op1=ALU.mult).then_inc(*p.count(taken, n=bn))
                    if n > 0:
                        dve.wait_ge(*p.last)
                        v.tensor_tensor(part(merged, m), part(merged, m), gate_tile(m), ALU.add).then_inc(*p.count("merged_tile" if n == 3 else None))
                    if n == 3:
                        for k in ([m - 1] if m else []) + ([7] if m == 7 else []):
                            dve.wait_ge(sems["merged_hi_ready"], p.value("merged_hi_ready", k + 1))
                            split_lo(part(h_lo, k), part(merged, k), 0.5, part(h_hi, k), "merged_ready")
                elif name == "out":
                    m = 2 * blk[1] + half
                    dve.wait_ge(sems[f"bank_ready{tile % 2}"], p.value(f"bank_ready{tile % 2}", bn))
                    stt(out=xk(m), in0=bank[:, :], scalar=mod[0][:, 16 + m:17 + m], in1=xk(m), op0=ALU.mult,
                        op1=ALU.add).then_inc(*p.count(taken, n=bn))

            with dve.Fori(0, LAYERS) as layer:
                p.enter(layer)
                for s in STEPS:
                    step(s, layer)
                p.leave("layer")
                tb.leave("before")
                ahead.enter(layer)
                with dve.Fori(0, QUARTERS) as q:
                    p.enter(layer, q)
                    for b, blk in enumerate(FF):
                        for half in range(2):
                            tile = 2 * b + half
                            bank, taken, bn = gemm[tile % 2], f"bank_taken{tile % 2}", tile // 2 + 1
                            if blk[0] == "ff1":
                                sq = part(prb, tile % 2)
                                dve.wait_ge(sems["relu_ready"], p.value("relu_ready", tile + 1))
                                stt(out=sq, in0=bank[:, :], scalar=0.0, in1=tmps[tile % 2], op0=ALU.max,
                                    op1=ALU.mult).then_inc(*p.count(taken, n=bn))
                                dve.wait_ge(sems["hidden_hi_ready"], p.value("hidden_hi_ready", tile + 1))
                                v.tensor_tensor(part(hid_lo, tile), sq, part(hid_hi, tile).bitcast(F32),
                                                ALU.subtract).then_inc(*p.count("hidden_ready"))
                            else:
                                m = tile - 8
                                dve.wait_ge(sems[f"bank_ready{tile % 2}"], p.value(f"bank_ready{tile % 2}", bn))
                                stt(out=xk(m), in0=bank[:, :], scalar=mod[1][:, 16 + m:17 + m], in1=xk(m),
                                    op0=ALU.mult, op1=ALU.add).then_inc(*p.count(taken, n=bn))
                            if half == 0 and b >= 5:
                                with dve.If(q > QUARTERS - 2):
                                    for k in (2 * (b - 5), 2 * (b - 5) + 1):
                                        if k > 0:
                                            add_next_square(k)
                            if half == 0 and b in FF_ADASUM:
                                u = FF_ADASUM[b]
                                ada_mod(u, mod[0][:, bass.ds(q * 4 + 2 * u, 2)],
                                        cols_a[:, bass.ds(q * 4 + (48 + 2 * u), 2)])
                        if b in FF_ADA:
                            dve.wait_ge(*p.last)
                            ada_unit(FF_ADA[b])
                    with dve.If(q > QUARTERS - 2):
                        add_next_square(KT - 2)
                    v.memset(stat[:, 19:20], 0.0).then_inc(*p.count())
                    p.leave("quarter")
                ahead.leave("layer")

            for n in range(2 * NCH):
                dve.wait_ge(sems["xt_ready"], n + 1)
                v.tensor_copy(x_out[n // 2][:, (n % 2) * T:(n % 2 + 1) * T], gemm[n % 2][:, :]).then_inc(
                    sems["xt_taken"], 1)

    return programs


def check_counts(programs):
    total = {name: [1, 0, 0] for name in STARTED}
    for _, p in programs:
        for region, i in (("before", 0), ("layer", 1), ("quarter", 2)):
            for name, n in p.seen.get(region, {}).items():
                total.setdefault(name, [0, 0, 0])[i] += n
    wrong = {name: tuple(t) for name, t in total.items() if tuple(t) != COUNTS[name] and not name.startswith("hi_ready")}
    assert not wrong, wrong


_INS = ["x", "c", "positions", "w_ada", "b_ada", "norm_g", "w_in", "mlstm_conv_w", "mlstm_conv_b", "mlstm_gate_b",
        "ret_norm_g", "swa_q_norm_g", "swa_k_norm_g", "swa_sinks", "rel_bias", "w_up", "w_out", "w_ff1", "w_ff2"]


def kernel(**inputs):
    import concourse.bacc as bacc
    from concourse.bass_utils import run_bass_kernel_spmd

    nc = bacc.Bacc("TRN2", target_bir_lowering=False, num_devices=1)
    arrays = {f"in_{name}": np.ascontiguousarray(inputs[name]) for name in _INS}
    half = HD // 2
    inv = np.float32(10000.0) ** (-np.arange(half, dtype=np.float32) / np.float32(half))
    arrays["rope_freq"] = np.tile(inv, P // half).reshape(P, 1).astype(np.float32)
    args = [nc.dram_tensor(name, a.shape, mybir.dt.from_np(a.dtype), kind="ExternalInput").ap()
            for name, a in arrays.items()]
    args.append(nc.dram_tensor("out", (1, T, D), F32, kind="ExternalOutput").ap())
    check_counts(trunk(nc, *args))
    return run_bass_kernel_spmd(nc, [arrays], core_ids=[0]).results[0]["out"]
```
